# Optimizing a Trainium2 kernel written in Bass

```python
import jax, jax.numpy as jnp
from jax import lax
import numpy as np

D_MODEL = 1024
BATCH = 1
SEQ = 256
DEPTH = 1

CHUNK = 64
Q_BLOCK = 128
RWKV_WIDTH = D_MODEL // 2
RWKV_HEAD = 64
RWKV_HEADS = RWKV_WIDTH // RWKV_HEAD
DECAY_LORA = 64
AAA_LORA = 64
GATE_LORA = 128
DIFF_WIDTH = D_MODEL - RWKV_WIDTH
DIFF_HEAD = 64
DIFF_HEADS = DIFF_WIDTH // (2 * DIFF_HEAD)
MEM_LEN = 256
XATTN_HEADS = 4
XATTN_HEAD = D_MODEL // XATTN_HEADS
N_EXPERTS = 32
TOP_K = 4
D_FF = D_MODEL
SWIGLU_LIMIT = 7.0
SWIGLU_ALPHA = 1.702
MOE_BLOCK = 256
NORM_EPS = 1e-5
GN_EPS = 64e-5
RWKV_COL_SIZES = (RWKV_WIDTH, RWKV_WIDTH, RWKV_WIDTH, DECAY_LORA, AAA_LORA, GATE_LORA)
SHIFT_COLS = sum(RWKV_COL_SIZES)
IN_COLS = SHIFT_COLS + 3 * DIFF_WIDTH

kernel_name = "hybrid_rwkv7_diffattn_moe_block"

def rms_norm(x, g):
    xf = x.astype(jnp.float32)
    y = xf * lax.rsqrt(jnp.mean(xf * xf, axis=-1, keepdims=True) + NORM_EPS)
    return (y * g.astype(jnp.float32)).astype(x.dtype)

def token_shift(p):
    return jnp.pad(p, ((0, 0), (1, 0), (0, 0)))[:, :-1]

def split_cols(p, sizes):
    idx = np.cumsum(sizes)[:-1].tolist()
    return jnp.split(p, idx, axis=-1)

def rwkv7_group(p, mu, w0, w2, a0, a2, g2, k_k, k_a, r_k, lnx_g, lnx_b):
    B, T, _ = p.shape
    H, N = RWKV_HEADS, RWKV_HEAD
    p = p + (token_shift(p) - p) * mu
    r, k, v, wd, ad, gd = split_cols(p, RWKV_COL_SIZES)
    w = -jax.nn.softplus(-(w0 + jnp.tanh(wd) @ w2)) - 0.5
    decay = jnp.exp(-jnp.exp(w.astype(jnp.float32)))
    a = jax.nn.sigmoid(a0 + ad @ a2)
    g = jax.nn.sigmoid(gd) @ g2
    kk = (k * k_k).reshape(B, T, H, N).astype(jnp.float32)
    kk = kk / jnp.maximum(jnp.sqrt(jnp.sum(kk * kk, axis=-1, keepdims=True)), 1e-12)
    k = k * (1.0 + (a - 1.0) * k_a)
    hs = lambda t: jnp.moveaxis(t.reshape(B, T, H, N).astype(jnp.float32), 1, 0)
    rh, kh, vh, ah = hs(r), hs(k), hs(v), hs(a)
    xs = (rh, hs(decay), kh, vh, jnp.moveaxis(kk, 1, 0), ah)

    def step(S, inp):
        rt, wt, kt, vt, kkt, at = inp
        sa = jnp.einsum('bhvk,bhk->bhv', S, -kkt)
        S = S * wt[:, :, None, :] + sa[..., None] * (kkt * at)[:, :, None, :] + vt[..., None] * kt[:, :, None, :]
        return S, jnp.einsum('bhvk,bhk->bhv', S, rt)

    S0 = jnp.zeros((B, H, N, N), jnp.float32)
    _, y = lax.scan(step, S0, xs)
    mean = jnp.mean(y, axis=-1, keepdims=True)
    var = jnp.mean(jnp.square(y - mean), axis=-1, keepdims=True)
    yn = ((y - mean) * lax.rsqrt(var + GN_EPS)).reshape(T, B, H * N)
    yn = yn * lnx_g.astype(jnp.float32) + lnx_b.astype(jnp.float32)
    yn = jnp.moveaxis(yn, 0, 1).reshape(B, T, H, N)
    bonus = jnp.sum(jnp.moveaxis(rh * kh, 0, 1) * r_k.astype(jnp.float32), axis=-1, keepdims=True) * jnp.moveaxis(vh, 0, 1)
    out = (yn + bonus).reshape(B, T, H * N).astype(p.dtype) * g
    return out

def diff_attn_group(q, k, v, lam_q1, lam_k1, lam_q2, lam_k2, subln_g, lambda_init):
    B, T, _ = q.shape
    H, d = DIFF_HEADS, DIFF_HEAD
    NB = T // Q_BLOCK
    qh = jnp.transpose(q.reshape(B, T, H, 2, d), (0, 2, 3, 1, 4))
    kh = jnp.transpose(k.reshape(B, T, H, 2, d), (0, 2, 3, 1, 4))
    vh = jnp.transpose(v.reshape(B, T, H, 2 * d), (0, 2, 1, 3))
    lam = (jnp.exp(jnp.sum(lam_q1.astype(jnp.float32) * lam_k1.astype(jnp.float32)))
           - jnp.exp(jnp.sum(lam_q2.astype(jnp.float32) * lam_k2.astype(jnp.float32))) + lambda_init)
    scale = d ** -0.5
    qb = jnp.moveaxis(qh.reshape(B, H, 2, NB, Q_BLOCK, d), 3, 0)
    k_chunk = jnp.arange(T) // CHUNK

    def block(args):
        qi, bi = args
        s = jnp.einsum('bhcqd,bhckd->bhcqk', qi, kh).astype(jnp.float32) * scale
        q_chunk = (bi * Q_BLOCK + jnp.arange(Q_BLOCK)) // CHUNK
        allowed = k_chunk[None, :] <= q_chunk[:, None]
        s = jnp.where(allowed, s, -1e30)
        pr = jax.nn.softmax(s, axis=-1)
        attn = pr[:, :, 0] - lam * pr[:, :, 1]
        return jnp.einsum('bhqk,bhkd->bhqd', attn.astype(vh.dtype), vh)

    o = lax.map(block, (qb, jnp.arange(NB)))
    o = jnp.moveaxis(o, 0, 2).reshape(B, H, T, 2 * d)
    o = rms_norm(o, subln_g) * (1.0 - lambda_init)
    return jnp.transpose(o, (0, 2, 1, 3)).reshape(B, T, H * 2 * d)

def cross_attn(hn, memn, wq, wkv, wo):
    B, T, _ = hn.shape
    q = (hn @ wq).reshape(B, T, XATTN_HEADS, XATTN_HEAD)
    kv = memn @ wkv
    km, vm = jnp.split(kv, 2, axis=-1)
    km = km.reshape(B, MEM_LEN, XATTN_HEADS, XATTN_HEAD)
    vm = vm.reshape(B, MEM_LEN, XATTN_HEADS, XATTN_HEAD)
    s = jnp.einsum('bqhd,bkhd->bhqk', q, km).astype(jnp.float32) * (XATTN_HEAD ** -0.5)
    pr = jax.nn.softmax(s, axis=-1).astype(vm.dtype)
    o = jnp.einsum('bhqk,bkhd->bqhd', pr, vm).reshape(B, T, D_MODEL)
    return o @ wo

def moe(xn, router_w, router_b, w1, b1, w2, b2):
    B, T, D = xn.shape
    N = B * T
    xf = xn.reshape(N, D)
    logits = (xf @ router_w + router_b).astype(jnp.float32)
    top_v, top_i = lax.top_k(logits, TOP_K)
    gates = jax.nn.softmax(top_v, axis=-1).astype(xn.dtype)
    M = N * TOP_K
    flat_e = top_i.reshape(M).astype(jnp.int32)
    flat_tok = jnp.repeat(jnp.arange(N, dtype=jnp.int32), TOP_K)
    flat_g = gates.reshape(M)
    order = jnp.argsort(flat_e, stable=True)
    sorted_e = flat_e[order]
    counts = jnp.bincount(flat_e, length=N_EXPERTS).astype(jnp.int32)
    offsets = jnp.cumsum(counts) - counts
    padded_counts = ((counts + MOE_BLOCK - 1) // MOE_BLOCK) * MOE_BLOCK
    padded_end = jnp.cumsum(padded_counts)
    padded_off = padded_end - padded_counts
    dest = padded_off[sorted_e] + (jnp.arange(M, dtype=jnp.int32) - offsets[sorted_e])
    P = M + N_EXPERTS * MOE_BLOCK
    NBLK = P // MOE_BLOCK
    row_tok = jnp.full((P,), N, jnp.int32).at[dest].set(flat_tok[order])
    row_g = jnp.zeros((P,), xn.dtype).at[dest].set(flat_g[order])
    block_start = jnp.arange(NBLK, dtype=jnp.int32) * MOE_BLOCK
    block_e = jnp.minimum(jnp.sum(block_start[:, None] >= padded_end[None, :], axis=1), N_EXPERTS - 1)
    x_pad = jnp.concatenate([xf, jnp.zeros((1, D), xf.dtype)], axis=0)
    xin = x_pad[row_tok].reshape(NBLK, MOE_BLOCK, D)

    def expert_block(args):
        xb, e = args
        h = xb @ w1[e] + b1[e]
        gate, lin = jnp.split(h, 2, axis=-1)
        gate = jnp.minimum(gate, SWIGLU_LIMIT)
        lin = jnp.clip(lin, -SWIGLU_LIMIT, SWIGLU_LIMIT)
        act = gate * jax.nn.sigmoid(SWIGLU_ALPHA * gate) * (lin + 1.0)
        return act @ w2[e] + b2[e]

    yb = lax.map(expert_block, (xin, block_e)).reshape(P, D) * row_g[:, None]
    y = jax.ops.segment_sum(yb, row_tok, num_segments=N + 1)[:N]
    return y.reshape(B, T, D)

def setup_inputs(seed: int = 0) -> dict:
    key = jax.random.key(seed)
    ks = iter(jax.random.split(key, 40))
    L, D, E, F = DEPTH, D_MODEL, N_EXPERTS, D_FF
    nrm = lambda shape, s: jax.random.normal(next(ks), shape, jnp.float32) * s
    ratio = jnp.linspace(0.0, 1.0, RWKV_WIDTH, dtype=jnp.float32)
    return {
        "x": nrm((BATCH, SEQ, D), 1.0),
        "mem": nrm((BATCH, MEM_LEN, D), 1.0),
        "norm1_g": 1.0 + nrm((L, D), 0.02),
        "w_in": nrm((L, D, IN_COLS), D ** -0.5),
        "mu_shift": jax.random.uniform(next(ks), (L, SHIFT_COLS), jnp.float32),
        "w0": (-6.5 + 5.0 * ratio ** 0.9)[None, :] + nrm((L, RWKV_WIDTH), 0.1),
        "w2": nrm((L, DECAY_LORA, RWKV_WIDTH), 0.1 * DECAY_LORA ** -0.5),
        "a0": nrm((L, RWKV_WIDTH), 0.1),
        "a2": nrm((L, AAA_LORA, RWKV_WIDTH), AAA_LORA ** -0.5),
        "g2": nrm((L, GATE_LORA, RWKV_WIDTH), GATE_LORA ** -0.5),
        "k_k": 0.85 + nrm((L, RWKV_WIDTH), 0.02),
        "k_a": 1.0 + nrm((L, RWKV_WIDTH), 0.02),
        "r_k": nrm((L, RWKV_HEADS, RWKV_HEAD), 0.1),
        "lnx_g": 1.0 + nrm((L, RWKV_WIDTH), 0.02),
        "lnx_b": nrm((L, RWKV_WIDTH), 0.02),
        "lam_q1": nrm((L, DIFF_HEAD), 0.1),
        "lam_k1": nrm((L, DIFF_HEAD), 0.1),
        "lam_q2": nrm((L, DIFF_HEAD), 0.1),
        "lam_k2": nrm((L, DIFF_HEAD), 0.1),
        "subln_g": 1.0 + nrm((L, 2 * DIFF_HEAD), 0.02),
        "w_out": nrm((L, D, D), D ** -0.5),
        "norm2_g": 1.0 + nrm((L, D), 0.02),
        "mem_norm_g": 1.0 + nrm((L, D), 0.02),
        "wq_x": nrm((L, D, D), D ** -0.5),
        "wkv_x": nrm((L, D, 2 * D), D ** -0.5),
        "wo_x": nrm((L, D, D), D ** -0.5),
        "norm3_g": 1.0 + nrm((L, D), 0.02),
        "router_w": nrm((L, D, E), D ** -0.5),
        "router_b": nrm((L, E), 0.01),
        "moe_w1": nrm((L, E, D, 2 * F), D ** -0.5),
        "moe_b1": nrm((L, E, 2 * F), 0.01),
        "moe_w2": nrm((L, E, F, D), F ** -0.5),
        "moe_b2": nrm((L, E, D), 0.01),
        "final_g": 1.0 + nrm((D,), 0.02),
    }

def reference(x, mem, norm1_g, w_in, mu_shift, w0, w2, a0, a2, g2, k_k, k_a, r_k, lnx_g, lnx_b,
              lam_q1, lam_k1, lam_q2, lam_k2, subln_g, w_out, norm2_g, mem_norm_g, wq_x, wkv_x, wo_x,
              norm3_g, router_w, router_b, moe_w1, moe_b1, moe_w2, moe_b2, final_g):
    h = x
    for i in range(DEPTH):
        lambda_init = 0.8 - 0.6 * float(np.exp(-0.3 * i))
        xn = rms_norm(h, norm1_g[i])
        proj = xn @ w_in[i]
        p_rwkv = proj[..., :SHIFT_COLS]
        q_d, k_d, v_d = split_cols(proj[..., SHIFT_COLS:], (DIFF_WIDTH, DIFF_WIDTH, DIFF_WIDTH))
        y_rwkv = rwkv7_group(p_rwkv, mu_shift[i], w0[i], w2[i], a0[i], a2[i], g2[i],
                             k_k[i], k_a[i], r_k[i], lnx_g[i], lnx_b[i])
        y_diff = diff_attn_group(q_d, k_d, v_d, lam_q1[i], lam_k1[i], lam_q2[i], lam_k2[i],
                                 subln_g[i], lambda_init)
        h = h + jnp.concatenate([y_rwkv, y_diff], axis=-1) @ w_out[i]
        h = h + cross_attn(rms_norm(h, norm2_g[i]), rms_norm(mem, mem_norm_g[i]), wq_x[i], wkv_x[i], wo_x[i])
        h = h + moe(rms_norm(h, norm3_g[i]), router_w[i], router_b[i], moe_w1[i], moe_b1[i], moe_w2[i], moe_b2[i])
    return rms_norm(h, final_g)


_drawn_inputs = setup_inputs


def setup_inputs(seed=0):
    import zlib

    import numpy as np

    out = dict(_drawn_inputs(seed))
    spreads = {}
    factors = {'w2': 4.234,
     'k_k': 4.781,
     'k_a': 2.906,
     'lnx_g': 2.67,
     'norm2_g': 5.141,
     'mem_norm_g': 4.244,
     'moe_b1': 38.543,
     'moe_b2': 44.625,
     'final_g': 8.089,
     'norm3_g': 3.971,
     'router_b': 8.0}
    for name, (base, spread) in spreads.items():
        noise = np.random.default_rng([zlib.crc32(name.encode()), seed]).standard_normal(out[name].shape)
        drawn = base * np.exp(spread * noise) if base else spread * noise
        out[name] = __import__('jax').numpy.asarray(drawn.astype(out[name].dtype))
    for name, factor in factors.items():
        out[name] = (out[name] * factor).astype(out[name].dtype)
    return out
```

```python
from contextlib import ExitStack

import concourse.bass as bass
from concourse import mybir

F32 = mybir.dt.float32
I32 = mybir.dt.int32
U32 = mybir.dt.uint32
ALU = mybir.AluOpType
ACT = mybir.ActivationFunctionType
AX = mybir.AxisListType

P = 128
T = 256
NT = T // P
D = 1024
KC = D // P
RW = 512
NH = 8
NP = NH // 2
HD = 64
SHIFT = 3 * RW + 64 + 64 + 128
DH = 4
XH = 4
E = 32
CH = 32
NCH = T // CH
SUB = 16
F = 1024
TOPK = 4
EPS = 1e-5
GN_EPS = 64e-5
LAMBDA_INIT = 0.8 - 0.6
XSCALE = (D // XH) ** -0.5
DSCALE = 64 ** -0.5
NEG_EXP_HALF = -0.6065306597126334
SLOT = 2048
RING = 12
PRE = 3
WCOL = 256
BLK = 64
PASSES = T // BLK

ROWS = [("norm1_g", KC), ("mu_shift", SHIFT // P), ("w0", 4), ("a0", 4), ("k_k", 4), ("k_a", 4), ("r_k", 4),
        ("lnx_g", 4), ("lnx_b", 4), ("norm2_g", KC), ("mem_norm_g", KC), ("norm3_g", KC), ("subln_g", 1)]
ROW = {}
NROWS = 0
for _name, _n in ROWS:
    ROW[_name] = NROWS
    NROWS += _n

PRE_CHUNKS = ([("wkv_x", n * WCOL) for n in range(8)] + [("w_in", n * WCOL) for n in range(13)]
              + [(w, n * WCOL) for w in ("w_out", "wq_x", "wo_x") for n in range(4)])
KV0, IN0, OUT0, WQ0, WO0 = 0, 8, 21, 25, 29


def program(nc, a, out):
    with ExitStack() as ctx:
        def sb(name, shape, dt=F32):
            return ctx.enter_context(nc.sbuf_tensor(name, shape, dt))

        sems = {}

        def sem(name):
            if name not in sems:
                sems[name] = ctx.enter_context(nc.semaphore(name))
            return sems[name]

        ring = sb("ring", [P, RING, SLOT])
        NF = 25088
        arena = sb("arena", [P, NF])
        ps = ctx.enter_context(nc.psum_tensor("ps", [P, 8, 512], F32))

        def cut(at, *shape):
            n = 1
            for s in shape:
                n *= s
            assert at + n <= NF
            v = arena[:, at:at + n]
            if len(shape) == 2:
                v = v.rearrange("p (a b) -> p a b", a=shape[0])
            if len(shape) == 3:
                v = v.rearrange("p (a b c) -> p a b c", a=shape[0], b=shape[1])
            if len(shape) == 4:
                v = v.rearrange("p (a b c d) -> p a b c d", a=shape[0], b=shape[1], c=shape[2])
            return v

        def side(slot, *shape):
            v = ring[:, slot:RING, :].rearrange("p a b -> p (a b)")
            n = 1
            for s in shape:
                n *= s
            v = v[:, 0:n]
            if len(shape) == 2:
                v = v.rearrange("p (a b) -> p a b", a=shape[0])
            if len(shape) == 3:
                v = v.rearrange("p (a b c) -> p a b c", a=shape[0], b=shape[1])
            if len(shape) == 4:
                v = v.rearrange("p (a b c d) -> p a b c d", a=shape[0], b=shape[1], c=shape[2])
            return v

        H0, XT0, E0, P0, AR0, BT0, KT0, BK0, GT0, QD0 = 0, 2048, 4096, 11264, 14848, 16896, 17920, 18944, 20992, 22016
        h = cut(H0, NT, D)
        xT = cut(XT0, KC, T)
        memT = cut(E0, KC, T)
        lw, cs, aa, kk, t1, t2 = (cut(E0 + 1024 * n, NP, T) for n in range(6))
        t3 = cut(QD0 + 2048, NP, T)
        pT = cut(P0, SHIFT // P, T)
        rT, kT, vT = (pT[:, 4 * n:4 * n + 4, :] for n in range(3))
        AR = cut(AR0, NP, NT, 2, P)
        BT, KT = cut(BT0, NP, T), cut(KT0, NP, T)
        Bd, Kd = cut(BK0, NP, T), cut(BK0 + 1024, NP, T)
        xs = cut(BK0, NT, D)
        gT = cut(GT0, NP, T)
        qd, kd = cut(QD0, DH, T), cut(QD0 + 1024, DH, T)
        vd = cut(QD0 + 2048, NT, RW)
        Zr = cut(E0, NT, NH, 2 * HD)
        Vn, Bn, Kn = (cut(E0 + 2048 + 1024 * n, NT, RW) for n in range(3))
        Zf = cut(E0 + 5120, NT, NH, 2 * HD)
        LGMH = side(4, NT, NH, 4 * P)
        XTb = side(8, NT, NH, P)
        Z1 = side(9, NT, NH, P)
        Lsb = side(9, NT, NH, P)
        Z2 = cut(BK0, NT, NH, P)
        PhiPsi = side(8, NCH, NP, 2 * HD)
        kmT = side(10, KC, T)
        vm = side(11, NT, D)
        soft = side(3, 2, 1024)
        St = cut(BK0, NCH, NP, HD)
        RhT = cut(BT0, NP, T)
        Y0 = cut(KT0, NT, RW)
        Yn = cut(P0 + 1024, NT, RW)
        prow = cut(GT0, P)[0:NROWS, :]
        lamv = cut(GT0 + 256, 4, HD)
        lora = cut(QD0 + 2048, RW)
        g2s = cut(QD0 + 2560, RW)
        atT = [cut(BT0 + 512 * n, 512) for n in range(2)]
        L16, X16, w16 = (cut(KT0 + 256 * n, SUB, SUB) for n in range(3))
        krs, kra, krb = (cut(KT0 + 256 * n, T) for n in range(3))
        odn = cut(XT0, NT, RW)
        dsq = cut(P0 + 3072, 512)
        sd = cut(P0 + 3072, NP, HD)
        bv = rT
        qx = cut(E0, KC, T)
        oT = cut(E0 + 2048, KC, T)
        px = cut(P0, 2, 2, T)
        pxT = cut(AR0, NT, 2, T)
        x3 = cut(XT0, NT, D)
        x3T = cut(E0, KC, T)
        n3g = cut(E0 + 2048, D)
        fing = cut(E0 + 3072, D)
        b1a = cut(E0 + 4096, 2 * F)
        b2a = cut(E0 + 6144, D)
        M0 = P0
        xe, xeT, gg, sg, ll, ac, acT, yy = (cut(M0 + 512 * n, 512) for n in range(8))
        sel = cut(M0 + 4096, NT, BLK)
        selg = cut(M0 + 4224, NT, P)
        GT = cut(M0 + 4480, T)
        onehot = cut(M0 + 4736, BLK)
        post = cut(M0 + 4800, NT, PASSES + 1, E)
        gate = cut(M0 + 5120, NT, E)
        mask = cut(M0 + 5184, NT, E)
        gateT = cut(M0 + 5248, T)
        lg = cut(M0 + 5504, NT, E)
        rt = cut(M0 + 5568, 256)

        ident = sb("ident", [P, P])
        masks = sb("masks", [P, 4, P])
        onesbd = sb("onesbd", [P, P])
        keep = sb("keep", [P, T])
        iota = sb("iota", [P, P])
        iotaE = sb("iotaE", [P, E])
        tri = sb("tri", [P, P])
        ones = sb("ones", [P, P])
        hsel = sb("hsel", [P, NP, NH])
        hselT = sb("hselT", [NH, NP, P])
        identE = sb("identE", [E, E + 1])
        prm = sb("prm", [P, NROWS])
        rws = sb("rws", [P, KC, E])
        rbs = sb("rbs", [1, E])
        mu1 = sb("mu1", [P, SHIFT // P])
        w0h = sb("w0h", [P, 8])
        tail = sb("tail", [P, NP, NCH])
        dec = sb("dec", [P, NP, NCH])
        st = sb("st", [P, 64])
        lam = sb("lam", [P, 8])
        dst_ = sb("dst_", [P, 64])
        xst = sb("xst", [P, 32])
        wk = sb("wk", [P, 64])
        ix8 = sb("ix8", [P, NT, 8], U32)
        npass = sb("npass", [1, 1], I32)

        blocks = nc.dram_tensor("blocks", (2, P // SUB, NT * NH, SUB, SUB), F32, kind="Internal").ap()

        filled = [sem(f"bank{b}_filled") for b in range(8)]
        drained = [sem(f"bank{b}_drained") for b in range(8)]
        where, count = {}, [0] * 8

        def place(name, bank):
            assert name not in where
            count[bank] += 1
            where[name] = (bank, count[bank])

        for s in ("mem", "x"):
            for n in range(4):
                place(f"{s}T{n}", 2 + n)
        place("prm", 6)
        for n in range(8):
            place(f"c{KV0 + n}", n % 2)
        for n in range(9):
            place(f"c{IN0 + n}", n % 2)
        for n in range(2):
            place(f"lw{n}", 2 + n)
            place(f"la{n}", 4 + n)
            place(f"lg{n}", 6 + n)
        place(f"c{IN0 + 9}", 1)
        place("ksum", 4)
        for n in range(2):
            place(f"kb{n}", 2 + n)
        for n in range(10, 13):
            place(f"c{IN0 + n}", n % 2)
        for n in range(2):
            place(f"bo{n}", 4 + n)
        for i in range(NT):
            for s in range(4):
                place(f"nat{i}{s}", (2, 3, 6, 7)[s])
        for i in range(NT):
            for n in range(NH):
                place(f"LGMH{i}{n}", 2 + n % 4)
            place(f"L{i}0", 6)
            place(f"L{i}1", 7)
        UNITS = [(0, (0, 1, 2, 3)), (1, (0, 1)), (1, (2, 3))]
        for u in range(3):
            place(f"sc{u}0", 0)
            place(f"sc{u}1", 1)
            place(f"at{u}", 2 + u % 2)
            if u != 1:
                place(f"od{UNITS[u][0]}", 4)
        for i in range(NT):
            place(f"MV{i}", 6 + i)
        for nm in ("z1", "z2", "z3"):
            for g in range(4):
                place(f"{nm}{g}", 2 + g)
        for i in range(NT):
            place(f"Rh{i}", 6)
            place(f"yz{i}", 7)
        for c in range(NCH - 1):
            place(f"PP{c}", 2 + c % 4)
        for i in range(NT):
            place(f"Y{i}0", 0)
            place(f"Y{i}1", 1)
            for c in range(4 * i, min(4 * i + 4, NCH - 1)):
                if c:
                    place(f"S{c}0", 6)
                    place(f"S{c}1", 7)
            if i == 0:
                place("odT0", 4)
                place("odT1", 5)
        for i in range(NT):
            place(f"ynT{i}", 2 + i)
        for n in range(4):
            place(f"c{OUT0 + n}", n % 2)
        for n in range(4):
            place(f"h1T{n}", 2 + n)
        for n in range(4):
            place(f"c{WQ0 + n}", n % 2)
        for n in range(XH // 2):
            for i in range(NT):
                place(f"xs{n}{i}", 2 + i)
            for i in range(NT):
                place(f"xp{n}{i}", 4 + i)
            for m in range(2):
                place(f"xo{n}{m}", 6 + m)
        for n in range(4):
            place(f"c{WO0 + n}", n % 2)
        for n in range(4):
            place(f"h2T{n}", 2 + n)
        place("logit", 6)
        place("pos", 7)
        place("gateT", 6)

        def begin(pe, name):
            b, k = where[name]
            if k > 1:
                pe.wait_ge(drained[b], k - 1)
            return ps[:, b, :]

        def done(ins, name):
            ins.then_inc(filled[where[name][0]], 1)

        def product(eng, name):
            b, k = where[name]
            eng.wait_ge(filled[b], k)
            return ps[:, b, :]

        def drain(ins, name):
            ins.then_inc(drained[where[name][0]], 1)

        def taken(eng, name):
            b, k = where[name]
            eng.wait_ge(drained[b], k)

        landed = [sem(f"slot{s}_landed") for s in range(PRE)]
        elanded = [sem(f"expert_chunk{c}_landed") for c in range(RING)]
        eused = sem("expert_chunks_used")

        mats = {n: a[n][0] for n in ("wkv_x", "w_in", "w_out", "wq_x", "wo_x")}

        def gbc(name, n0, n):
            r = ROW[name] + n0
            return prm[:, r:r + n].unsqueeze(2).to_broadcast([P, n, P])

        block = ctx.enter_context(nc.Block())

        @block.sync
        def _(sp):
            sp.dma_start(xs[:, :, :], a["mem"][0].rearrange("(i p) d -> p i d", p=P)).then_inc(sem("mem_in"), 16)
            sp.dma_start(h[:, :, :], a["x"][0].rearrange("(i p) d -> p i d", p=P)).then_inc(sem("x_in"), 16)
            def expert_chunk(e, c):
                if c < 8:
                    src = w1v[c, e]
                    dst = ring[:, c, :]
                else:
                    src = w2v[c - 8, e]
                    dst = ring[:, c, :].rearrange("p (j n) -> p j n", j=2)
                sp.dma_start(dst, src).then_inc(elanded[c], 16)

            w1v = a["moe_w1"][0].rearrange("e (c p) n -> c e p n", p=P)
            w2v = a["moe_w2"][0].rearrange("e (c j p) n -> c e p j n", p=P, j=2)
            for n, (w, c0) in enumerate(PRE_CHUNKS):
                if n == WQ0 + 1:
                    sp.wait_ge(sem("mixers_through"), 1)
                    for c in range(PRE, 10):
                        expert_chunk(0, c)
                if n >= PRE:
                    product(sp, f"c{n - PRE}")
                sp.dma_start(ring[:, n % PRE, :].rearrange("p (k n) -> p k n", k=KC),
                             mats[w][:, c0:c0 + WCOL].rearrange("(k p) n -> p k n", p=P)).then_inc(landed[n % PRE], 16)

            sp.wait_ge(sem("cross_through"), 1)
            for c in range(10, RING):
                expert_chunk(0, c)
            for c in range(PRE):
                product(sp, f"c{len(PRE_CHUNKS) - PRE + c}")
                expert_chunk(0, (len(PRE_CHUNKS) - PRE + c) % PRE)
            with sp.Fori(1, E) as e:
                for c in range(RING):
                    sp.wait_ge(eused, e * RING + (c - RING + 1))
                    expert_chunk(e, c)
            sp.wait_ge(sem("npass_ready"), 1)
            np_ = sp.value_load(npass[0:1, 0:1], min_val=1, max_val=PASSES)
            with sp.If(np_ > 1):
                with sp.Fori(1, np_) as q:
                    with sp.Fori(0, E) as e:
                        for c in range(RING):
                            sp.wait_ge(eused, q * (E * RING) + e * RING + (c - RING + 1))
                            expert_chunk(e, c)
            sp.wait_ge(sem("y_ready"), 2)
            sp.dma_start(out[0].rearrange("(i p) d -> p i d", p=P), x3[:, :, :]).then_inc(sem("out_written"), 16)
            sp.wait_ge(sem("out_written"), 16)

        @block.gpsimd
        def _(pool):
            g = nc.gpsimd
            n = [0]

            def link(ins):
                n[0] += 1
                ins.then_inc(sem("pool_step"), 1)
                pool.wait_ge(sem("pool_step"), n[0])

            link(g.memset(ident[:, :], 0.0))
            link(g.affine_select(out=ident[:, :], in_=ident[:, :], compare_op=ALU.not_equal, fill=1.0, base=0,
                                 pattern=[[-1, P]], channel_multiplier=1))
            pool.sem_inc(sem("ident_ready"), 1)
            g.memset(ones[:, :], 1.0).then_inc(sem("ones_ready"), 1)
            link(g.memset(onesbd[:, :], 1.0))
            link(g.affine_select(out=onesbd[:, 0:HD], in_=onesbd[:, 0:HD], compare_op=ALU.is_ge, fill=0.0, base=HD - 1,
                                 pattern=[[0, HD]], channel_multiplier=-1))
            link(g.affine_select(out=onesbd[:, HD:P], in_=onesbd[:, HD:P], compare_op=ALU.is_ge, fill=0.0, base=-HD,
                                 pattern=[[0, HD]], channel_multiplier=1))
            link(g.memset(keep[:, :], 1.0))
            link(g.memset(keep[:, 0:T:CH], 0.0))
            link(g.memset(masks[:, :, :], 1.0))
            for m in range(4):
                v = masks[:, m, :].rearrange("p (c t) -> p c t", t=CH)
                link(g.affine_select(out=v, in_=v, compare_op=ALU.is_ge, fill=0.0, base=0,
                                     pattern=[[-CH, P // CH], [0, CH]], channel_multiplier=1))
                link(g.affine_select(out=v, in_=v, compare_op=ALU.is_ge, fill=0.0, base=CH - 1 if m else SUB - 1,
                                     pattern=[[CH, P // CH], [0, CH]], channel_multiplier=-1))
                if m:
                    w = masks[:, m, :]
                    link(g.affine_select(out=w, in_=w, compare_op=ALU.is_ge, fill=0.0, base=-1 if m == 2 else 0,
                                         pattern=[[1, P]], channel_multiplier=-1))
                else:
                    link(g.affine_select(out=v, in_=v, compare_op=ALU.is_ge, fill=0.0, base=-SUB,
                                         pattern=[[0, P // CH], [1, CH]], channel_multiplier=0))
            link(g.memset(tri[:, :], 1.0))
            link(g.affine_select(out=tri[:, :], in_=tri[:, :], compare_op=ALU.is_ge, fill=0.0, base=-1,
                                 pattern=[[1, P]], channel_multiplier=-1))
            link(g.iota(iota[:, :].rearrange("p (a b) -> p a b", a=2), [[0, 2], [1, BLK]], base=0, channel_multiplier=0,
                        allow_small_or_imprecise_dtypes=True))
            link(g.iota(iotaE[:, :], [[1, E]], base=0, channel_multiplier=0, allow_small_or_imprecise_dtypes=True))
            link(g.memset(hsel[:, :, :], 0.0))
            for j in range(NP):
                link(g.memset(hsel[0:HD, j, 2 * j:2 * j + 1], 1.0))
                link(g.memset(hsel[HD:P, j, 2 * j + 1:2 * j + 2], 1.0))
            link(g.memset(hselT[:, :, :], 0.0))
            hv = hselT[:, :, :].rearrange("p j (q c) -> p j q c", q=2)
            link(g.affine_select(out=hv, in_=hv, compare_op=ALU.not_equal, fill=1.0, base=0,
                                 pattern=[[-2, NP], [-1, 2], [0, HD]], channel_multiplier=1))
            link(g.memset(identE[:, :], 0.0))
            link(g.affine_select(out=identE[:, 0:E], in_=identE[:, 0:E], compare_op=ALU.not_equal, fill=1.0, base=0,
                                 pattern=[[-1, E]], channel_multiplier=1))
            link(g.affine_select(out=identE[:, E:E + 1], in_=identE[:, E:E + 1], compare_op=ALU.not_equal, fill=1.0, base=0,
                                 pattern=[[0, 1]], channel_multiplier=1))
            link(g.memset(XTb[:, :, :, :], 0.0))
            pool.sem_inc(sem("const_ready"), 1)

            taken(pool, "L11")
            link(g.memset(X16[:, :, :], 0.0))
            g.affine_select(out=X16[:, :, :], in_=X16[:, :, :], compare_op=ALU.not_equal, fill=1.0, base=0,
                            pattern=[[1, SUB], [-1, SUB]], channel_multiplier=0).then_inc(sem("X16_unit"), 1)

        @block.scalar
        def _(act):
            s = nc.scalar
            n = [0]

            def link(ins):
                n[0] += 1
                ins.then_inc(sem("act_step"), 1)
                act.wait_ge(sem("act_step"), n[0])

            for name, rows in ROWS:
                src = a[name]
                src = src[0].rearrange("h n -> (h n)") if name == "r_k" else src[0]
                act.dma_start(prow[ROW[name]:ROW[name] + rows, :], src.rearrange("(r p) -> r p", p=P)).then_inc(sem("rows_in"), 16)
            act.dma_start(lora[0:64, :], a["w2"][0]).then_inc(sem("lora_in"), 16)
            act.dma_start(lora[64:128, :], a["a2"][0]).then_inc(sem("lora_in"), 16)
            act.dma_start(g2s[:, :], a["g2"][0]).then_inc(sem("lora_in"), 16)
            act.dma_start(rws[:, :, :], a["router_w"][0].rearrange("(k p) e -> p k e", p=P)).then_inc(sem("router_in"), 16)
            act.dma_start(rbs[:, :], a["router_b"]).then_inc(sem("router_in"), 16)
            for m, name in enumerate(("lam_q1", "lam_k1", "lam_q2", "lam_k2")):
                act.dma_start(lamv[:, m, :], a[name].to_broadcast([P, HD])).then_inc(sem("lam_in"), 16)

            def sumsq(src, col):
                for i in range(NT):
                    link(s.activation(t3scr, src[:, i, :], ACT.Square, accum_out=st[:, col + i:col + i + 1]))
                act.sem_inc(sem("stat_ready"), 1)

            t3scr = cut(P0, D)
            act.wait_ge(sem("mem_in"), 16)
            sumsq(xs, 0)
            act.wait_ge(sem("x_in"), 16)
            sumsq(h, 2)

            def copy(dst, name, view=None):
                src = product(act, name)
                drain(s.activation(dst, view(src) if view else src, ACT.Copy), name)

            two = lambda v: v.rearrange("p (a b) -> p a b", a=2)
            act.wait_ge(sem("lam_sum_ready"), 1)
            s.activation(lam[:, 2:4], lam[:, 0:2], ACT.Exp).then_inc(sem("lam_exp_ready"), 1)
            for m in range(4):
                copy(kmT[:, 2 * m:2 * m + 2, :], f"c{KV0 + m}", two)
            for m in range(4):
                copy(vm[:, :, m * WCOL:(m + 1) * WCOL], f"c{KV0 + 4 + m}", two)
            act.wait_ge(sem("mu_ready"), 1)
            for m in range(7):
                src = two(product(act, f"c{IN0 + m}"))
                for q in range(2):
                    j = 2 * m + q
                    s.activation(pT[:, j, :], src[:, q, :], ACT.Identity, scale=mu1[:, j:j + 1]).then_inc(sem("unshifted_ready"), 1)
            act.wait_ge(sem("shifted_ready"), 14)
            s.activation(pT[0:64, 12, :], pT[0:64, 12, :], ACT.Tanh).then_inc(sem("lora_x_ready"), 1)
            s.activation(pT[:, 13, :], pT[:, 13, :], ACT.Tanh, scale=0.5).then_inc(sem("gd_tanh_ready"), 1)
            for m in range(2):
                copy(qd[:, 2 * m:2 * m + 2, :], f"c{IN0 + 7 + m}", two)
            for m in range(2):
                for (z, dst, b0) in (("lw", lw, 0), ("la", aa, 4)):
                    src = two(product(act, f"{z}{m}"))
                    for q in range(2):
                        j = 2 * m + q
                        ins = s.activation(dst[:, j, :], src[:, q, :], ACT.Tanh, bias=w0h[:, b0 + j:b0 + j + 1], scale=0.5)
                        if q == 0:
                            link(ins)
                    drain(ins, f"{z}{m}")
                copy(gT[:, 2 * m:2 * m + 2, :], f"lg{m}", two)
            copy(kd[:, 0:2, :], f"c{IN0 + 9}", two)
            copy(kd[:, 2:4, :], f"c{IN0 + 10}", two)
            act.wait_ge(sem("cs_ready"), 1)
            s.activation(t1[:, :, :], cs[:, :, :], ACT.Exp).then_inc(sem("exp_ready"), 1)
            s.activation(dec[:, :, :], tail[:, :, :], ACT.Exp).then_inc(sem("exp_ready"), 1)
            act.wait_ge(sem("ex_ready"), 1)
            s.activation(lw[:, :, :], lw[:, :, :], ACT.Exp).then_inc(sem("exp_ready"), 1)
            act.wait_ge(sem("t1_free"), 1)
            s.activation(t1[:, :, :], cs[:, :, :], ACT.Exp, scale=-1.0).then_inc(sem("exp_ready"), 1)
            act.wait_ge(sem("rest_ready"), 1)
            s.activation(t3[:, :, :], t3[:, :, :], ACT.Exp).then_inc(sem("exp_ready"), 1)
            act.wait_ge(sem("t3_free"), 1)
            for m in range(2):
                copy(vd[:, :, m * WCOL:(m + 1) * WCOL], f"c{IN0 + 11 + m}", two)
            for i in range(NT):
                copy(Zr[:, i, :, 0:HD], f"nat{i}0", lambda v: v.rearrange("p (h k) -> p h k", h=NH))
                copy(Vn[:, i, :], f"nat{i}1")
            for i in range(NT):
                for q in range(2):
                    copy(Lsb[:, i, q:NH:2, :], f"L{i}{q}", lambda v: v.rearrange("p (h k) -> p h k", h=NP))
                    act.wait_ge(drained[where[f"L{i}{q}"][0]], where[f"L{i}{q}"][1])
            for j in range(P // SUB):
                act.dma_start(blocks[0, j].rearrange("q a b -> a q b"),
                              Lsb[SUB * j:SUB * j + SUB, :, :, SUB * j:SUB * j + SUB].rearrange("a i h b -> a (i h) b"))\
                   .then_inc(sem("L_blocks_out"), 16)
            act.wait_ge(sem("L_blocks_out"), 16 * (P // SUB))
            act.dma_start(L16[:, :, :], blocks[0].rearrange("j q a b -> (j q) a b")).then_inc(sem("L16_in"), 16)

            for u, (i, heads) in enumerate(UNITS):
                act.wait_ge(sem("dmax_ready"), u + 1)
                w = P * (i + 1)
                if u:
                    act.wait_ge(sem("soft_free"), u)
                for c in range(2):
                    src = ps[:, where[f"sc{u}{c}"][0], :]
                    for m, hh in enumerate(heads):
                        col = 8 * u + 4 * c + m
                        ins = s.activation(soft[:, c, m * w:(m + 1) * w], src[:, m * w:(m + 1) * w], ACT.Exp, scale=DSCALE,
                                           bias=dst_[:, col:col + 1], accum_out=dst_[:, 32 + col:33 + col])
                        if m < len(heads) - 1:
                            link(ins)
                    drain(ins, f"sc{u}{c}")
                    act.wait_ge(drained[where[f"sc{u}{c}"][0]], where[f"sc{u}{c}"][1])
                act.sem_inc(sem("dexp_ready"), 1)

            act.wait_ge(sem("X16_ready"), 1)
            act.wait_ge(sem("const_ready"), 1)
            act.dma_start(blocks[1].rearrange("j q a b -> (j q) a b"), X16[:, :, :]).then_inc(sem("X_blocks_out"), 16)
            act.wait_ge(sem("X_blocks_out"), 16)
            for j in range(P // SUB):
                act.dma_start(XTb[SUB * j:SUB * j + SUB, :, :, SUB * j:SUB * j + SUB].rearrange("c i h a -> c (i h) a"),
                              blocks[1, j].rearrange("q c a -> c q a")).then_inc(sem("XT_in"), 16)
            for i in range(NT):
                copy(Zr[:, i, :, HD:P], f"MV{i}", lambda v: v.rearrange("p (h k) -> p h k", h=NH))
            four = lambda v: v.rearrange("p (h k) -> p h k", h=4)
            for q in range(4):
                copy(Z1[:, q // 2, 4 * (q % 2):4 * (q % 2) + 4, :], f"z1{q}", four)
            for q in range(4):
                copy(Z2[:, q // 2, 4 * (q % 2):4 * (q % 2) + 4, :], f"z2{q}", four)
            for i in range(NT):
                copy(Y0[:, i, :], f"yz{i}")
            for c in range(NCH - 1):
                copy(PhiPsi[:, c, :, :], f"PP{c}", four)
            act.wait_ge(sem("sub_gain_ready"), 1)
            for i in range(NT):
                o = product(act, f"odT{i}")
                drain(s.activation(xT[:, NP:KC, i * P:(i + 1) * P], four(o), ACT.Copy, scale=lam[:, 5:6]), f"odT{i}")
            act.wait_ge(sem("h_ready"), 1)
            sumsq(h, 4)
            for m in range(4):
                copy(qx[:, 2 * m:2 * m + 2, :], f"c{WQ0 + m}", two)
            for m in range(XH // 2):
                for i in range(NT):
                    act.wait_ge(sem("xmax_ready"), 2 * m + i + 1)
                    src = two(ps[:, where[f"xs{m}{i}"][0], :])
                    if m:
                        taken(act, f"xp{m - 1}{i}")
                    for q in range(2):
                        col = 4 * m + 2 * i + q
                        ins = s.activation(px[:, i, q, :], src[:, q, :], ACT.Exp, scale=XSCALE, bias=xst[:, col:col + 1],
                                           accum_out=xst[:, 8 + col:9 + col])
                        if q == 0:
                            link(ins)
                    drain(ins, f"xs{m}{i}")
                for q in range(2):
                    copy(oT[:, 4 * m + 2 * q:4 * m + 2 * q + 2, :], f"xo{m}{q}", two)
            act.wait_ge(sem("h_ready"), 2)
            sumsq(h, 6)
            taken(act, f"c{WO0 + 3}")
            act.dma_start(n3g[:, :], a["norm3_g"].to_broadcast([P, D])).then_inc(sem("n3g_in"), 16)
            act.dma_start(fing[:, :], a["final_g"].unsqueeze(0).to_broadcast([P, D])).then_inc(sem("fing_in"), 16)
            act.dma_start(b1a[0:E, :], a["moe_b1"][0]).then_inc(sem("bias_in"), 16)
            act.dma_start(b2a[0:E, :], a["moe_b2"][0]).then_inc(sem("bias_in"), 16)
            for i in range(NT):
                act.wait_ge(sem("top_ready"), i + 1)
                s.activation(rt[:, 16 * i + 8:16 * i + 12], rt[:, 16 * i:16 * i + 4], ACT.Exp, bias=rt[:, 16 * i + 12:16 * i + 13],
                             accum_out=rt[:, 16 * i + 13:16 * i + 14]).then_inc(sem("gexp_ready"), 1)

            act.wait_ge(sem("npass_ready"), 1)
            act.wait_ge(sem("xe_filled"), 1)
            s.activation(xe[:, :], ps[:, 6, :], ACT.Copy).then_inc(sem("xe_ready"), 1)
            np_ = act.value_load(npass[0:1, 0:1], min_val=1, max_val=PASSES)
            with act.Fori(0, np_) as q:
                with act.Fori(0, E) as e:
                    it = act.snap(q * E + e)
                    act.wait_ge(sem("gate_ready"), it + 1)
                    s.activation(sg[:, :], gg[:, :], ACT.Sigmoid, scale=1.702).then_inc(sem("sig_ready"), 1)
                    act.wait_ge(sem("GT_filled"), it + 1)
                    s.activation(GT[:, :], ps[:, 7, 0:T], ACT.Copy).then_inc(sem("GT_ready"), 1)
                    act.wait_ge(sem("xe_filled"), it + 2)
                    s.activation(xe[:, :], ps[:, 6, :], ACT.Copy).then_inc(sem("xe_ready"), 1)
                    act.wait_ge(sem("acT_filled"), it + 1)
                    s.activation(acT[:, :], ps[:, 7, :], ACT.Copy).then_inc(sem("acT_ready"), 1)
            act.wait_ge(sem("h_ready"), 3)
            sumsq(h, 32)

        @block.tensor
        def _(pe):
            t = nc.tensor

            def weights(n):
                pe.wait_ge(landed[n % PRE], 16 * (n // PRE + 1))
                return ring[:, n % PRE, :].rearrange("p (k n) -> p k n", k=KC)

            def turned(n, src):
                w = weights(n)
                o = begin(pe, f"c{n}")
                for q in range(2):
                    for k in range(KC):
                        ins = t.matmul(o[:, q * T:(q + 1) * T], w[:, k, q * P:(q + 1) * P], src[:, k, :],
                                       start=(k == 0), stop=(k == KC - 1))
                done(ins, f"c{n}")

            def natural(n, src):
                w = weights(n)
                o = begin(pe, f"c{n}")
                for i in range(NT):
                    for k in range(KC):
                        ins = t.matmul(o[:, i * WCOL:(i + 1) * WCOL], src[:, k, i * P:(i + 1) * P], w[:, k, :],
                                       start=(k == 0), stop=(k == KC - 1))
                done(ins, f"c{n}")

            def turn4(name, srcs):
                o = begin(pe, name)
                for q, v in enumerate(srcs):
                    ins = t.transpose(o[:, q * P:(q + 1) * P], v, ident[:, :])
                done(ins, name)

            def turn_rows(s, k):
                pe.wait_ge(sem("scaled_ready"), k)
                for i in range(NT):
                    for q in range(2):
                        turn4(f"{s}T{2 * i + q}", [xs[:, i, (4 * q + m) * P:(4 * q + m + 1) * P] for m in range(4)])

            pe.wait_ge(sem("ident_ready"), 1)
            turn_rows("mem", 1)
            turn_rows("x", 2)
            pe.wait_ge(sem("rows_in"), 16 * len(ROWS))
            o = begin(pe, "prm")
            done(t.transpose(o[:, 0:NROWS], prow[:, :], ident[0:NROWS, 0:NROWS]), "prm")
            pe.wait_ge(sem("memT_ready"), 1)
            for m in range(4):
                turned(KV0 + m, memT)
            for m in range(4, 8):
                natural(KV0 + m, memT)
            for q in range(4):
                taken(pe, f"xT{q}")
            for m in range(9):
                turned(IN0 + m, xT)
            pe.wait_ge(sem("lora_in"), 48)
            pe.wait_ge(sem("lora_x_ready"), 1)
            pe.wait_ge(sem("gd_ready"), 1)
            for m in range(2):
                for nm, lo, hi, lw_, rhs in (("lw", 0, 64, lora, 12), ("la", 64, 128, lora, 12), ("lg", 0, 128, g2s, 13)):
                    o = begin(pe, f"{nm}{m}")
                    for q in range(2):
                        j = 2 * m + q
                        ins = t.matmul(o[:, q * T:(q + 1) * T], lw_[lo:hi, j * P:(j + 1) * P], pT[lo:hi, rhs, :], start=True, stop=True)
                    done(ins, f"{nm}{m}")
            turned(IN0 + 9, xT)
            pe.wait_ge(sem("kksq_ready"), 1)
            pe.wait_ge(sem("const_ready"), 1)
            o = begin(pe, "ksum")
            for j in range(NP):
                ins = t.matmul(o[0:NH, 0:T], hsel[:, j, :], t2[:, j, :], start=(j == 0), stop=(j == NP - 1))
            done(ins, "ksum")
            turned(IN0 + 10, xT)
            pe.wait_ge(sem("knorm_ready"), 1)
            for m in range(2):
                o = begin(pe, f"kb{m}")
                for q in range(2):
                    ins = t.matmul(o[:, q * T:(q + 1) * T], hselT[:, 2 * m + q, :], krs[0:NH, :], start=True, stop=True)
                done(ins, f"kb{m}")
            natural(IN0 + 11, xT)
            natural(IN0 + 12, xT)
            pe.wait_ge(sem("rk_ready"), 1)
            for m in range(2):
                o = begin(pe, f"bo{m}")
                done(t.matmul(o[:, :], onesbd[:, :], t1[:, 2 * m:2 * m + 2, :].rearrange("p a b -> p (a b)"), start=True, stop=True), f"bo{m}")
            pe.wait_ge(sem("ops_ready"), 1)
            for i in range(NT):
                tok = slice(i * P, (i + 1) * P)
                turn4(f"nat{i}0", [AR[:, j, i, 0, :] for j in range(NP)])
                turn4(f"nat{i}1", [vT[:, j, tok] for j in range(NP)])
                turn4(f"nat{i}2", [Bd[:, j, tok] for j in range(NP)])
                turn4(f"nat{i}3", [Kd[:, j, tok] for j in range(NP)])
            for i in range(NT):
                tok = slice(i * P, (i + 1) * P)
                oL = [begin(pe, f"L{i}{q}") for q in range(2)]
                for hh in range(NH):
                    j, q = hh // 2, hh % 2
                    rows = slice(q * HD, (q + 1) * HD)
                    ar = AR[rows, j, i, :, :].rearrange("p a b -> p (a b)")
                    o = begin(pe, f"LGMH{i}{hh}")
                    t.matmul(o[:, 0:T], BT[rows, j, tok], ar, start=True, stop=True)
                    done(t.matmul(o[:, T:2 * T], KT[rows, j, tok], ar, start=True, stop=True), f"LGMH{i}{hh}")
                    ins = t.matmul(oL[q][:, j * P:(j + 1) * P], AR[rows, j, i, 0, :], BT[rows, j, tok], start=True, stop=True)
                    if j == NP - 1:
                        done(ins, f"L{i}{q}")
            for m in range(7, 13):
                taken(pe, f"c{IN0 + m}")
            for u, (i, heads) in enumerate(UNITS):
                w = P * (i + 1)
                o = [begin(pe, f"sc{u}{c}") for c in range(2)]
                for m, hh in enumerate(heads):
                    for c in range(2):
                        rows = slice(c * HD, (c + 1) * HD)
                        ins = t.matmul(o[c][:, m * w:(m + 1) * w], qd[rows, hh, i * P:(i + 1) * P], kd[rows, hh, 0:w], start=True, stop=True)
                        if m == len(heads) - 1:
                            done(ins, f"sc{u}{c}")
                pe.wait_ge(sem("attn_ready"), u + 1)
                turn4(f"at{u}", [soft[:, 0, m * P:(m + 1) * P] for m in range(4)])
                if u != 2:
                    oo = begin(pe, f"od{i}")
                taken(pe, f"at{u}")
                for m, hh in enumerate(heads):
                    for kb in range(i + 1):
                        ins = t.matmul(oo[:, hh * P:(hh + 1) * P], atT[u % 2][:, (m * (i + 1) + kb) * P:(m * (i + 1) + kb + 1) * P],
                                       vd[:, kb, hh * P:(hh + 1) * P], start=(kb == 0), stop=(kb == i))
                if u != 1:
                    done(ins, f"od{i}")
            for i in range(NT):
                o = begin(pe, f"MV{i}")
                for hh in range(NH):
                    if hh == 0:
                        taken(pe, f"LGMH{i}7")
                        taken(pe, f"LGMH{i}6")
                        taken(pe, f"LGMH{i}5")
                        taken(pe, f"LGMH{i}4")
                        taken(pe, f"nat{i}1")
                    ins = t.matmul(o[:, hh * HD:(hh + 1) * HD], LGMH[:, i, hh, 2 * P:3 * P], Vn[:, i, hh * HD:(hh + 1) * HD],
                                   start=True, stop=True)
                done(ins, f"MV{i}")
            pe.wait_ge(sem("XT_in"), 16 * (P // SUB))

            def pairs(nm, left, right, before):
                for g in range(4):
                    before(g)
                    o = begin(pe, f"{nm}{g}")
                    for m in range(4):
                        i, hh = g // 2, 4 * (g % 2) + m
                        ins = t.matmul(o[:, m * P:(m + 1) * P], left(i, hh), right(i, hh), start=True, stop=True)
                    done(ins, f"{nm}{g}")

            pairs("z1", lambda i, hh: XTb[:, i, hh, :], lambda i, hh: Zr[:, i, hh, :], lambda g: taken(pe, f"MV{g // 2}"))
            pairs("z2", lambda i, hh: LGMH[:, i, hh, 0:P], lambda i, hh: Z1[:, i, hh, :], lambda g: taken(pe, f"z1{g}"))
            pairs("z3", lambda i, hh: XTb[:, i, hh, :], lambda i, hh: Z2[:, i, hh, :], lambda g: taken(pe, f"z2{g}"))
            for q in range(4):
                taken(pe, f"z3{q}")
            for i in range(NT):
                tok = slice(i * P, (i + 1) * P)
                o = begin(pe, f"Rh{i}")
                for hh in range(NH):
                    j, q = hh // 2, hh % 2
                    ins = t.matmul(o[q * HD:(q + 1) * HD, j * P:(j + 1) * P], Zf[:, i, hh, 0:HD], LGMH[:, i, hh, P:2 * P],
                                   start=True, stop=True)
                done(ins, f"Rh{i}")
                o = begin(pe, f"yz{i}")
                for hh in range(NH):
                    t.matmul(o[:, hh * HD:(hh + 1) * HD], LGMH[:, i, hh, P:2 * P], Zf[:, i, hh, HD:P], start=True, stop=False)
                    ins = t.matmul(o[:, hh * HD:(hh + 1) * HD], LGMH[:, i, hh, 3 * P:4 * P], Vn[:, i, hh * HD:(hh + 1) * HD],
                                   start=False, stop=True)
                done(ins, f"yz{i}")
            for i in range(NT):
                chunks = [c for c in range(4 * i, 4 * i + 4) if c < NCH - 1]
                os_ = {c: begin(pe, f"PP{c}") for c in chunks}
                for hh in range(NH):
                    j, q = hh // 2, hh % 2
                    col = slice(hh * HD, (hh + 1) * HD)
                    for step in range(3):
                        for c in chunks:
                            r = slice(CH * (c % 4), CH * (c % 4) + CH)
                            at = os_[c][q * HD:(q + 1) * HD, j * P + (HD if step else 0):j * P + (2 * HD if step else HD)]
                            left, right = ((Zf[r, i, hh, 0:HD], Bn[r, i, col]), (Bn[r, i, col], Zf[r, i, hh, HD:P]),
                                           (Kn[r, i, col], Vn[r, i, col]))[step]
                            ins = t.matmul(at, left, right, start=(step < 2), stop=(step != 1),
                                           tile_position=(CH * (c % 4), q * HD))
                            if step == 2 and hh == NH - 1:
                                done(ins, f"PP{c}")
            for i in range(NT):
                oy = [begin(pe, f"Y{i}{q}") for q in range(2)]
                for c in range(4 * i, 4 * i + 4):
                    pe.wait_ge(sem("S_ready"), c + 1)
                    if c == 0:
                        taken(pe, "Rh0")
                        taken(pe, "Rh1")
                    if 0 < c < NCH - 1:
                        taken(pe, f"PP{c}")
                        o = [begin(pe, f"S{c}{q}") for q in range(2)]
                        for j in range(NP):
                            for q in range(2):
                                rows = slice(q * HD, (q + 1) * HD)
                                ins = t.matmul(o[q][rows, j * HD:(j + 1) * HD], PhiPsi[rows, c, j, 0:HD], St[rows, c, j, :],
                                               start=True, stop=True)
                                if j == NP - 1:
                                    done(ins, f"S{c}{q}")
                    r = slice(CH * (c % 4), CH * (c % 4) + CH)
                    for j in range(NP):
                        for q in range(2):
                            rows = slice(q * HD, (q + 1) * HD)
                            ins = t.matmul(oy[q][r, j * HD:(j + 1) * HD], RhT[rows, j, c * CH:(c + 1) * CH], St[rows, c, j, :],
                                           start=True, stop=True, tile_position=(q * HD, CH * (c % 4)))
                            if j == NP - 1 and c % 4 == 3:
                                done(ins, f"Y{i}{q}")
                if i == 0:
                    pe.wait_ge(sem("odn_ready"), 1)
                    for i2 in range(NT):
                        turn4(f"odT{i2}", [odn[:, i2, m * P:(m + 1) * P] for m in range(4)])
            pe.wait_ge(sem("yn_ready"), 1)
            for i in range(NT):
                turn4(f"ynT{i}", [Yn[:, i, m * P:(m + 1) * P] for m in range(4)])
            t.sem_inc(sem("mixers_through"), 1)
            pe.wait_ge(sem("yT_ready"), 1)
            for i in range(NT):
                taken(pe, f"odT{i}")
            for m in range(4):
                natural(OUT0 + m, xT)
            turn_rows("h1", 3)
            for q in range(4):
                taken(pe, f"h1T{q}")
            for m in range(4):
                turned(WQ0 + m, xT)
            for m in range(4):
                taken(pe, f"c{WQ0 + m}")
            for m in range(XH // 2):
                for i in range(NT):
                    o = begin(pe, f"xs{m}{i}")
                    for q in range(2):
                        for k in range(2):
                            c = 2 * (2 * m + q) + k
                            ins = t.matmul(o[:, q * T:(q + 1) * T], qx[:, c, i * P:(i + 1) * P], kmT[:, c, :], start=(k == 0), stop=(k == 1))
                    done(ins, f"xs{m}{i}")
                pe.wait_ge(sem("xp_ready"), 2 * m + 2)
                for i in range(NT):
                    turn4(f"xp{m}{i}", [px[:, i, q, kb * P:(kb + 1) * P] for q in range(2) for kb in range(2)])
                for i in range(NT):
                    taken(pe, f"xp{m}{i}")
                for q in range(2):
                    o = begin(pe, f"xo{m}{q}")
                    for c in range(2):
                        for kb in range(2):
                            col = (2 * m + q) * T + c * P
                            ins = t.matmul(o[:, c * T:(c + 1) * T], vm[:, kb, col:col + P], pxT[:, kb, q, :], start=(kb == 0), stop=(kb == 1))
                    done(ins, f"xo{m}{q}")
            for m in range(XH // 2):
                for q in range(2):
                    taken(pe, f"xo{m}{q}")
            t.sem_inc(sem("cross_through"), 1)
            for m in range(4):
                natural(WO0 + m, oT)
            turn_rows("h2", 4)
            for q in range(4):
                taken(pe, f"h2T{q}")
            pe.wait_ge(sem("router_in"), 32)
            o = begin(pe, "logit")
            for i in range(NT):
                for k in range(KC):
                    t.matmul(o[:, i * E:(i + 1) * E], x3T[:, k, i * P:(i + 1) * P], rws[:, k, :], start=(k == 0), stop=False)
                ins = t.matmul(o[:, i * E:(i + 1) * E], ones[0:1, :], rbs[:, :], start=False, stop=True)
            done(ins, "logit")
            pe.wait_ge(sem("mask_ready"), 1)
            o = begin(pe, "pos")
            t.matmul(o[:, 0:E], tri[:, :], mask[:, 0, :], start=True, stop=True)
            t.matmul(o[:, E:2 * E], tri[:, :], mask[:, 1, :], start=True, stop=False)
            t.matmul(o[:, E:2 * E], ones[:, :], mask[:, 0, :], start=False, stop=True)
            t.matmul(o[0:1, 2 * E:3 * E], ones[:, 0:1], mask[:, 0, :], start=True, stop=False)
            done(t.matmul(o[0:1, 2 * E:3 * E], ones[:, 0:1], mask[:, 1, :], start=False, stop=True), "pos")
            pe.wait_ge(sem("gates_ready"), 1)
            o = begin(pe, "gateT")
            for i in range(NT):
                ins = t.transpose(o[0:E, i * P:(i + 1) * P], gate[:, i, :], ident[:, :])
            done(ins, "gateT")
            taken(pe, "gateT")
            pe.wait_ge(sem("bias_in"), 32)
            for b, nm in ((0, f"c{WO0 + 2}"), (1, f"c{WO0 + 3}"), (2, "h2T0"), (3, "h2T1")):
                taken(pe, nm)
            for i in range(NT):
                for c in range(2):
                    t.matmul(ps[:, 2 * i + c, :], gateT[0:E, i * P:(i + 1) * P], b2a[0:E, c * 512:(c + 1) * 512],
                             start=True, stop=False, skip_group_check=True)

            def gather():
                for i in range(NT):
                    for c in range(2):
                        ins = t.matmul(ps[c * BLK:(c + 1) * BLK, 6, :], sel[:, i, :], x3[:, i, c * 512:(c + 1) * 512],
                                       start=(i == 0), stop=(i == NT - 1), skip_group_check=True)
                ins.then_inc(sem("xe_filled"), 1)

            def gather_turn():
                for m in range(4):
                    ins = t.transpose(ps[:, 6, m * P:(m + 1) * P], xe[:, m * P:(m + 1) * P], ident[:, :])
                ins.then_inc(sem("xeT_filled"), 1)

            def gate_turn():
                for i in range(NT):
                    ins = t.transpose(ps[:, 7, i * P:(i + 1) * P], selg[:, i, :], ident[:, :])
                ins.then_inc(sem("GT_filled"), 1)

            def scatter():
                for i in range(NT):
                    for c in range(2):
                        rows = slice(c * BLK, (c + 1) * BLK)
                        ins = t.matmul(ps[:, 2 * i + c, :], GT[rows, i * P:(i + 1) * P], yy[rows, :], start=False, stop=False,
                                       skip_group_check=True)
                ins.then_inc(sem("scattered"), 1)

            for b, nm in ((4, "xp10"), (5, "xp11"), (6, "gateT"), (7, "pos")):
                taken(pe, nm)
            taken(pe, "h2T2")
            taken(pe, "h2T3")
            pe.wait_ge(sem("sel_ready"), 2)
            pe.wait_ge(sem("x3_ready"), 1)
            gather()
            pe.wait_ge(sem("xe_ready"), 1)
            gather_turn()
            pe.wait_ge(sem("npass_ready"), 1)
            np_ = pe.value_load(npass[0:1, 0:1], min_val=1, max_val=PASSES)
            with pe.Fori(0, np_) as q_:
                with pe.Fori(0, E) as e:
                    it = pe.snap(q_ * E + e)
                    pe.wait_ge(sem("onehot_ready"), it + 1)
                    pe.wait_ge(sem("lin_read"), it + 1)
                    for b in range(2):
                        for c in range(2):
                            f0 = b * F + c * 512
                            t.matmul(ps[c * BLK:(c + 1) * BLK, 4 + b, :], onehot[0:E, :], b1a[0:E, f0:f0 + 512], start=True, stop=False,
                                     skip_group_check=True)
                    pe.wait_ge(sem("xeT_ready"), it + 1)
                    for k in range(KC):
                        pe.wait_ge(elanded[k], it * 16 + 16)
                        for b in range(2):
                            for c in range(2):
                                f0 = b * F + c * 512
                                col = (k % 4) * P + (k // 4) * BLK
                                ins = t.matmul(ps[c * BLK:(c + 1) * BLK, 4 + b, :], xeT[:, col:col + BLK], ring[:, k, f0:f0 + 512],
                                               start=False, stop=(k == KC - 1), skip_group_check=True)
                        if k < KC - 1:
                            ins.then_inc(eused, 1)
                        else:
                            ins.then_inc(sem("hid_filled"), 1)
                    pe.wait_ge(sem("GT_ready"), it + 1)
                    pe.wait_ge(sem("yy_ready"), it + 1)
                    scatter()
                    pe.wait_ge(sem("selg_ready"), it * 2 + 2)
                    gate_turn()
                    pe.wait_ge(sem("hid_filled"), it + 1)
                    t.sem_inc(eused, 1)
                    pe.wait_ge(sem("sel_ready"), it * 2 + 4)
                    gather()
                    pe.wait_ge(sem("GT_ready"), it + 2)
                    pe.wait_ge(sem("ac_ready"), it + 1)
                    for m in range(4):
                        ins = t.transpose(ps[:, 7, m * P:(m + 1) * P], ac[:, m * P:(m + 1) * P], ident[:, :])
                    ins.then_inc(sem("acT_filled"), 1)
                    pe.wait_ge(sem("xe_ready"), it + 2)
                    gather_turn()
                    pe.wait_ge(sem("acT_ready"), it + 1)
                    for k in range(KC):
                        if k % 2 == 0:
                            pe.wait_ge(elanded[8 + k // 2], it * 16 + 16)
                        w = ring[:, 8 + k // 2, (k % 2) * D:(k % 2 + 1) * D]
                        col = (k % 4) * P + (k // 4) * BLK
                        for c in range(2):
                            ins = t.matmul(ps[c * BLK:(c + 1) * BLK, 7, :], acT[:, col:col + BLK], w[:, c * 512:(c + 1) * 512],
                                           start=(k == 0), stop=(k == KC - 1), skip_group_check=True)
                        if k % 2 and k < KC - 1:
                            ins.then_inc(eused, 1)
                    ins.then_inc(sem("yy_filled"), 1)
                    pe.wait_ge(sem("yy_filled"), it + 1)
                    t.sem_inc(eused, 1)
            n_it = pe.snap(np_ * E)
            pe.wait_ge(sem("GT_ready"), n_it + 1)
            pe.wait_ge(sem("yy_ready"), n_it + 1)
            for i in range(NT):
                for c in range(2):
                    rows = slice(c * BLK, (c + 1) * BLK)
                    ins = t.matmul(ps[:, 2 * i + c, :], GT[rows, i * P:(i + 1) * P], yy[rows, :], start=False, stop=True,
                                   skip_group_check=True)
            ins.then_inc(sem("sum_ready"), 1)

        @block.vector
        def _(dve):
            v = nc.vector
            n = [0]

            def link(ins):
                n[0] += 1
                ins.then_inc(sem("dve_step"), 1)
                dve.wait_ge(sem("dve_step"), n[0])

            def dlink(ins, name):
                drain(ins, name)
                taken(dve, name)

            four = lambda x: x.rearrange("p (h k) -> p h k", h=4)
            two = lambda x: x.rearrange("p (a b) -> p a b", a=2)

            def rsqrt(y, x, s1, s2):
                link(v.tensor_scalar(s1, x, -0.5, None, ALU.mult))
                link(v.tensor_scalar(y.bitcast(I32), x.bitcast(I32), -0.5, 1597463007.0, ALU.mult, ALU.add))
                for _ in range(4):
                    link(v.tensor_tensor(s2, y, y, ALU.mult))
                    link(v.tensor_tensor(s2, s2, s1, ALU.mult))
                    link(v.scalar_tensor_tensor(out=y, in0=s2, scalar=1.5, in1=y, op0=ALU.add, op1=ALU.mult))

            def rstd(c0, c1, width, eps):
                x = st[:, c0:c1]
                link(v.tensor_scalar(x, x, 1.0 / width, eps, ALU.mult, ALU.add))
                rsqrt(x, x, wk[:, 0:c1 - c0], wk[:, 32:32 + c1 - c0])

            def scale_rows(src, col, k):
                dve.wait_ge(sem("stat_ready"), k)
                rstd(col, col + 2, D, EPS)
                for i in range(NT):
                    link(v.tensor_scalar(xs[:, i, :], src[:, i, :], st[:, col + i:col + i + 1], None, ALU.mult))
                dve.sem_inc(sem("scaled_ready"), 1)

            def take_rows(s, dst, g):
                for i in range(NT):
                    for q in range(2):
                        nm = f"{s}T{2 * i + q}"
                        o = four(product(dve, nm))
                        drain(v.tensor_tensor(dst[:, 4 * q:4 * q + 4, i * P:(i + 1) * P], o, gbc(g, 4 * q, 4), ALU.mult), nm)

            scale_rows(xs, 0, 1)
            for i in range(NT):
                for q in range(2):
                    nm = f"memT{2 * i + q}"
                    drain(v.tensor_copy(memT[:, 4 * q:4 * q + 4, i * P:(i + 1) * P], four(product(dve, nm))), nm)
            scale_rows(h, 2, 2)
            o = product(dve, "prm")
            for q in range(4):
                product(dve, f"xT{q}")
            dlink(v.tensor_copy(prm[:, :], o[:, 0:NROWS]), "prm")
            link(v.tensor_tensor(memT[:, :, :], memT[:, :, :], prm[:, ROW["mem_norm_g"]:ROW["mem_norm_g"] + KC].unsqueeze(2)
                                 .to_broadcast([P, KC, T]), ALU.mult))
            dve.sem_inc(sem("memT_ready"), 1)
            take_rows("x", xT, "norm1_g")
            link(v.tensor_scalar(mu1[:, :], prm[:, ROW["mu_shift"]:ROW["mu_shift"] + 14], -1.0, 1.0, ALU.mult, ALU.add))
            dve.sem_inc(sem("mu_ready"), 1)
            link(v.tensor_scalar(w0h[:, :], prm[:, ROW["w0"]:ROW["w0"] + 8], 0.5, None, ALU.mult))
            dve.wait_ge(sem("lam_in"), 64)
            for m in range(2):
                link(v.tensor_tensor(lamv[:, 2 * m, :], lamv[:, 2 * m, :], lamv[:, 2 * m + 1, :], ALU.mult))
                link(v.reduce_sum(lam[:, m:m + 1], lamv[:, 2 * m, :], AX.X))
            dve.sem_inc(sem("lam_sum_ready"), 1)
            link(v.tensor_scalar(lam[:, 5:6], prm[:, ROW["subln_g"]:ROW["subln_g"] + 1], 1.0 - LAMBDA_INIT, None, ALU.mult))
            dve.sem_inc(sem("sub_gain_ready"), 1)
            dve.wait_ge(sem("const_ready"), 1)

            for m in range(7):
                src = two(product(dve, f"c{IN0 + m}"))
                dve.wait_ge(sem("unshifted_ready"), 2 * m + 2)
                for q in range(2):
                    j = 2 * m + q
                    mu = prm[:, ROW["mu_shift"] + j:ROW["mu_shift"] + j + 1]
                    ins = v.scalar_tensor_tensor(out=pT[:, j, 1:T], in0=src[:, q, 0:T - 1], scalar=mu, in1=pT[:, j, 1:T],
                                                 op0=ALU.mult, op1=ALU.add)
                    if q == 0:
                        link(ins)
                dlink(ins, f"c{IN0 + m}")
                dve.sem_inc(sem("shifted_ready"), 2)

            pr = lambda nm, j: prm[:, ROW[nm] + j:ROW[nm] + j + 1]
            for j in range(NP):
                link(v.tensor_scalar(kk[:, j, :], kT[:, j, :], pr("k_k", j), None, ALU.mult))
            link(v.tensor_tensor(t2[:, :, :], kk[:, :, :], kk[:, :, :], ALU.mult))
            dve.sem_inc(sem("kksq_ready"), 1)
            dve.wait_ge(sem("gd_tanh_ready"), 1)
            link(v.tensor_scalar(pT[:, 13, :], pT[:, 13, :], 0.5, 0.5, ALU.mult, ALU.add))
            dve.sem_inc(sem("gd_ready"), 1)
            o = product(dve, "ksum")
            dlink(v.tensor_scalar(krs[0:NH, :], o[0:NH, 0:T], 1e-24, None, ALU.max), "ksum")
            rsqrt(krs[0:NH, :], krs[0:NH, :], kra[0:NH, :], krb[0:NH, :])
            dve.sem_inc(sem("knorm_ready"), 1)
            for m in range(2):
                taken(dve, f"lw{m}")
                taken(dve, f"la{m}")
            link(v.tensor_scalar(lw[:, :, :], lw[:, :, :], 1.0, 0.5 * NEG_EXP_HALF, ALU.add, ALU.mult))
            for j in range(NP):
                link(v.tensor_tensor_scan(cs[:, j, :], keep[:, :], lw[:, j, :], 0.0, ALU.mult, ALU.add))
            link(v.tensor_copy(tail[:, :, :], cs[:, :, CH - 1:T:CH]))
            dve.sem_inc(sem("cs_ready"), 1)
            link(v.tensor_tensor(lw[:, :, :], cs[:, :, :], lw[:, :, :], ALU.subtract))
            dve.sem_inc(sem("ex_ready"), 1)
            cs4 = cs[:, :, :].rearrange("p j (c t) -> p j c t", t=CH)
            t34 = t3[:, :, :].rearrange("p j (c t) -> p j c t", t=CH)
            product(dve, "lg1")
            for j in range(NP):
                link(v.tensor_tensor(t34[:, j], tail[:, j, :].unsqueeze(2).to_broadcast([P, NCH, CH]), cs4[:, j], ALU.subtract))
            dve.sem_inc(sem("rest_ready"), 1)
            link(v.tensor_scalar(aa[:, :, :], aa[:, :, :], 0.5, 0.5, ALU.mult, ALU.add))
            for j in range(NP):
                link(v.tensor_scalar(BT[:, j, :], aa[:, j, :], 1.0, pr("k_a", j), ALU.subtract, ALU.mult))
                link(v.scalar_tensor_tensor(out=kT[:, j, :], in0=BT[:, j, :], scalar=1.0, in1=kT[:, j, :], op0=ALU.add, op1=ALU.mult))
            dve.wait_ge(sem("exp_ready"), 1)
            for j in range(NP):
                link(v.tensor_tensor(AR[:, j, :, 1, :], two(rT[:, j, :]), two(t1[:, j, :]), ALU.mult))
            dve.sem_inc(sem("t1_free"), 1)
            for m in range(2):
                o = two(product(dve, f"kb{m}"))
                kv = kk[:, 2 * m:2 * m + 2, :]
                dlink(v.tensor_tensor(kv, o, kv, ALU.mult), f"kb{m}")
            dve.wait_ge(sem("exp_ready"), 3)
            for j in range(NP):
                link(v.scalar_tensor_tensor(out=AR[:, j, :, 0, :], in0=two(kk[:, j, :]), scalar=-1.0, in1=two(lw[:, j, :]),
                                            op0=ALU.mult, op1=ALU.mult))
            link(v.tensor_tensor(aa[:, :, :], kk[:, :, :], aa[:, :, :], ALU.mult))
            dve.wait_ge(sem("exp_ready"), 5)
            link(v.tensor_tensor(BT[:, :, :], aa[:, :, :], t1[:, :, :], ALU.mult))
            link(v.tensor_tensor(KT[:, :, :], kT[:, :, :], t1[:, :, :], ALU.mult))
            link(v.tensor_tensor(Bd[:, :, :], aa[:, :, :], t3[:, :, :], ALU.mult))
            link(v.tensor_tensor(Kd[:, :, :], kT[:, :, :], t3[:, :, :], ALU.mult))
            dve.sem_inc(sem("t3_free"), 1)
            dve.sem_inc(sem("ops_ready"), 1)
            for j in range(NP):
                link(v.scalar_tensor_tensor(out=t1[:, j, :], in0=rT[:, j, :], scalar=pr("r_k", j), in1=kT[:, j, :],
                                            op0=ALU.mult, op1=ALU.mult))
            dve.sem_inc(sem("rk_ready"), 1)
            for m in range(2):
                o = two(product(dve, f"bo{m}"))
                dlink(v.tensor_tensor(bv[:, 2 * m:2 * m + 2, :], o, vT[:, 2 * m:2 * m + 2, :], ALU.mult), f"bo{m}")
            for i in range(NT):
                o = product(dve, f"nat{i}2")
                drain(v.tensor_copy(Bn[:, i, :], o), f"nat{i}2")
                o = product(dve, f"nat{i}3")
                drain(v.tensor_copy(Kn[:, i, :], o), f"nat{i}3")
            for i in range(NT):
                for hh in range(NH):
                    o = product(dve, f"LGMH{i}{hh}")
                    drain(v.tensor_tensor(LGMH[:, i, hh, :], o, masks[:, :, :].rearrange("p a b -> p (a b)"), ALU.mult), f"LGMH{i}{hh}")

            dve.wait_ge(sem("L16_in"), 16)
            dve.wait_ge(sem("X16_unit"), 1)
            for r in range(1, SUB):
                link(v.tensor_tensor(w16[:, 0:r, 0:r], X16[:, 0:r, 0:r], L16[:, r:r + 1, 0:r].to_broadcast([P, r, r]), ALU.mult))
                link(v.reduce_sum(X16[:, 0:r, r:r + 1], w16[:, 0:r, 0:r], AX.X))
            dve.sem_inc(sem("X16_ready"), 1)

            dve.wait_ge(sem("lam_exp_ready"), 1)
            link(v.tensor_tensor(lam[:, 4:5], lam[:, 3:4], lam[:, 2:3], ALU.subtract))
            link(v.tensor_scalar(lam[:, 4:5], lam[:, 4:5], -LAMBDA_INIT, None, ALU.add))
            for u, (i, heads) in enumerate(UNITS):
                w = P * (i + 1)
                nh = len(heads)
                for c in range(2):
                    o = product(dve, f"sc{u}{c}").rearrange("p (h k) -> p h k", h=nh)
                    link(v.memset(o[0:64, :, w - 64:w], -1e30))
                    col = 8 * u + 4 * c
                    link(v.reduce_max(dst_[:, col:col + nh], o, AX.X))
                    link(v.tensor_scalar(dst_[:, col:col + nh], dst_[:, col:col + nh], -DSCALE, None, ALU.mult))
                dve.sem_inc(sem("dmax_ready"), 1)
                dve.wait_ge(sem("dexp_ready"), u + 1)
                for c in range(2):
                    col = 32 + 8 * u + 4 * c
                    link(v.reciprocal(dst_[:, col:col + nh], dst_[:, col:col + nh]))
                col = 32 + 8 * u + 4
                link(v.tensor_scalar(dst_[:, col:col + nh], dst_[:, col:col + nh], lam[:, 4:5], None, ALU.mult))
                for m in range(nh):
                    a0 = soft[:, 0, m * w:(m + 1) * w]
                    a1 = soft[:, 1, m * w:(m + 1) * w]
                    link(v.tensor_scalar(a0, a0, dst_[:, 32 + 8 * u + m:33 + 8 * u + m], None, ALU.mult))
                    link(v.scalar_tensor_tensor(out=a0, in0=a1, scalar=dst_[:, 36 + 8 * u + m:37 + 8 * u + m], in1=a0,
                                                op0=ALU.mult, op1=ALU.add))
                dve.sem_inc(sem("attn_ready"), 1)
                o = product(dve, f"at{u}")
                dlink(v.tensor_copy(atT[u % 2][:, :], o), f"at{u}")
                dve.sem_inc(sem("soft_free"), 1)
                if u != 1:
                    o = product(dve, f"od{i}")
                    dlink(v.tensor_copy(odn[:, i, :], o), f"od{i}")
            for i in range(NT):
                link(v.tensor_tensor(dsq[:, :], odn[:, i, :], odn[:, i, :], ALU.mult))
                link(v.reduce_sum(st[:, 8 + 4 * i:12 + 4 * i], four(dsq[:, :]), AX.X))
            rstd(8, 16, P, EPS)
            for q in range(4):
                i, h0 = q // 2, 4 * (q % 2)
                o = four(product(dve, f"z3{q}"))
                drain(v.tensor_tensor(Zf[:, i, h0:h0 + 4, :], o, Z1[:, i, h0:h0 + 4, :], ALU.add), f"z3{q}")
            for i in range(NT):
                o = four(product(dve, f"Rh{i}"))
                drain(v.tensor_tensor(RhT[:, :, i * P:(i + 1) * P], o, AR[:, :, i, 1, :], ALU.add), f"Rh{i}")
            for i in range(NT):
                link(v.tensor_tensor(four(odn[:, i, :]), four(odn[:, i, :]), st[:, 8 + 4 * i:12 + 4 * i].unsqueeze(2).to_broadcast([P, 4, P]), ALU.mult))
            dve.sem_inc(sem("odn_ready"), 1)
            def outputs(i):
                for q in range(2):
                    o = product(dve, f"Y{i}{q}")[:, 0:NP * HD].rearrange("p (j k) -> p j k", j=NP)
                    y0 = Y0[:, i, :].rearrange("p (j q k) -> p j q k", j=NP, q=2)[:, :, q, :]
                    yn = Yn[:, i, :].rearrange("p (j q k) -> p j q k", j=NP, q=2)[:, :, q, :]
                    dlink(v.tensor_tensor(yn, o, y0, ALU.add), f"Y{i}{q}")

            link(v.memset(St[:, 0, :, :], 0.0))
            dve.sem_inc(sem("S_ready"), 1)
            taken(dve, "PP0")
            link(v.tensor_copy(St[:, 1, :, :], PhiPsi[:, 0, :, HD:P]))
            dve.sem_inc(sem("S_ready"), 1)
            for c in range(1, NCH - 1):
                taken(dve, f"PP{c}")
                link(v.tensor_tensor(sd[:, :, :], St[:, c, :, :], dec[:, :, c:c + 1].to_broadcast([P, NP, HD]), ALU.mult))
                link(v.tensor_tensor(sd[:, :, :], sd[:, :, :], PhiPsi[:, c, :, HD:P], ALU.add))
                for q in range(2):
                    rows = slice(q * HD, (q + 1) * HD)
                    o = product(dve, f"S{c}{q}")[rows, 0:NP * HD].rearrange("p (j k) -> p j k", j=NP)
                    dlink(v.tensor_tensor(St[rows, c + 1, :, :], o, sd[rows, :, :], ALU.add), f"S{c}{q}")
                dve.sem_inc(sem("S_ready"), 1)
                if c == 3:
                    outputs(0)
            outputs(1)
            for i in range(NT):
                yv = Yn[:, i, :].rearrange("p (h k) -> p h k", h=NH)
                link(v.reduce_sum(st[:, 40 + 8 * i:48 + 8 * i], yv, AX.X))
                link(v.tensor_scalar(st[:, 40 + 8 * i:48 + 8 * i], st[:, 40 + 8 * i:48 + 8 * i], 1.0 / HD, None, ALU.mult))
                link(v.tensor_tensor(yv, yv, st[:, 40 + 8 * i:48 + 8 * i].unsqueeze(2).to_broadcast([P, NH, HD]), ALU.subtract))
                link(v.tensor_tensor(dsq[:, :], Yn[:, i, :], Yn[:, i, :], ALU.mult))
                link(v.reduce_sum(st[:, 16 + 8 * i:24 + 8 * i], dsq[:, :].rearrange("p (h k) -> p h k", h=NH), AX.X))
            rstd(16, 32, HD, GN_EPS)
            for i in range(NT):
                yv = Yn[:, i, :].rearrange("p (h k) -> p h k", h=NH)
                link(v.tensor_tensor(yv, yv, st[:, 16 + 8 * i:24 + 8 * i].unsqueeze(2).to_broadcast([P, NH, HD]), ALU.mult))
            dve.sem_inc(sem("yn_ready"), 1)
            for i in range(NT):
                tok = slice(i * P, (i + 1) * P)
                o = four(product(dve, f"ynT{i}"))
                for j in range(NP):
                    ins = v.tensor_scalar(xT[:, j, tok], o[:, j, :], pr("lnx_g", j), pr("lnx_b", j), ALU.mult, ALU.add)
                    if j < NP - 1:
                        link(ins)
                dlink(ins, f"ynT{i}")
            link(v.tensor_tensor(xT[:, 0:NP, :], xT[:, 0:NP, :], bv[:, :, :], ALU.add))
            link(v.tensor_tensor(xT[:, 0:NP, :], xT[:, 0:NP, :], gT[:, :, :], ALU.mult))
            dve.sem_inc(sem("yT_ready"), 1)
            for m in range(4):
                o = two(product(dve, f"c{OUT0 + m}"))
                hv = h[:, :, m * WCOL:(m + 1) * WCOL]
                dlink(v.tensor_tensor(hv, o, hv, ALU.add), f"c{OUT0 + m}")
            dve.sem_inc(sem("h_ready"), 1)
            scale_rows(h, 4, 3)
            take_rows("h1", xT, "norm2_g")
            for m in range(XH // 2):
                for i in range(NT):
                    o = two(product(dve, f"xs{m}{i}"))
                    col = 4 * m + 2 * i
                    link(v.reduce_max(xst[:, col:col + 2], o, AX.X))
                    link(v.tensor_scalar(xst[:, col:col + 2], xst[:, col:col + 2], -XSCALE, None, ALU.mult))
                    dve.sem_inc(sem("xmax_ready"), 1)
                for i in range(NT):
                    taken(dve, f"xs{m}{i}")
                    col = 8 + 4 * m + 2 * i
                    link(v.reciprocal(xst[:, col:col + 2], xst[:, col:col + 2]))
                    link(v.tensor_tensor(px[:, i, :, :], px[:, i, :, :], xst[:, col:col + 2].unsqueeze(2).to_broadcast([P, 2, T]), ALU.mult))
                    dve.sem_inc(sem("xp_ready"), 1)
                for i in range(NT):
                    nm = f"xp{m}{i}"
                    o = product(dve, nm).rearrange("p (q b t) -> p b q t", q=2, b=2)
                    if m:
                        for q in range(2):
                            product(dve, f"xo{m - 1}{q}")
                    for kb in range(2):
                        ins = v.tensor_copy(pxT[:, kb, :, i * P:(i + 1) * P], o[:, kb])
                        if kb == 0:
                            link(ins)
                    dlink(ins, nm)
            for m in range(4):
                o = two(product(dve, f"c{WO0 + m}"))
                hv = h[:, :, m * WCOL:(m + 1) * WCOL]
                dlink(v.tensor_tensor(hv, o, hv, ALU.add), f"c{WO0 + m}")
            dve.sem_inc(sem("h_ready"), 1)
            scale_rows(h, 6, 4)
            take_rows("h2", x3T, "norm3_g")
            dve.wait_ge(sem("n3g_in"), 16)
            for i in range(NT):
                link(v.scalar_tensor_tensor(out=x3[:, i, :], in0=h[:, i, :], scalar=st[:, 6 + i:7 + i], in1=n3g[:, :],
                                            op0=ALU.mult, op1=ALU.mult))
            dve.sem_inc(sem("x3_ready"), 1)
            o = product(dve, "logit")
            dlink(v.tensor_copy(lg[:, :, :], o[:, 0:NT * E].rearrange("p (i e) -> p i e", i=NT)), "logit")
            for i in range(NT):
                r0 = 16 * i
                link(v.max(rt[:, r0:r0 + 8], lg[:, i, :]))
                link(v.tensor_scalar(rt[:, r0 + 12:r0 + 13], rt[:, r0:r0 + 1], -1.0, None, ALU.mult))
                dve.sem_inc(sem("top_ready"), 1)
                link(v.max_index(ix8[:, i, :], rt[:, r0:r0 + 8], lg[:, i, :]))
                link(v.tensor_copy(rt[:, 32 + 8 * i:40 + 8 * i], ix8[:, i, :]))
                link(v.tensor_scalar(mask[:, i, :], iotaE[:, :], rt[:, 32 + 8 * i:33 + 8 * i], None, ALU.is_equal))
                for k in range(1, TOPK):
                    link(v.scalar_tensor_tensor(out=mask[:, i, :], in0=iotaE[:, :], scalar=rt[:, 32 + 8 * i + k:33 + 8 * i + k],
                                                in1=mask[:, i, :], op0=ALU.is_equal, op1=ALU.add))
            dve.sem_inc(sem("mask_ready"), 1)
            for i in range(NT):
                r0 = 16 * i
                dve.wait_ge(sem("gexp_ready"), i + 1)
                link(v.reciprocal(rt[:, r0 + 14:r0 + 15], rt[:, r0 + 13:r0 + 14]))
                link(v.tensor_scalar(rt[:, r0 + 8:r0 + 12], rt[:, r0 + 8:r0 + 12], rt[:, r0 + 14:r0 + 15], None, ALU.mult))
                link(v.memset(gate[:, i, :], 0.0))
                for k in range(TOPK):
                    link(v.tensor_scalar(rt[:, 64:64 + E], iotaE[:, :], rt[:, 32 + 8 * i + k:33 + 8 * i + k], rt[:, r0 + 8 + k:r0 + 9 + k],
                                         ALU.is_equal, ALU.mult))
                    link(v.tensor_tensor(gate[:, i, :], gate[:, i, :], rt[:, 64:64 + E], ALU.add))
            dve.sem_inc(sem("gates_ready"), 1)
            o = product(dve, "pos")
            link(v.scalar_tensor_tensor(out=post[:, :, 0, :], in0=o[:, 0:NT * E].rearrange("p (i e) -> p i e", i=NT), scalar=1.0,
                                        in1=mask[:, :, :], op0=ALU.add, op1=ALU.mult))
            for k in range(PASSES, -1, -1):
                link(v.tensor_scalar(post[:, :, k, :], post[:, :, 0, :], -1.0 - BLK * k, None, ALU.add))
            link(v.reduce_max(rt[0:1, 128:129], o[0:1, 2 * E:3 * E], AX.X))
            link(v.tensor_scalar(rt[0:1, 129:130], rt[0:1, 128:129], float(BLK), 1.0, ALU.is_gt, ALU.add))
            for k in range(2, PASSES):
                link(v.tensor_scalar(rt[0:1, 130:131], rt[0:1, 128:129], float(k * BLK), None, ALU.is_gt))
                link(v.tensor_tensor(rt[0:1, 129:130], rt[0:1, 129:130], rt[0:1, 130:131], ALU.add))
            dlink(v.tensor_copy(npass[0:1, 0:1], rt[0:1, 129:130]), "pos")
            dve.sem_inc(sem("npass_ready"), 1)
            o = product(dve, "gateT")
            dlink(v.tensor_copy(gateT[0:E, :], o[0:E, 0:T]), "gateT")

            postv = [post[:, i, :, :].rearrange("p k e -> p (k e)") for i in range(NT)]

            for i in range(NT):
                v.tensor_scalar(sel[:, i, :], iota[:, 0:BLK], postv[i][:, 0:1], None, ALU.is_equal).then_inc(sem("sel_ready"), 1)
            link(v.memset(yy[:, :], 0.0))
            dve.sem_inc(sem("yy_ready"), 1)
            link(v.memset(GT[:, :], 0.0))
            dve.sem_inc(sem("GT_ready"), 1)
            dve.sem_inc(sem("lin_read"), 1)
            v.tensor_copy(onehot[0:E, :], identE[:, 0:1].to_broadcast([E, BLK])).then_inc(sem("onehot_ready"), 1)
            dve.wait_ge(sem("xeT_filled"), 1)
            v.tensor_copy(xeT[:, :], ps[:, 6, :]).then_inc(sem("xeT_ready"), 1)
            np_ = dve.value_load(npass[0:1, 0:1], min_val=1, max_val=PASSES)
            with dve.Fori(0, np_) as q_:
                with dve.Fori(0, E) as e:
                    it = dve.snap(q_ * E + e)
                    dve.wait_ge(sem("GT_ready"), it + 1)
                    for i in range(NT):
                        v.tensor_scalar(selg[:, i, :], iota[:, :], postv[i][:, bass.ds(it, 1)], gate[:, i, bass.ds(e, 1)],
                                        ALU.is_equal, ALU.mult).then_inc(sem("selg_ready"), 1)
                    dve.wait_ge(sem("xe_filled"), it + 1)
                    for i in range(NT):
                        v.tensor_scalar(sel[:, i, :], iota[:, 0:BLK], postv[i][:, bass.ds(it + 1, 1)], None, ALU.is_equal)\
                            .then_inc(sem("sel_ready"), 1)
                    dve.wait_ge(sem("hid_filled"), it + 1)
                    v.tensor_scalar(gg[:, :], ps[:, 4, :], 7.0, None, ALU.min).then_inc(sem("gate_ready"), 1)
                    v.tensor_scalar(ll[:, :], ps[:, 5, :], 7.0, -7.0, ALU.min, ALU.max).then_inc(sem("lin_read"), 1)
                    v.tensor_copy(onehot[0:E, :], identE[:, bass.ds(e + 1, 1)].to_broadcast([E, BLK])).then_inc(sem("onehot_ready"), 1)
                    dve.wait_ge(sem("lin_read"), it + 2)
                    dve.wait_ge(sem("gate_ready"), it + 1)
                    v.scalar_tensor_tensor(out=ll[:, :], in0=ll[:, :], scalar=1.0, in1=gg[:, :], op0=ALU.add, op1=ALU.mult)\
                        .then_inc(sem("swi_step"), 1)
                    dve.wait_ge(sem("swi_step"), it + 1)
                    dve.wait_ge(sem("sig_ready"), it + 1)
                    v.tensor_tensor(ac[:, :], ll[:, :], sg[:, :], ALU.mult).then_inc(sem("ac_ready"), 1)
                    dve.wait_ge(sem("xeT_filled"), it + 2)
                    v.tensor_copy(xeT[:, :], ps[:, 6, :]).then_inc(sem("xeT_ready"), 1)
                    dve.wait_ge(sem("yy_filled"), it + 1)
                    v.tensor_copy(yy[:, :], ps[:, 7, :]).then_inc(sem("yy_ready"), 1)
            dve.wait_ge(sem("sum_ready"), 1)
            for i in range(NT):
                for c in range(2):
                    hv = h[:, i, c * 512:(c + 1) * 512]
                    link(v.tensor_tensor(hv, ps[:, 2 * i + c, :], hv, ALU.add))
            dve.sem_inc(sem("h_ready"), 1)
            dve.wait_ge(sem("stat_ready"), 5)
            rstd(32, 34, D, EPS)
            dve.wait_ge(sem("fing_in"), 16)
            for i in range(NT):
                v.scalar_tensor_tensor(out=x3[:, i, :], in0=h[:, i, :], scalar=st[:, 32 + i:33 + i], in1=fing[:, :],
                                       op0=ALU.mult, op1=ALU.mult).then_inc(sem("y_ready"), 1)


_INS = ["x", "mem", "norm1_g", "w_in", "mu_shift", "w0", "w2", "a0", "a2", "g2", "k_k", "k_a", "r_k", "lnx_g", "lnx_b",
        "lam_q1", "lam_k1", "lam_q2", "lam_k2", "subln_g", "w_out", "norm2_g", "mem_norm_g", "wq_x", "wkv_x", "wo_x",
        "norm3_g", "router_w", "router_b", "moe_w1", "moe_b1", "moe_w2", "moe_b2", "final_g"]


def kernel(**inputs):
    import numpy as _np
    import concourse.bacc as _bacc
    from concourse import mybir as _mybir
    from concourse.bass_utils import run_bass_kernel_spmd as _run

    nc = _bacc.Bacc("TRN2", target_bir_lowering=False, num_devices=1)
    arrays, aps = {}, {}
    for name in _INS:
        v = _np.ascontiguousarray(inputs[name])
        arrays[f"in_{name}"] = v
        aps[name] = nc.dram_tensor(f"in_{name}", v.shape, _mybir.dt.from_np(v.dtype), kind="ExternalInput").ap()
    out = nc.dram_tensor("out_0", (1, T, D), F32, kind="ExternalOutput").ap()
    program(nc, aps, out)
    r = _run(nc, [arrays], core_ids=[0])
    return r.results[0]["out_0"]
```

```python
import itertools
from contextlib import ExitStack

import concourse.bass as bass
from concourse import mybir

F32 = mybir.dt.float32
I32 = mybir.dt.int32
U32 = mybir.dt.uint32
ALU = mybir.AluOpType
ACT = mybir.ActivationFunctionType
AX = mybir.AxisListType

P = 128
T = 256
NT = T // P
D = 1024
KC = D // P
RW = 512
NH = 8
NP = NH // 2
HD = 64
SHIFT = 3 * RW + 64 + 64 + 128
DH = 4
XH = 4
E = 32
CH = 32
NCH = T // CH
SUB = 16
F = 1024
TOPK = 4
EPS = 1e-5
GN_EPS = 64e-5
LAMBDA_INIT = 0.8 - 0.6
XSCALE = (D // XH) ** -0.5
DSCALE = 64 ** -0.5
NEG_EXP_HALF = -0.6065306597126334
SLOT = 2048
RING = 12
PRE = 3
WCOL = 256
BLK = 64
PASSES = T // BLK

ROWS = [("norm1_g", KC), ("mu_shift", SHIFT // P), ("w0", 4), ("a0", 4), ("k_k", 4), ("k_a", 4), ("r_k", 4),
        ("lnx_g", 4), ("lnx_b", 4), ("norm2_g", KC), ("mem_norm_g", KC), ("norm3_g", KC), ("subln_g", 1)]
ROW = {}
NROWS = 0
for _name, _n in ROWS:
    ROW[_name] = NROWS
    NROWS += _n

PRE_CHUNKS = {}
for _w, _m, _ns in (("in", "w_in", (2, 3, 6, 0, 1, 4, 5, 7, 8, 9, 10, 11, 12)), ("kv", "wkv_x", (0, 1, 2, 3, 4, 5)),
                    ("out", "w_out", range(4)), ("kv", "wkv_x", (6,)), ("wq", "wq_x", range(4)), ("kv", "wkv_x", (7,)),
                    ("wo", "wo_x", range(4))):
    for _n in _ns:
        PRE_CHUNKS[f"{_w}{_n}"] = (_m, _n * WCOL)
ORDER = list(PRE_CHUNKS)


def program(nc, a, out):
    with ExitStack() as ctx:
        def sb(name, shape, dt=F32):
            return ctx.enter_context(nc.sbuf_tensor(name, shape, dt))

        sems = {}

        def sem(name):
            if name not in sems:
                sems[name] = ctx.enter_context(nc.semaphore(name))
            return sems[name]

        ring = sb("ring", [P, RING, SLOT])
        NF = 25088
        arena = sb("arena", [P, NF])
        ps = ctx.enter_context(nc.psum_tensor("ps", [P, 8, 512], F32))

        def cut(at, *shape):
            n = 1
            for s in shape:
                n *= s
            assert at + n <= NF
            v = arena[:, at:at + n]
            if len(shape) == 2:
                v = v.rearrange("p (a b) -> p a b", a=shape[0])
            if len(shape) == 3:
                v = v.rearrange("p (a b c) -> p a b c", a=shape[0], b=shape[1])
            if len(shape) == 4:
                v = v.rearrange("p (a b c d) -> p a b c d", a=shape[0], b=shape[1], c=shape[2])
            return v

        def side(slot, *shape):
            v = ring[:, slot:RING, :].rearrange("p a b -> p (a b)")
            n = 1
            for s in shape:
                n *= s
            v = v[:, 0:n]
            if len(shape) == 2:
                v = v.rearrange("p (a b) -> p a b", a=shape[0])
            if len(shape) == 3:
                v = v.rearrange("p (a b c) -> p a b c", a=shape[0], b=shape[1])
            if len(shape) == 4:
                v = v.rearrange("p (a b c d) -> p a b c d", a=shape[0], b=shape[1], c=shape[2])
            return v

        H0, XT0, E0, P0, AR0, BT0, KT0, BK0, GT0, QD0 = 0, 2048, 4096, 11264, 14848, 16896, 17920, 18944, 20992, 22016
        h = cut(H0, NT, D)
        xT = cut(XT0, KC, T)
        lw, cs, aa, kk, t1, t2 = (cut(E0 + 1024 * n, NP, T) for n in range(6))
        t3 = cut(QD0 + 2048, NP, T)
        pT = cut(P0, SHIFT // P, T)
        rT, kT, vT = (pT[:, 4 * n:4 * n + 4, :] for n in range(3))
        AR = cut(AR0, NP, NT, 2, P)
        BT, KT = cut(BT0, NP, T), cut(KT0, NP, T)
        Bd, Kd = cut(BK0, NP, T), cut(BK0 + 1024, NP, T)
        xs = cut(BK0, NT, D)
        gT = cut(GT0, NP, T)
        qd, kd = cut(QD0, DH, T), cut(QD0 + 1024, DH, T)
        vd = cut(QD0 + 2048, NT, RW)
        Zr = cut(E0, NT, NH, 2 * HD)
        Vn, Bn, Kn = (cut(E0 + 2048 + 1024 * n, NT, RW) for n in range(3))
        Zf = cut(E0 + 5120, NT, NH, 2 * HD)
        LGMH = side(4, NT, NH, 4 * P)
        XTb = side(8, NT, NH, P)
        Z1 = side(9, NT, NH, P)
        Lsb = side(9, NT, NH, P)
        Z2 = cut(BK0, NT, NH, P)
        PhiPsi = side(8, NCH, NP, 2 * HD)
        kmT = side(10, KC, T)
        memT = side(3, KC, T)
        memN = side(4, NT, D)
        vm = side(11, NT, D)
        soft = cut(XT0 + 1024, 2, 512)
        St = cut(BK0, NCH, NP, HD)
        RhT = cut(BT0, NP, T)
        Y0 = cut(KT0, NT, RW)
        Yn = cut(P0 + 1024, NT, RW)
        prow = cut(GT0, P)[0:NROWS, :]
        lamv = cut(GT0 + 256, 4, HD)
        lora = cut(QD0 + 2048, RW)
        g2s = cut(QD0 + 2560, RW)
        atT = [cut(P0 + 2048 + 512 * n, 512) for n in range(2)]
        L16, X16, w16 = (cut(E0 + 5120 + 256 * n, SUB, SUB) for n in range(3))
        rk = cut(E0 + 6144, NP, T)
        krs, kra, krb = (cut(KT0 + 256 * n, T) for n in range(3))
        odn = cut(XT0, NT, RW)
        dsq = cut(P0 + 3072, 512)
        osq = side(11, P)
        squares = cut(P0, D)
        sd = cut(P0 + 3072, NP, HD)
        bv = rT
        qx = cut(E0, KC, T)
        oT = cut(E0 + 2048, KC, T)
        px = [cut(P0 + 1024 * n, 2, 2, T) for n in range(XH // 2)]
        pxT = [cut(AR0 + 1024 * n, NT, 2, T) for n in range(XH // 2)]
        x3 = cut(XT0, NT, D)
        x3T = cut(E0, KC, T)
        n3g = cut(E0 + 2048, D)
        fing = cut(E0 + 3072, D)
        b1a = cut(E0 + 4096, 2 * F)
        b2a = cut(E0 + 6144, D)
        M0 = P0
        xe, xeT, gg, sg, ll, ac, acT, yy = (cut(M0 + 512 * n, 512) for n in range(8))
        sel = cut(M0 + 4096, NT, BLK)
        selg = cut(M0 + 4224, NT, P)
        GT = cut(M0 + 4480, T)
        onehot = cut(M0 + 4736, BLK)
        post = cut(M0 + 4800, NT, PASSES + 1, E)
        gate = cut(M0 + 5120, NT, E)
        mask = cut(M0 + 5184, NT, E)
        gateT = cut(M0 + 5248, T)
        lg = cut(M0 + 5504, NT, E)
        rt = cut(M0 + 5568, 256)

        ident = sb("ident", [P, P])
        masks = sb("masks", [P, 4, P])
        onesbd = sb("onesbd", [P, P])
        keep = sb("keep", [P, T])
        iota = sb("iota", [P, P])
        iotaE = sb("iotaE", [P, E])
        tri = sb("tri", [P, P])
        ones = sb("ones", [P, P])
        hsel = sb("hsel", [P, NP, NH])
        hselT = sb("hselT", [NH, NP, P])
        identE = sb("identE", [E, E + 1])
        prm = sb("prm", [P, NROWS])
        rws = sb("rws", [P, KC, E])
        rbs = sb("rbs", [1, E])
        mu1 = sb("mu1", [P, SHIFT // P])
        w0h = sb("w0h", [P, 8])
        tail = sb("tail", [P, NP, NCH])
        dec = sb("dec", [P, NP, NCH])
        st = sb("st", [P, 64])
        lam = sb("lam", [P, 8])
        dst_ = sb("dst_", [P, 64])
        xst = sb("xst", [P, 32])
        wk = sb("wk", [P, 64])
        ix8 = sb("ix8", [P, NT, 8], U32)
        npass = sb("npass", [1, 1], I32)

        blocks = nc.dram_tensor("blocks", (2, P // SUB, NT * NH, SUB, SUB), F32, kind="Internal").ap()

        filled = [sem(f"bank{b}_filled") for b in range(8)]
        drained = [sem(f"bank{b}_drained") for b in range(8)]
        where, count = {}, [0] * 8

        def place(name, bank):
            assert name not in where
            count[bank] += 1
            where[name] = (bank, count[bank])

        def chunk(label, bank=None):
            place(label, ORDER.index(label) % 2 if bank is None else bank)

        for n in range(4):
            place(f"xT{n}", 2 + n)
        place("prm", 6)
        chunk("in2")
        chunk("in3")
        for n in range(4):
            place(f"memT{n}", 2 + n)
        chunk("in6")
        chunk("in0")
        place("ksum", 6)
        chunk("in1")
        for n in range(2):
            place(f"lw{n}", 2 + n)
            place(f"la{n}", 4 + n)
            place(f"lg{n}", 6 + n)
        chunk("in4")
        for n in range(2):
            place(f"kb{n}", 2 + n)
        for n in (5, 7, 8, 9, 10):
            chunk(f"in{n}")
        for i in range(NT):
            place(f"L{i}0", 6)
            place(f"L{i}1", 7)
        for i in range(NT):
            for q in range(4):
                place(f"nat{i}{q}", 2 + q)
        for n in range(NH):
            place(f"LGMH0{n}", 2 + n % 4)
        chunk("in11")
        chunk("in12")
        for n in range(NH):
            place(f"LGMH1{n}", 2 + n % 4)
        for n in range(2):
            place(f"bo{n}", 4 + n)
        for i in range(NT):
            place(f"MV{i}", 6 + i)
        UNITS = [(0, (0, 1, 2, 3)), (1, (0, 1)), (1, (2, 3))]
        for g in range(4):
            place(f"z1{g}", 2 + g)
        place("sc00", 0)
        place("sc01", 1)
        for nm in ("z2", "z3"):
            for g in range(4):
                place(f"{nm}{g}", 2 + g)
        for i in range(NT):
            place(f"Rh{i}", 6)
            place(f"yz{i}", 7)
        place("at0", 2)
        place("od0", 3)
        place("sc10", 0)
        place("sc11", 1)
        for c in range(NCH - 1):
            place(f"PP{c}", (4, 5, 6, 7)[c % 4])
        place("at1", 2)
        place("od1", 3)
        place("sc20", 0)
        place("sc21", 1)
        chunk("kv0", 2)
        place("at2", 3)
        place("od2", 2)
        for i in range(NT):
            place(f"Y{i}0", 0)
            place(f"Y{i}1", 1)
            for c in range(4 * i, min(4 * i + 4, NCH - 1)):
                if c:
                    place(f"S{c}0", 6)
                    place(f"S{c}1", 7)
        chunk("kv1", 4)
        chunk("kv2", 5)
        for i in range(NT):
            place(f"odT{i}", 2 + i)
        chunk("kv3")
        chunk("kv4")
        chunk("kv5")
        for i in range(NT):
            place(f"ynT{i}", 2 + i)
        for n in range(4):
            chunk(f"out{n}")
        chunk("kv6")
        for n in range(4):
            place(f"h1T{n}", 2 + n)
        for n in range(4):
            chunk(f"wq{n}")
        for n in range(XH // 2):
            for i in range(NT):
                place(f"xs{n}{i}", 2 + 2 * n + i)
        chunk("kv7")
        for n in range(XH // 2):
            for i in range(NT):
                place(f"xp{n}{i}", (6, 4)[n] + i)
            for m in range(2):
                place(f"xo{n}{m}", (2, 6)[n] + m)
        for n in range(4):
            chunk(f"wo{n}")
        for n in range(4):
            place(f"h2T{n}", 2 + n)
        place("logit", 6)
        place("pos", 7)
        place("gateT", 6)

        def begin(pe, name):
            b, k = where[name]
            if k > 1:
                pe.wait_ge(drained[b], k - 1)
            return ps[:, b, :]

        def done(ins, name):
            ins.then_inc(filled[where[name][0]], 1)

        def product(eng, name):
            b, k = where[name]
            eng.wait_ge(filled[b], k)
            return ps[:, b, :]

        def drain(ins, name):
            ins.then_inc(drained[where[name][0]], 1)

        def taken(eng, name):
            b, k = where[name]
            eng.wait_ge(drained[b], k)

        landed = [sem(f"slot{s}_landed") for s in range(PRE)]
        elanded = [sem(f"expert_chunk{c}_landed") for c in range(RING)]
        eused = sem("expert_chunks_used")

        mats = {n: a[n][0] for n in ("wkv_x", "w_in", "w_out", "wq_x", "wo_x")}

        def gbc(name, n0, n):
            r = ROW[name] + n0
            return prm[:, r:r + n].unsqueeze(2).to_broadcast([P, n, P])

        def rows_dma(eng, rows):
            for name, n in rows:
                src = a[name]
                src = src[0].rearrange("h n -> (h n)") if name == "r_k" else src[0]
                eng.dma_start(prow[ROW[name]:ROW[name] + n, :], src.rearrange("(r p) -> r p", p=P)).then_inc(sem("rows_in"), 16)

        block = ctx.enter_context(nc.Block())

        @block.sync
        def _(sp):
            for i in range(NT):
                sp.dma_start(h[:, i, :], a["x"][0, i * P:(i + 1) * P, :]).then_inc(sem("x_in"), 16)
            rows_dma(sp, ROWS[7:])

            def expert_chunk(e, c):
                if c < 8:
                    src = w1v[c, e]
                    dst = ring[:, c, :]
                else:
                    src = w2v[c - 8, e]
                    dst = ring[:, c, :].rearrange("p (j n) -> p j n", j=2)
                sp.dma_start(dst, src).then_inc(elanded[c], 16)

            w1v = a["moe_w1"][0].rearrange("e (c p) n -> c e p n", p=P)
            w2v = a["moe_w2"][0].rearrange("e (c j p) n -> c e p j n", p=P, j=2)
            early = list(range(PRE + 1, 10))
            for n, (w, c0) in enumerate(PRE_CHUNKS.values()):
                if n >= PRE:
                    product(sp, ORDER[n - PRE])
                sp.dma_start(ring[:, n % PRE, :].rearrange("p (k n) -> p k n", k=KC),
                             mats[w][:, c0:c0 + WCOL].rearrange("(k p) n -> p k n", p=P)).then_inc(landed[n % PRE], 16)
                if n == 1:
                    sp.dma_start(memN[:, :, :], a["mem"][0].rearrange("(i p) d -> p i d", p=P)).then_inc(sem("mem_in"), 16)
                if n == 2:
                    sp.dma_start(lora[0:64, :], a["w2"][0]).then_inc(sem("lora_in"), 16)
                    sp.dma_start(lora[64:128, :], a["a2"][0]).then_inc(sem("lora_in"), 16)
                    sp.dma_start(g2s[:, :], a["g2"][0]).then_inc(sem("lora_in"), 16)
                    sp.dma_start(rws[:, :, :], a["router_w"][0].rearrange("(k p) e -> p k e", p=P)).then_inc(sem("router_in"), 16)
                    sp.dma_start(rbs[:, :], a["router_b"]).then_inc(sem("router_in"), 16)
                    for m, name in enumerate(("lam_q1", "lam_k1", "lam_q2", "lam_k2")):
                        sp.dma_start(lamv[:, m, :], a[name].to_broadcast([P, HD])).then_inc(sem("lam_in"), 16)
                if n >= ORDER.index("out0") + PRE and early:
                    if early[0] == PRE + 1:
                        sp.wait_ge(sem("mixers_through"), 1)
                    for _ in range(2):
                        expert_chunk(0, early.pop(0))
            assert not early
            product(sp, "kv7")
            expert_chunk(0, PRE)
            sp.wait_ge(sem("cross_through"), 1)
            for c in range(10, RING):
                expert_chunk(0, c)
            for c in range(PRE):
                product(sp, ORDER[len(ORDER) - PRE + c])
                expert_chunk(0, (len(ORDER) - PRE + c) % PRE)
            with sp.Fori(1, E) as e:
                for c in range(RING):
                    sp.wait_ge(eused, e * RING + (c - RING + 1))
                    expert_chunk(e, c)
            sp.wait_ge(sem("npass_ready"), 1)
            np_ = sp.value_load(npass[0:1, 0:1], min_val=1, max_val=PASSES)
            with sp.If(np_ > 1):
                with sp.Fori(1, np_) as q:
                    with sp.Fori(0, E) as e:
                        for c in range(RING):
                            sp.wait_ge(eused, q * (E * RING) + e * RING + (c - RING + 1))
                            expert_chunk(e, c)
            sp.wait_ge(sem("y_ready"), 2)
            sp.dma_start(out[0].rearrange("(i p) d -> p i d", p=P), x3[:, :, :]).then_inc(sem("out_written"), 16)
            sp.wait_ge(sem("out_written"), 16)

        @block.gpsimd
        def _(pool):
            g = nc.gpsimd
            n = [0]

            def link(ins):
                n[0] += 1
                ins.then_inc(sem("pool_step"), 1)
                pool.wait_ge(sem("pool_step"), n[0])

            link(g.memset(ident[:, :], 0.0))
            link(g.affine_select(out=ident[:, :], in_=ident[:, :], compare_op=ALU.not_equal, fill=1.0, base=0,
                                 pattern=[[-1, P]], channel_multiplier=1))
            pool.sem_inc(sem("ident_ready"), 1)
            g.memset(ones[:, :], 1.0).then_inc(sem("ones_ready"), 1)
            link(g.memset(onesbd[:, :], 1.0))
            link(g.affine_select(out=onesbd[:, 0:HD], in_=onesbd[:, 0:HD], compare_op=ALU.is_ge, fill=0.0, base=HD - 1,
                                 pattern=[[0, HD]], channel_multiplier=-1))
            link(g.affine_select(out=onesbd[:, HD:P], in_=onesbd[:, HD:P], compare_op=ALU.is_ge, fill=0.0, base=-HD,
                                 pattern=[[0, HD]], channel_multiplier=1))
            link(g.memset(keep[:, :], 1.0))
            link(g.memset(keep[:, 0:T:CH], 0.0))
            link(g.memset(masks[:, :, :], 1.0))
            for m in range(4):
                v = masks[:, m, :].rearrange("p (c t) -> p c t", t=CH)
                link(g.affine_select(out=v, in_=v, compare_op=ALU.is_ge, fill=0.0, base=0,
                                     pattern=[[-CH, P // CH], [0, CH]], channel_multiplier=1))
                link(g.affine_select(out=v, in_=v, compare_op=ALU.is_ge, fill=0.0, base=CH - 1 if m else SUB - 1,
                                     pattern=[[CH, P // CH], [0, CH]], channel_multiplier=-1))
                if m:
                    w = masks[:, m, :]
                    link(g.affine_select(out=w, in_=w, compare_op=ALU.is_ge, fill=0.0, base=-1 if m == 2 else 0,
                                         pattern=[[1, P]], channel_multiplier=-1))
                else:
                    link(g.affine_select(out=v, in_=v, compare_op=ALU.is_ge, fill=0.0, base=-SUB,
                                         pattern=[[0, P // CH], [1, CH]], channel_multiplier=0))
            link(g.memset(tri[:, :], 1.0))
            link(g.affine_select(out=tri[:, :], in_=tri[:, :], compare_op=ALU.is_ge, fill=0.0, base=-1,
                                 pattern=[[1, P]], channel_multiplier=-1))
            link(g.iota(iota[:, :].rearrange("p (a b) -> p a b", a=2), [[0, 2], [1, BLK]], base=0, channel_multiplier=0,
                        allow_small_or_imprecise_dtypes=True))
            link(g.iota(iotaE[:, :], [[1, E]], base=0, channel_multiplier=0, allow_small_or_imprecise_dtypes=True))
            link(g.memset(hsel[:, :, :], 0.0))
            for j in range(NP):
                link(g.memset(hsel[0:HD, j, 2 * j:2 * j + 1], 1.0))
                link(g.memset(hsel[HD:P, j, 2 * j + 1:2 * j + 2], 1.0))
            link(g.memset(hselT[:, :, :], 0.0))
            hv = hselT[:, :, :].rearrange("p j (q c) -> p j q c", q=2)
            link(g.affine_select(out=hv, in_=hv, compare_op=ALU.not_equal, fill=1.0, base=0,
                                 pattern=[[-2, NP], [-1, 2], [0, HD]], channel_multiplier=1))
            link(g.memset(identE[:, :], 0.0))
            link(g.affine_select(out=identE[:, 0:E], in_=identE[:, 0:E], compare_op=ALU.not_equal, fill=1.0, base=0,
                                 pattern=[[-1, E]], channel_multiplier=1))
            link(g.affine_select(out=identE[:, E:E + 1], in_=identE[:, E:E + 1], compare_op=ALU.not_equal, fill=1.0, base=0,
                                 pattern=[[0, 1]], channel_multiplier=1))
            link(g.memset(XTb[:, :, :, :], 0.0))
            pool.sem_inc(sem("const_ready"), 1)

            product(pool, "ksum")
            link(g.memset(X16[:, :, :], 0.0))
            g.affine_select(out=X16[:, :, :], in_=X16[:, :, :], compare_op=ALU.not_equal, fill=1.0, base=0,
                            pattern=[[1, SUB], [-1, SUB]], channel_multiplier=0).then_inc(sem("X16_unit"), 1)

        @block.scalar
        def _(act):
            s = nc.scalar
            n = [0]

            def link(ins):
                n[0] += 1
                ins.then_inc(sem("act_step"), 1)
                act.wait_ge(sem("act_step"), n[0])

            rows_dma(act, ROWS[0:7])

            def sumsq(src, col):
                for i in range(NT):
                    link(s.activation(squares[:, :], src[:, i, :], ACT.Square, accum_out=st[:, col + i:col + i + 1]))
                act.sem_inc(sem("stat_ready"), 1)

            act.wait_ge(sem("x_in"), 16 * NT)
            sumsq(h, 2)
            act.wait_ge(sem("mem_in"), 16)
            sumsq(memN, 0)

            def copy(dst, name, view=None):
                src = product(act, name)
                drain(s.activation(dst, view(src) if view else src, ACT.Copy), name)

            two = lambda v: v.rearrange("p (a b) -> p a b", a=2)

            def unshifted(m):
                src = two(product(act, f"in{m}"))
                for q in range(2):
                    j = 2 * m + q
                    s.activation(pT[:, j, :], src[:, q, :], ACT.Identity, scale=mu1[:, j:j + 1]).then_inc(sem("unshifted_ready"), 1)

            act.wait_ge(sem("mu_ready"), 1)
            for m in (2, 3, 6):
                unshifted(m)
            act.wait_ge(sem("shifted_ready"), 3)
            s.activation(pT[0:64, 12, :], pT[0:64, 12, :], ACT.Tanh).then_inc(sem("lora_x_ready"), 1)
            s.activation(pT[:, 13, :], pT[:, 13, :], ACT.Tanh, scale=0.5).then_inc(sem("gd_tanh_ready"), 1)
            unshifted(0)
            unshifted(1)
            for m in range(2):
                for (z, dst, b0) in (("lw", lw, 0), ("la", aa, 4)):
                    src = two(product(act, f"{z}{m}"))
                    for q in range(2):
                        j = 2 * m + q
                        ins = s.activation(dst[:, j, :], src[:, q, :], ACT.Tanh, bias=w0h[:, b0 + j:b0 + j + 1], scale=0.5)
                        if q == 0:
                            link(ins)
                    drain(ins, f"{z}{m}")
                act.wait_ge(sem("lam_sum_ready"), 1)
                copy(gT[:, 2 * m:2 * m + 2, :], f"lg{m}", two)
            unshifted(4)
            act.wait_ge(sem("cs_ready"), 1)
            s.activation(t1[:, :, :], cs[:, :, :], ACT.Exp).then_inc(sem("exp_ready"), 1)
            s.activation(dec[:, :, :], tail[:, :, :], ACT.Exp).then_inc(sem("exp_ready"), 1)
            act.wait_ge(sem("ex_ready"), 1)
            s.activation(lw[:, :, :], lw[:, :, :], ACT.Exp).then_inc(sem("exp_ready"), 1)
            unshifted(5)
            act.wait_ge(sem("t1_free"), 1)
            s.activation(t1[:, :, :], cs[:, :, :], ACT.Exp, scale=-1.0).then_inc(sem("exp_ready"), 1)
            act.wait_ge(sem("rest_ready"), 1)
            s.activation(t3[:, :, :], t3[:, :, :], ACT.Exp).then_inc(sem("exp_ready"), 1)
            for m in range(2):
                copy(qd[:, 2 * m:2 * m + 2, :], f"in{7 + m}", two)
            for m in range(2):
                copy(kd[:, 2 * m:2 * m + 2, :], f"in{9 + m}", two)
            for i in range(NT):
                for q in range(2):
                    copy(Lsb[:, i, q:NH:2, :], f"L{i}{q}", lambda v: v.rearrange("p (h k) -> p h k", h=NP))
                    taken(act, f"L{i}{q}")
            for j in range(P // SUB):
                act.dma_start(blocks[0, j].rearrange("q a b -> a q b"),
                              Lsb[SUB * j:SUB * j + SUB, :, :, SUB * j:SUB * j + SUB].rearrange("a i h b -> a (i h) b"))\
                   .then_inc(sem("L_blocks_out"), 16)
            for i in range(NT):
                copy(Zr[:, i, :, 0:HD], f"nat{i}0", lambda v: v.rearrange("p (h k) -> p h k", h=NH))
                copy(Vn[:, i, :], f"nat{i}1")
            act.wait_ge(sem("L_blocks_out"), 16 * (P // SUB))
            act.dma_start(L16[:, :, :], blocks[0].rearrange("j q a b -> (j q) a b")).then_inc(sem("L16_in"), 16)
            act.wait_ge(sem("t3_free"), 1)
            for m in range(2):
                copy(vd[:, :, m * WCOL:(m + 1) * WCOL], f"in{11 + m}", two)

            act.wait_ge(sem("X16_ready"), 1)
            act.wait_ge(sem("const_ready"), 1)
            act.dma_start(blocks[1].rearrange("j q a b -> (j q) a b"), X16[:, :, :]).then_inc(sem("X_blocks_out"), 16)
            act.wait_ge(sem("X_blocks_out"), 16)
            for j in range(P // SUB):
                act.dma_start(XTb[SUB * j:SUB * j + SUB, :, :, SUB * j:SUB * j + SUB].rearrange("c i h a -> c (i h) a"),
                              blocks[1, j].rearrange("q c a -> c q a")).then_inc(sem("XT_in"), 16)
            for i in range(NT):
                copy(Zr[:, i, :, HD:P], f"MV{i}", lambda v: v.rearrange("p (h k) -> p h k", h=NH))
            four = lambda v: v.rearrange("p (h k) -> p h k", h=4)
            for q in range(4):
                copy(Z1[:, q // 2, 4 * (q % 2):4 * (q % 2) + 4, :], f"z1{q}", four)

            def exps(u):
                i, heads = UNITS[u]
                act.wait_ge(sem("dmax_ready"), u + 1)
                w = P * (i + 1)
                if u:
                    product(act, f"at{u - 1}")
                for c in range(2):
                    src = ps[:, where[f"sc{u}{c}"][0], :]
                    for m, hh in enumerate(heads):
                        col = 8 * u + 4 * c + m
                        ins = s.activation(soft[:, c, m * w:(m + 1) * w], src[:, m * w:(m + 1) * w], ACT.Exp, scale=DSCALE,
                                           bias=dst_[:, col:col + 1], accum_out=dst_[:, 32 + col:33 + col])
                        if m < len(heads) - 1:
                            link(ins)
                    drain(ins, f"sc{u}{c}")
                    taken(act, f"sc{u}{c}")
                act.sem_inc(sem("dexp_ready"), 1)

            def head_outputs(u):
                i, heads = UNITS[u]
                n0, nh = heads[0], len(heads)
                copy(odn[:, i, n0 * P:(n0 + nh) * P], f"od{u}", lambda v: v[:, 0:nh * P])
                taken(act, f"od{u}")
                for hh in heads:
                    link(s.activation(osq[:, :], odn[:, i, hh * P:(hh + 1) * P], ACT.Square,
                                      accum_out=st[:, 8 + 4 * i + hh:9 + 4 * i + hh]))

            for q in range(4):
                copy(Z2[:, q // 2, 4 * (q % 2):4 * (q % 2) + 4, :], f"z2{q}", four)
            act.wait_ge(sem("lam_sum_ready"), 1)
            s.activation(lam[:, 2:4], lam[:, 0:2], ACT.Exp).then_inc(sem("lam_exp_ready"), 1)
            exps(0)
            for i in range(NT):
                copy(Y0[:, i, :], f"yz{i}")
            taken(act, "bo1")
            copy(atT[0][:, :], "at0")
            for c in range(NCH - 1):
                copy(PhiPsi[:, c, :, :], f"PP{c}", four)
            head_outputs(0)
            exps(1)
            copy(atT[1][:, :], "at1")
            exps(2)
            head_outputs(1)
            copy(kmT[:, 0:2, :], "kv0", two)
            product(act, "od0")
            copy(atT[0][:, :], "at2")
            head_outputs(2)
            act.sem_inc(sem("osq_ready"), 1)
            act.wait_ge(sem("osr_ready"), 1)
            for i in range(NT):
                for hh in range(DH):
                    link(s.activation(odn[:, i, hh * P:(hh + 1) * P], odn[:, i, hh * P:(hh + 1) * P], ACT.Copy,
                                      scale=st[:, 8 + 4 * i + hh:9 + 4 * i + hh]))
            act.sem_inc(sem("odn_ready"), 1)
            copy(kmT[:, 2:4, :], "kv1", two)
            copy(kmT[:, 4:6, :], "kv2", two)
            act.wait_ge(sem("sub_gain_ready"), 1)
            for i in range(NT):
                o = product(act, f"odT{i}")
                drain(s.activation(xT[:, NP:KC, i * P:(i + 1) * P], four(o), ACT.Copy, scale=lam[:, 5:6]), f"odT{i}")
            copy(kmT[:, 6:8, :], "kv3", two)
            for m in range(2):
                copy(vm[:, :, m * WCOL:(m + 1) * WCOL], f"kv{4 + m}", two)
            act.wait_ge(sem("h_ready"), 1)
            sumsq(h, 4)
            copy(vm[:, :, 2 * WCOL:3 * WCOL], "kv6", two)
            for m in range(4):
                copy(qx[:, 2 * m:2 * m + 2, :], f"wq{m}", two)
            for m in range(XH // 2):
                for i in range(NT):
                    act.wait_ge(sem("xmax_ready"), 2 * m + i + 1)
                    src = two(ps[:, where[f"xs{m}{i}"][0], :])
                    for q in range(2):
                        col = 4 * m + 2 * i + q
                        ins = s.activation(px[m][:, i, q, :], src[:, q, :], ACT.Exp, scale=XSCALE, bias=xst[:, col:col + 1],
                                           accum_out=xst[:, 8 + col:9 + col])
                        if q == 0:
                            link(ins)
                    drain(ins, f"xs{m}{i}")
            copy(vm[:, :, 3 * WCOL:4 * WCOL], "kv7", two)
            for m in range(XH // 2):
                for q in range(2):
                    copy(oT[:, 4 * m + 2 * q:4 * m + 2 * q + 2, :], f"xo{m}{q}", two)
            act.wait_ge(sem("h_ready"), 2)
            sumsq(h, 6)
            taken(act, "wo3")
            act.dma_start(n3g[:, :], a["norm3_g"].to_broadcast([P, D])).then_inc(sem("n3g_in"), 16)
            act.dma_start(fing[:, :], a["final_g"].unsqueeze(0).to_broadcast([P, D])).then_inc(sem("fing_in"), 16)
            act.dma_start(b1a[0:E, :], a["moe_b1"][0]).then_inc(sem("bias_in"), 16)
            act.dma_start(b2a[0:E, :], a["moe_b2"][0]).then_inc(sem("bias_in"), 16)
            for i in range(NT):
                act.wait_ge(sem("top_ready"), i + 1)
                s.activation(rt[:, 16 * i + 8:16 * i + 12], rt[:, 16 * i:16 * i + 4], ACT.Exp, bias=rt[:, 16 * i + 12:16 * i + 13],
                             accum_out=rt[:, 16 * i + 13:16 * i + 14]).then_inc(sem("gexp_ready"), 1)

            act.wait_ge(sem("npass_ready"), 1)
            act.wait_ge(sem("xe_filled"), 1)
            s.activation(xe[:, :], ps[:, 6, :], ACT.Copy).then_inc(sem("xe_ready"), 1)
            np_ = act.value_load(npass[0:1, 0:1], min_val=1, max_val=PASSES)
            with act.Fori(0, np_) as q:
                with act.Fori(0, E) as e:
                    it = act.snap(q * E + e)
                    act.wait_ge(sem("gate_ready"), it + 1)
                    s.activation(sg[:, :], gg[:, :], ACT.Sigmoid, scale=1.702).then_inc(sem("sig_ready"), 1)
                    act.wait_ge(sem("GT_filled"), it + 1)
                    s.activation(GT[:, :], ps[:, 7, 0:T], ACT.Copy).then_inc(sem("GT_ready"), 1)
                    act.wait_ge(sem("xe_filled"), it + 2)
                    s.activation(xe[:, :], ps[:, 6, :], ACT.Copy).then_inc(sem("xe_ready"), 1)
                    act.wait_ge(sem("acT_filled"), it + 1)
                    s.activation(acT[:, :], ps[:, 7, :], ACT.Copy).then_inc(sem("acT_ready"), 1)
            act.wait_ge(sem("h_ready"), 3)
            sumsq(h, 32)

        @block.tensor
        def _(pe):
            t = nc.tensor

            def weights(label):
                n = ORDER.index(label)
                pe.wait_ge(landed[n % PRE], 16 * (n // PRE + 1))
                return ring[:, n % PRE, :].rearrange("p (k n) -> p k n", k=KC)

            def turned_parts(label, src):
                w = weights(label)
                o = begin(pe, label)
                for q in range(2):
                    for k in range(KC):
                        ins = t.matmul(o[:, q * T:(q + 1) * T], w[:, k, q * P:(q + 1) * P], src[:, k, :],
                                       start=(k == 0), stop=(k == KC - 1))
                        if k == KC // 2 - 1:
                            yield
                    if q == 0:
                        yield
                done(ins, label)
                yield

            def turned(label, src):
                for _ in turned_parts(label, src):
                    pass

            def natural(label, src):
                w = weights(label)
                o = begin(pe, label)
                for i in range(NT):
                    for k in range(KC):
                        ins = t.matmul(o[:, i * WCOL:(i + 1) * WCOL], src[:, k, i * P:(i + 1) * P], w[:, k, :],
                                       start=(k == 0), stop=(k == KC - 1))
                done(ins, label)

            def turn4(name, srcs):
                o = begin(pe, name)
                for q, v in enumerate(srcs):
                    ins = t.transpose(o[:, q * P:(q + 1) * P], v, ident[:, :])
                done(ins, name)

            def turn_rows(s, k, src=xs):
                pe.wait_ge(sem("scaled_ready"), k)
                for i in range(NT):
                    for q in range(2):
                        turn4(f"{s}T{2 * i + q}", [src[:, i, (4 * q + m) * P:(4 * q + m + 1) * P] for m in range(4)])

            pe.wait_ge(sem("ident_ready"), 1)
            turn_rows("x", 1)
            pe.wait_ge(sem("rows_in"), 16 * len(ROWS))
            o = begin(pe, "prm")
            done(t.transpose(o[:, 0:NROWS], prow[:, :], ident[0:NROWS, 0:NROWS]), "prm")
            for q in range(4):
                taken(pe, f"xT{q}")
            turned("in2", xT)
            turned("in3", xT)
            turn_rows("mem", 2, memN)
            turned("in6", xT)
            turned("in0", xT)
            pe.wait_ge(sem("kksq_ready"), 1)
            pe.wait_ge(sem("const_ready"), 1)
            o = begin(pe, "ksum")
            for j in range(NP):
                ins = t.matmul(o[0:NH, 0:T], hsel[:, j, :], t2[:, j, :], start=(j == 0), stop=(j == NP - 1))
            done(ins, "ksum")
            turned("in1", xT)
            pe.wait_ge(sem("lora_in"), 48)
            pe.wait_ge(sem("lora_x_ready"), 1)
            pe.wait_ge(sem("gd_ready"), 1)
            for m in range(2):
                for nm, lo, hi, lw_, rhs in (("lw", 0, 64, lora, 12), ("la", 64, 128, lora, 12), ("lg", 0, 128, g2s, 13)):
                    o = begin(pe, f"{nm}{m}")
                    for q in range(2):
                        j = 2 * m + q
                        ins = t.matmul(o[:, q * T:(q + 1) * T], lw_[lo:hi, j * P:(j + 1) * P], pT[lo:hi, rhs, :], start=True, stop=True)
                    done(ins, f"{nm}{m}")
            turned("in4", xT)
            pe.wait_ge(sem("knorm_ready"), 1)
            for m in range(2):
                o = begin(pe, f"kb{m}")
                for q in range(2):
                    ins = t.matmul(o[:, q * T:(q + 1) * T], hselT[:, 2 * m + q, :], krs[0:NH, :], start=True, stop=True)
                done(ins, f"kb{m}")
            for m in (5, 7, 8, 9, 10):
                turned(f"in{m}", xT)

            pe.wait_ge(sem("ab_ready"), 1)
            for i in range(NT):
                tok = slice(i * P, (i + 1) * P)
                oL = [begin(pe, f"L{i}{q}") for q in range(2)]
                for hh in range(NH):
                    j, q = hh // 2, hh % 2
                    rows = slice(q * HD, (q + 1) * HD)
                    ins = t.matmul(oL[q][:, j * P:(j + 1) * P], AR[rows, j, i, 0, :], BT[rows, j, tok], start=True, stop=True)
                    if j == NP - 1:
                        done(ins, f"L{i}{q}")
            pe.wait_ge(sem("ops_ready"), 1)
            for i in range(NT):
                tok = slice(i * P, (i + 1) * P)
                turn4(f"nat{i}0", [AR[:, j, i, 0, :] for j in range(NP)])
                turn4(f"nat{i}1", [vT[:, j, tok] for j in range(NP)])
                turn4(f"nat{i}2", [Bd[:, j, tok] for j in range(NP)])
                turn4(f"nat{i}3", [Kd[:, j, tok] for j in range(NP)])

            def chunk_products(i):
                tok = slice(i * P, (i + 1) * P)
                for hh in range(NH):
                    j, q = hh // 2, hh % 2
                    rows = slice(q * HD, (q + 1) * HD)
                    ar = AR[rows, j, i, :, :].rearrange("p a b -> p (a b)")
                    o = begin(pe, f"LGMH{i}{hh}")
                    t.matmul(o[:, 0:T], BT[rows, j, tok], ar, start=True, stop=True)
                    done(t.matmul(o[:, T:2 * T], KT[rows, j, tok], ar, start=True, stop=True), f"LGMH{i}{hh}")

            chunk_products(0)
            natural("in11", xT)
            natural("in12", xT)
            chunk_products(1)
            pe.wait_ge(sem("rk_ready"), 1)
            for m in range(2):
                o = begin(pe, f"bo{m}")
                done(t.matmul(o[:, :], onesbd[:, :], rk[:, 2 * m:2 * m + 2, :].rearrange("p a b -> p (a b)"), start=True, stop=True), f"bo{m}")

            def scores(u):
                i, heads = UNITS[u]
                w = P * (i + 1)
                o = [begin(pe, f"sc{u}{c}") for c in range(2)]
                for m, hh in enumerate(heads):
                    for c in range(2):
                        rows = slice(c * HD, (c + 1) * HD)
                        ins = t.matmul(o[c][:, m * w:(m + 1) * w], qd[rows, hh, i * P:(i + 1) * P], kd[rows, hh, 0:w], start=True, stop=True)
                        if m == len(heads) - 1:
                            done(ins, f"sc{u}{c}")

            def turn_weights(u):
                pe.wait_ge(sem("attn_ready"), u + 1)
                turn4(f"at{u}", [soft[:, 0, m * P:(m + 1) * P] for m in range(4)])

            def values(u):
                i, heads = UNITS[u]
                oo = begin(pe, f"od{u}")
                taken(pe, f"at{u}")
                for m, hh in enumerate(heads):
                    for kb in range(i + 1):
                        ins = t.matmul(oo[:, m * P:(m + 1) * P], atT[u % 2][:, (m * (i + 1) + kb) * P:(m * (i + 1) + kb + 1) * P],
                                       vd[:, kb, hh * P:(hh + 1) * P], start=(kb == 0), stop=(kb == i))
                done(ins, f"od{u}")

            for i in range(NT):
                o = begin(pe, f"MV{i}")
                for hh in range(NH):
                    if hh == 0:
                        taken(pe, f"LGMH{i}7")
                        taken(pe, f"LGMH{i}6")
                        taken(pe, f"LGMH{i}5")
                        taken(pe, f"LGMH{i}4")
                        taken(pe, f"nat{i}1")
                    ins = t.matmul(o[:, hh * HD:(hh + 1) * HD], LGMH[:, i, hh, 2 * P:3 * P], Vn[:, i, hh * HD:(hh + 1) * HD],
                                   start=True, stop=True)
                done(ins, f"MV{i}")
            pe.wait_ge(sem("XT_in"), 16 * (P // SUB))

            def pairs(nm, left, right, before):
                for g in range(4):
                    before(g)
                    o = begin(pe, f"{nm}{g}")
                    for m in range(4):
                        i, hh = g // 2, 4 * (g % 2) + m
                        ins = t.matmul(o[:, m * P:(m + 1) * P], left(i, hh), right(i, hh), start=True, stop=True)
                    done(ins, f"{nm}{g}")

            pairs("z1", lambda i, hh: XTb[:, i, hh, :], lambda i, hh: Zr[:, i, hh, :], lambda g: taken(pe, f"MV{g // 2}"))
            for m in range(7, 13):
                taken(pe, f"in{m}")
            scores(0)
            pairs("z2", lambda i, hh: LGMH[:, i, hh, 0:P], lambda i, hh: Z1[:, i, hh, :], lambda g: taken(pe, f"z1{g}"))
            pairs("z3", lambda i, hh: XTb[:, i, hh, :], lambda i, hh: Z2[:, i, hh, :], lambda g: taken(pe, f"z2{g}"))
            for q in range(4):
                taken(pe, f"z3{q}")
            for i in range(NT):
                tok = slice(i * P, (i + 1) * P)
                o = begin(pe, f"Rh{i}")
                for hh in range(NH):
                    j, q = hh // 2, hh % 2
                    ins = t.matmul(o[q * HD:(q + 1) * HD, j * P:(j + 1) * P], Zf[:, i, hh, 0:HD], LGMH[:, i, hh, P:2 * P],
                                   start=True, stop=True)
                done(ins, f"Rh{i}")
                o = begin(pe, f"yz{i}")
                for hh in range(NH):
                    t.matmul(o[:, hh * HD:(hh + 1) * HD], LGMH[:, i, hh, P:2 * P], Zf[:, i, hh, HD:P], start=True, stop=False)
                    ins = t.matmul(o[:, hh * HD:(hh + 1) * HD], LGMH[:, i, hh, 3 * P:4 * P], Vn[:, i, hh * HD:(hh + 1) * HD],
                                   start=False, stop=True)
                done(ins, f"yz{i}")
            turn_weights(0)
            values(0)
            scores(1)
            for i in range(NT):
                chunks = [c for c in range(4 * i, 4 * i + 4) if c < NCH - 1]
                os_ = {c: begin(pe, f"PP{c}") for c in chunks}
                for hh in range(NH):
                    j, q = hh // 2, hh % 2
                    col = slice(hh * HD, (hh + 1) * HD)
                    for step in range(3):
                        for c in chunks:
                            r = slice(CH * (c % 4), CH * (c % 4) + CH)
                            at = os_[c][q * HD:(q + 1) * HD, j * P + (HD if step else 0):j * P + (2 * HD if step else HD)]
                            left, right = ((Zf[r, i, hh, 0:HD], Bn[r, i, col]), (Bn[r, i, col], Zf[r, i, hh, HD:P]),
                                           (Kn[r, i, col], Vn[r, i, col]))[step]
                            ins = t.matmul(at, left, right, start=(step < 2), stop=(step != 1),
                                           tile_position=(CH * (c % 4), q * HD))
                            if step == 2 and hh == NH - 1:
                                done(ins, f"PP{c}")
            turn_weights(1)
            values(1)
            scores(2)
            for q in range(4):
                taken(pe, f"memT{q}")
            turned("kv0", memT)
            turn_weights(2)
            values(2)
            filler = itertools.chain(turned_parts("kv1", memT), turned_parts("kv2", memT))
            for i in range(NT):
                oy = [begin(pe, f"Y{i}{q}") for q in range(2)]
                for c in range(4 * i, 4 * i + 4):
                    pe.wait_ge(sem("S_ready"), c + 1)
                    if c == 0:
                        taken(pe, "Rh0")
                        taken(pe, "Rh1")
                    if 0 < c < NCH - 1:
                        taken(pe, f"PP{c}")
                        o = [begin(pe, f"S{c}{q}") for q in range(2)]
                        for j in range(NP):
                            for q in range(2):
                                rows = slice(q * HD, (q + 1) * HD)
                                ins = t.matmul(o[q][rows, j * HD:(j + 1) * HD], PhiPsi[rows, c, j, 0:HD], St[rows, c, j, :],
                                               start=True, stop=True)
                                if j == NP - 1:
                                    done(ins, f"S{c}{q}")
                        next(filler)
                    r = slice(CH * (c % 4), CH * (c % 4) + CH)
                    for j in range(NP):
                        for q in range(2):
                            rows = slice(q * HD, (q + 1) * HD)
                            ins = t.matmul(oy[q][r, j * HD:(j + 1) * HD], RhT[rows, j, c * CH:(c + 1) * CH], St[rows, c, j, :],
                                           start=True, stop=True, tile_position=(q * HD, CH * (c % 4)))
                            if j == NP - 1 and c % 4 == 3:
                                done(ins, f"Y{i}{q}")
            for _ in filler:
                pass
            pe.wait_ge(sem("odn_ready"), 1)
            for i in range(NT):
                turn4(f"odT{i}", [odn[:, i, m * P:(m + 1) * P] for m in range(4)])
            turned("kv3", memT)
            natural("kv4", memT)
            natural("kv5", memT)
            pe.wait_ge(sem("yn_ready"), 1)
            for i in range(NT):
                turn4(f"ynT{i}", [Yn[:, i, m * P:(m + 1) * P] for m in range(4)])
            t.sem_inc(sem("mixers_through"), 1)
            pe.wait_ge(sem("yT_ready"), 1)
            for i in range(NT):
                taken(pe, f"odT{i}")
            for m in range(4):
                natural(f"out{m}", xT)
            natural("kv6", memT)
            turn_rows("h1", 3)
            for q in range(4):
                taken(pe, f"h1T{q}")
            for m in range(4):
                turned(f"wq{m}", xT)
            for m in range(4):
                taken(pe, f"wq{m}")
                taken(pe, f"kv{m}")
            for m in range(XH // 2):
                for i in range(NT):
                    o = begin(pe, f"xs{m}{i}")
                    for q in range(2):
                        for k in range(2):
                            c = 2 * (2 * m + q) + k
                            ins = t.matmul(o[:, q * T:(q + 1) * T], qx[:, c, i * P:(i + 1) * P], kmT[:, c, :], start=(k == 0), stop=(k == 1))
                    done(ins, f"xs{m}{i}")
            natural("kv7", memT)
            for m in range(4, 8):
                taken(pe, f"kv{m}")
            for m in range(XH // 2):
                for i in range(NT):
                    pe.wait_ge(sem("xp_ready"), 2 * m + i + 1)
                    turn4(f"xp{m}{i}", [px[m][:, i, q, kb * P:(kb + 1) * P] for q in range(2) for kb in range(2)])
                for i in range(NT):
                    taken(pe, f"xp{m}{i}")
                for q in range(2):
                    o = begin(pe, f"xo{m}{q}")
                    for c in range(2):
                        for kb in range(2):
                            col = (2 * m + q) * T + c * P
                            ins = t.matmul(o[:, c * T:(c + 1) * T], vm[:, kb, col:col + P], pxT[m][:, kb, q, :], start=(kb == 0), stop=(kb == 1))
                    done(ins, f"xo{m}{q}")
            for m in range(XH // 2):
                for q in range(2):
                    taken(pe, f"xo{m}{q}")
            t.sem_inc(sem("cross_through"), 1)
            for m in range(4):
                natural(f"wo{m}", oT)
            turn_rows("h2", 4)
            for q in range(4):
                taken(pe, f"h2T{q}")
            pe.wait_ge(sem("router_in"), 32)
            o = begin(pe, "logit")
            for i in range(NT):
                for k in range(KC):
                    t.matmul(o[:, i * E:(i + 1) * E], x3T[:, k, i * P:(i + 1) * P], rws[:, k, :], start=(k == 0), stop=False)
                ins = t.matmul(o[:, i * E:(i + 1) * E], ones[0:1, :], rbs[:, :], start=False, stop=True)
            done(ins, "logit")
            pe.wait_ge(sem("mask_ready"), 1)
            o = begin(pe, "pos")
            t.matmul(o[:, 0:E], tri[:, :], mask[:, 0, :], start=True, stop=True)
            t.matmul(o[:, E:2 * E], tri[:, :], mask[:, 1, :], start=True, stop=False)
            t.matmul(o[:, E:2 * E], ones[:, :], mask[:, 0, :], start=False, stop=True)
            t.matmul(o[0:1, 2 * E:3 * E], ones[:, 0:1], mask[:, 0, :], start=True, stop=False)
            done(t.matmul(o[0:1, 2 * E:3 * E], ones[:, 0:1], mask[:, 1, :], start=False, stop=True), "pos")
            pe.wait_ge(sem("gates_ready"), 1)
            o = begin(pe, "gateT")
            for i in range(NT):
                ins = t.transpose(o[0:E, i * P:(i + 1) * P], gate[:, i, :], ident[:, :])
            done(ins, "gateT")
            taken(pe, "gateT")
            pe.wait_ge(sem("bias_in"), 32)
            for nm in ("wo2", "wo3", "h2T0", "h2T1"):
                taken(pe, nm)
            for i in range(NT):
                for c in range(2):
                    t.matmul(ps[:, 2 * i + c, :], gateT[0:E, i * P:(i + 1) * P], b2a[0:E, c * 512:(c + 1) * 512],
                             start=True, stop=False, skip_group_check=True)

            def gather():
                for i in range(NT):
                    for c in range(2):
                        ins = t.matmul(ps[c * BLK:(c + 1) * BLK, 6, :], sel[:, i, :], x3[:, i, c * 512:(c + 1) * 512],
                                       start=(i == 0), stop=(i == NT - 1), skip_group_check=True)
                ins.then_inc(sem("xe_filled"), 1)

            def gather_turn():
                for m in range(4):
                    ins = t.transpose(ps[:, 6, m * P:(m + 1) * P], xe[:, m * P:(m + 1) * P], ident[:, :])
                ins.then_inc(sem("xeT_filled"), 1)

            def gate_turn():
                for i in range(NT):
                    ins = t.transpose(ps[:, 7, i * P:(i + 1) * P], selg[:, i, :], ident[:, :])
                ins.then_inc(sem("GT_filled"), 1)

            def scatter():
                for i in range(NT):
                    for c in range(2):
                        rows = slice(c * BLK, (c + 1) * BLK)
                        ins = t.matmul(ps[:, 2 * i + c, :], GT[rows, i * P:(i + 1) * P], yy[rows, :], start=False, stop=False,
                                       skip_group_check=True)
                ins.then_inc(sem("scattered"), 1)

            for b, nm in ((4, "xp10"), (5, "xp11"), (6, "gateT"), (7, "pos")):
                taken(pe, nm)
            taken(pe, "h2T2")
            taken(pe, "h2T3")
            pe.wait_ge(sem("sel_ready"), 2)
            pe.wait_ge(sem("x3_ready"), 1)
            gather()
            pe.wait_ge(sem("xe_ready"), 1)
            gather_turn()
            pe.wait_ge(sem("npass_ready"), 1)
            np_ = pe.value_load(npass[0:1, 0:1], min_val=1, max_val=PASSES)
            with pe.Fori(0, np_) as q_:
                with pe.Fori(0, E) as e:
                    it = pe.snap(q_ * E + e)
                    pe.wait_ge(sem("onehot_ready"), it + 1)
                    pe.wait_ge(sem("lin_read"), it + 1)
                    for b in range(2):
                        for c in range(2):
                            f0 = b * F + c * 512
                            t.matmul(ps[c * BLK:(c + 1) * BLK, 4 + b, :], onehot[0:E, :], b1a[0:E, f0:f0 + 512], start=True, stop=False,
                                     skip_group_check=True)
                    pe.wait_ge(sem("xeT_ready"), it + 1)
                    for k in range(KC):
                        pe.wait_ge(elanded[k], it * 16 + 16)
                        for b in range(2):
                            for c in range(2):
                                f0 = b * F + c * 512
                                col = (k % 4) * P + (k // 4) * BLK
                                ins = t.matmul(ps[c * BLK:(c + 1) * BLK, 4 + b, :], xeT[:, col:col + BLK], ring[:, k, f0:f0 + 512],
                                               start=False, stop=(k == KC - 1), skip_group_check=True)
                        if k < KC - 1:
                            ins.then_inc(eused, 1)
                        else:
                            ins.then_inc(sem("hid_filled"), 1)
                    pe.wait_ge(sem("GT_ready"), it + 1)
                    pe.wait_ge(sem("yy_ready"), it + 1)
                    scatter()
                    pe.wait_ge(sem("selg_ready"), it * 2 + 2)
                    gate_turn()
                    pe.wait_ge(sem("hid_filled"), it + 1)
                    t.sem_inc(eused, 1)
                    pe.wait_ge(sem("sel_ready"), it * 2 + 4)
                    gather()
                    pe.wait_ge(sem("GT_ready"), it + 2)
                    pe.wait_ge(sem("ac_ready"), it + 1)
                    for m in range(4):
                        ins = t.transpose(ps[:, 7, m * P:(m + 1) * P], ac[:, m * P:(m + 1) * P], ident[:, :])
                    ins.then_inc(sem("acT_filled"), 1)
                    pe.wait_ge(sem("xe_ready"), it + 2)
                    gather_turn()
                    pe.wait_ge(sem("acT_ready"), it + 1)
                    for k in range(KC):
                        if k % 2 == 0:
                            pe.wait_ge(elanded[8 + k // 2], it * 16 + 16)
                        w = ring[:, 8 + k // 2, (k % 2) * D:(k % 2 + 1) * D]
                        col = (k % 4) * P + (k // 4) * BLK
                        for c in range(2):
                            ins = t.matmul(ps[c * BLK:(c + 1) * BLK, 7, :], acT[:, col:col + BLK], w[:, c * 512:(c + 1) * 512],
                                           start=(k == 0), stop=(k == KC - 1), skip_group_check=True)
                        if k % 2 and k < KC - 1:
                            ins.then_inc(eused, 1)
                    ins.then_inc(sem("yy_filled"), 1)
                    pe.wait_ge(sem("yy_filled"), it + 1)
                    t.sem_inc(eused, 1)
            n_it = pe.snap(np_ * E)
            pe.wait_ge(sem("GT_ready"), n_it + 1)
            pe.wait_ge(sem("yy_ready"), n_it + 1)
            for i in range(NT):
                for c in range(2):
                    rows = slice(c * BLK, (c + 1) * BLK)
                    ins = t.matmul(ps[:, 2 * i + c, :], GT[rows, i * P:(i + 1) * P], yy[rows, :], start=False, stop=True,
                                   skip_group_check=True)
            ins.then_inc(sem("sum_ready"), 1)

        @block.vector
        def _(dve):
            v = nc.vector
            n = [0]

            def link(ins):
                n[0] += 1
                ins.then_inc(sem("dve_step"), 1)
                dve.wait_ge(sem("dve_step"), n[0])

            def dlink(ins, name):
                drain(ins, name)
                taken(dve, name)

            four = lambda x: x.rearrange("p (h k) -> p h k", h=4)
            two = lambda x: x.rearrange("p (a b) -> p a b", a=2)

            def rsqrt(y, x, s1, s2):
                link(v.tensor_scalar(s1, x, -0.5, None, ALU.mult))
                link(v.tensor_scalar(y.bitcast(I32), x.bitcast(I32), -0.5, 1597463007.0, ALU.mult, ALU.add))
                for _ in range(4):
                    link(v.tensor_tensor(s2, y, y, ALU.mult))
                    link(v.tensor_tensor(s2, s2, s1, ALU.mult))
                    link(v.scalar_tensor_tensor(out=y, in0=s2, scalar=1.5, in1=y, op0=ALU.add, op1=ALU.mult))

            def rstd(c0, c1, width, eps):
                x = st[:, c0:c1]
                link(v.tensor_scalar(x, x, 1.0 / width, eps, ALU.mult, ALU.add))
                rsqrt(x, x, wk[:, 0:c1 - c0], wk[:, 32:32 + c1 - c0])

            def scale_rows(src, col, k, dst=xs):
                dve.wait_ge(sem("stat_ready"), k)
                rstd(col, col + 2, D, EPS)
                for i in range(NT):
                    link(v.tensor_scalar(dst[:, i, :], src[:, i, :], st[:, col + i:col + i + 1], None, ALU.mult))
                dve.sem_inc(sem("scaled_ready"), 1)

            def take_rows(s, dst, g):
                for i in range(NT):
                    for q in range(2):
                        nm = f"{s}T{2 * i + q}"
                        o = four(product(dve, nm))
                        drain(v.tensor_tensor(dst[:, 4 * q:4 * q + 4, i * P:(i + 1) * P], o, gbc(g, 4 * q, 4), ALU.mult), nm)

            scale_rows(h, 2, 1)
            o = product(dve, "prm")
            for q in range(4):
                product(dve, f"xT{q}")
            dlink(v.tensor_copy(prm[:, :], o[:, 0:NROWS]), "prm")
            take_rows("x", xT, "norm1_g")
            link(v.tensor_scalar(mu1[:, :], prm[:, ROW["mu_shift"]:ROW["mu_shift"] + 14], -1.0, 1.0, ALU.mult, ALU.add))
            dve.sem_inc(sem("mu_ready"), 1)
            link(v.tensor_scalar(w0h[:, :], prm[:, ROW["w0"]:ROW["w0"] + 8], 0.5, None, ALU.mult))
            scale_rows(memN, 0, 2, memN)
            dve.wait_ge(sem("const_ready"), 1)

            shifts = [0]

            def shift(m):
                src = two(product(dve, f"in{m}"))
                shifts[0] += 1
                dve.wait_ge(sem("unshifted_ready"), 2 * shifts[0])
                for q in range(2):
                    j = 2 * m + q
                    mu = prm[:, ROW["mu_shift"] + j:ROW["mu_shift"] + j + 1]
                    ins = v.scalar_tensor_tensor(out=pT[:, j, 1:T], in0=src[:, q, 0:T - 1], scalar=mu, in1=pT[:, j, 1:T],
                                                 op0=ALU.mult, op1=ALU.add)
                    if q == 0:
                        link(ins)
                dlink(ins, f"in{m}")
                dve.sem_inc(sem("shifted_ready"), 1)

            pr = lambda nm, j: prm[:, ROW[nm] + j:ROW[nm] + j + 1]
            shift(2)
            shift(3)
            for j in range(NP):
                ins = v.tensor_scalar(kk[:, j, :], kT[:, j, :], pr("k_k", j), None, ALU.mult)
            link(ins)
            link(v.tensor_tensor(t2[:, :, :], kk[:, :, :], kk[:, :, :], ALU.mult))
            dve.sem_inc(sem("kksq_ready"), 1)
            take_rows("mem", memT, "mem_norm_g")
            shift(6)
            dve.wait_ge(sem("gd_tanh_ready"), 1)
            link(v.tensor_scalar(pT[:, 13, :], pT[:, 13, :], 0.5, 0.5, ALU.mult, ALU.add))
            dve.sem_inc(sem("gd_ready"), 1)
            dve.wait_ge(sem("lam_in"), 64)
            for m in range(2):
                link(v.tensor_tensor(lamv[:, 2 * m, :], lamv[:, 2 * m, :], lamv[:, 2 * m + 1, :], ALU.mult))
                link(v.reduce_sum(lam[:, m:m + 1], lamv[:, 2 * m, :], AX.X))
            dve.sem_inc(sem("lam_sum_ready"), 1)
            shift(0)
            o = product(dve, "ksum")
            dlink(v.tensor_scalar(krs[0:NH, :], o[0:NH, 0:T], 1e-24, None, ALU.max), "ksum")
            rsqrt(krs[0:NH, :], krs[0:NH, :], kra[0:NH, :], krb[0:NH, :])
            dve.sem_inc(sem("knorm_ready"), 1)
            shift(1)
            for m in range(2):
                taken(dve, f"lw{m}")
            link(v.tensor_scalar(lw[:, :, :], lw[:, :, :], 1.0, 0.5 * NEG_EXP_HALF, ALU.add, ALU.mult))
            for j in range(NP):
                ins = v.tensor_tensor_scan(cs[:, j, :], keep[:, :], lw[:, j, :], 0.0, ALU.mult, ALU.add)
            link(ins)
            link(v.tensor_copy(tail[:, :, :], cs[:, :, CH - 1:T:CH]))
            dve.sem_inc(sem("cs_ready"), 1)
            link(v.tensor_tensor(lw[:, :, :], cs[:, :, :], lw[:, :, :], ALU.subtract))
            dve.sem_inc(sem("ex_ready"), 1)
            cs4 = cs[:, :, :].rearrange("p j (c t) -> p j c t", t=CH)
            t34 = t3[:, :, :].rearrange("p j (c t) -> p j c t", t=CH)
            for m in range(2):
                taken(dve, f"la{m}")
            link(v.tensor_scalar(aa[:, :, :], aa[:, :, :], 0.5, 0.5, ALU.mult, ALU.add))
            for m in range(2):
                o = two(product(dve, f"kb{m}"))
                kv = kk[:, 2 * m:2 * m + 2, :]
                dlink(v.tensor_tensor(kv, o, kv, ALU.mult), f"kb{m}")
            dve.wait_ge(sem("exp_ready"), 1)
            for j in range(NP):
                ins = v.tensor_tensor(AR[:, j, :, 1, :], two(rT[:, j, :]), two(t1[:, j, :]), ALU.mult)
            link(ins)
            dve.sem_inc(sem("t1_free"), 1)
            shift(4)
            product(dve, "lg1")
            for j in range(NP):
                ins = v.tensor_tensor(t34[:, j], tail[:, j, :].unsqueeze(2).to_broadcast([P, NCH, CH]), cs4[:, j], ALU.subtract)
            link(ins)
            dve.sem_inc(sem("rest_ready"), 1)
            for j in range(NP):
                link(v.tensor_scalar(KT[:, j, :], aa[:, j, :], 1.0, pr("k_a", j), ALU.subtract, ALU.mult))
                link(v.scalar_tensor_tensor(out=kT[:, j, :], in0=KT[:, j, :], scalar=1.0, in1=kT[:, j, :], op0=ALU.add, op1=ALU.mult))
            link(v.tensor_tensor(aa[:, :, :], kk[:, :, :], aa[:, :, :], ALU.mult))
            dve.wait_ge(sem("exp_ready"), 3)
            for j in range(NP):
                link(v.scalar_tensor_tensor(out=AR[:, j, :, 0, :], in0=two(kk[:, j, :]), scalar=-1.0, in1=two(lw[:, j, :]),
                                            op0=ALU.mult, op1=ALU.mult))
            dve.wait_ge(sem("exp_ready"), 4)
            link(v.tensor_tensor(BT[:, :, :], aa[:, :, :], t1[:, :, :], ALU.mult))
            dve.sem_inc(sem("ab_ready"), 1)
            shift(5)
            link(v.tensor_tensor(KT[:, :, :], kT[:, :, :], t1[:, :, :], ALU.mult))
            dve.wait_ge(sem("exp_ready"), 5)
            link(v.tensor_tensor(Bd[:, :, :], aa[:, :, :], t3[:, :, :], ALU.mult))
            link(v.tensor_tensor(Kd[:, :, :], kT[:, :, :], t3[:, :, :], ALU.mult))
            dve.sem_inc(sem("t3_free"), 1)
            dve.sem_inc(sem("ops_ready"), 1)
            for i in range(NT):
                o = product(dve, f"nat{i}2")
                drain(v.tensor_copy(Bn[:, i, :], o), f"nat{i}2")
                o = product(dve, f"nat{i}3")
                drain(v.tensor_copy(Kn[:, i, :], o), f"nat{i}3")

            def masked(i):
                for hh in range(NH):
                    o = product(dve, f"LGMH{i}{hh}")
                    drain(v.tensor_tensor(LGMH[:, i, hh, :], o, masks[:, :, :].rearrange("p a b -> p (a b)"), ALU.mult), f"LGMH{i}{hh}")

            masked(0)
            dve.wait_ge(sem("L16_in"), 16)
            dve.wait_ge(sem("X16_unit"), 1)
            for r in range(1, SUB):
                link(v.tensor_tensor(w16[:, 0:r, 0:r], X16[:, 0:r, 0:r], L16[:, r:r + 1, 0:r].to_broadcast([P, r, r]), ALU.mult))
                link(v.reduce_sum(X16[:, 0:r, r:r + 1], w16[:, 0:r, 0:r], AX.X))
            dve.sem_inc(sem("X16_ready"), 1)

            for j in range(NP):
                ins = v.scalar_tensor_tensor(out=rk[:, j, :], in0=rT[:, j, :], scalar=pr("r_k", j), in1=kT[:, j, :],
                                             op0=ALU.mult, op1=ALU.mult)
            link(ins)
            dve.sem_inc(sem("rk_ready"), 1)
            masked(1)
            for m in range(2):
                o = two(product(dve, f"bo{m}"))
                dlink(v.tensor_tensor(bv[:, 2 * m:2 * m + 2, :], o, vT[:, 2 * m:2 * m + 2, :], ALU.mult), f"bo{m}")

            link(v.tensor_scalar(lam[:, 5:6], prm[:, ROW["subln_g"]:ROW["subln_g"] + 1], 1.0 - LAMBDA_INIT, None, ALU.mult))
            dve.sem_inc(sem("sub_gain_ready"), 1)

            def score_max(u):
                i, heads = UNITS[u]
                w = P * (i + 1)
                nh = len(heads)
                for c in range(2):
                    o = product(dve, f"sc{u}{c}").rearrange("p (h k) -> p h k", h=nh)
                    link(v.memset(o[0:64, :, w - 64:w], -1e30))
                    col = 8 * u + 4 * c
                    link(v.reduce_max(dst_[:, col:col + nh], o, AX.X))
                    link(v.tensor_scalar(dst_[:, col:col + nh], dst_[:, col:col + nh], -DSCALE, None, ALU.mult))
                dve.sem_inc(sem("dmax_ready"), 1)

            def combine(u):
                i, heads = UNITS[u]
                w = P * (i + 1)
                nh = len(heads)
                dve.wait_ge(sem("dexp_ready"), u + 1)
                for c in range(2):
                    col = 32 + 8 * u + 4 * c
                    link(v.reciprocal(dst_[:, col:col + nh], dst_[:, col:col + nh]))
                col = 32 + 8 * u + 4
                link(v.tensor_scalar(dst_[:, col:col + nh], dst_[:, col:col + nh], lam[:, 4:5], None, ALU.mult))
                for m in range(nh):
                    a0 = soft[:, 0, m * w:(m + 1) * w]
                    a1 = soft[:, 1, m * w:(m + 1) * w]
                    link(v.tensor_scalar(a0, a0, dst_[:, 32 + 8 * u + m:33 + 8 * u + m], None, ALU.mult))
                    link(v.scalar_tensor_tensor(out=a0, in0=a1, scalar=dst_[:, 36 + 8 * u + m:37 + 8 * u + m], in1=a0,
                                                op0=ALU.mult, op1=ALU.add))
                dve.sem_inc(sem("attn_ready"), 1)

            score_max(0)
            for q in range(4):
                i, h0 = q // 2, 4 * (q % 2)
                o = four(product(dve, f"z3{q}"))
                drain(v.tensor_tensor(Zf[:, i, h0:h0 + 4, :], o, Z1[:, i, h0:h0 + 4, :], ALU.add), f"z3{q}")
            for i in range(NT):
                o = four(product(dve, f"Rh{i}"))
                drain(v.tensor_tensor(RhT[:, :, i * P:(i + 1) * P], o, AR[:, :, i, 1, :], ALU.add), f"Rh{i}")
            dve.wait_ge(sem("lam_exp_ready"), 1)
            link(v.tensor_tensor(lam[:, 4:5], lam[:, 3:4], lam[:, 2:3], ALU.subtract))
            link(v.tensor_scalar(lam[:, 4:5], lam[:, 4:5], -LAMBDA_INIT, None, ALU.add))
            combine(0)
            score_max(1)
            combine(1)
            score_max(2)
            combine(2)

            def outputs(i):
                for q in range(2):
                    o = product(dve, f"Y{i}{q}")[:, 0:NP * HD].rearrange("p (j k) -> p j k", j=NP)
                    y0 = Y0[:, i, :].rearrange("p (j q k) -> p j q k", j=NP, q=2)[:, :, q, :]
                    yn = Yn[:, i, :].rearrange("p (j q k) -> p j q k", j=NP, q=2)[:, :, q, :]
                    dlink(v.tensor_tensor(yn, o, y0, ALU.add), f"Y{i}{q}")

            link(v.memset(St[:, 0, :, :], 0.0))
            dve.sem_inc(sem("S_ready"), 1)
            taken(dve, "PP0")
            link(v.tensor_copy(St[:, 1, :, :], PhiPsi[:, 0, :, HD:P]))
            dve.sem_inc(sem("S_ready"), 1)
            for c in range(1, NCH - 1):
                taken(dve, f"PP{c}")
                link(v.tensor_tensor(sd[:, :, :], St[:, c, :, :], dec[:, :, c:c + 1].to_broadcast([P, NP, HD]), ALU.mult))
                link(v.tensor_tensor(sd[:, :, :], sd[:, :, :], PhiPsi[:, c, :, HD:P], ALU.add))
                for q in range(2):
                    rows = slice(q * HD, (q + 1) * HD)
                    o = product(dve, f"S{c}{q}")[rows, 0:NP * HD].rearrange("p (j k) -> p j k", j=NP)
                    dlink(v.tensor_tensor(St[rows, c + 1, :, :], o, sd[rows, :, :], ALU.add), f"S{c}{q}")
                dve.sem_inc(sem("S_ready"), 1)
                if c == 3:
                    outputs(0)
                if c == 4:
                    dve.wait_ge(sem("osq_ready"), 1)
                    rstd(8, 16, P, EPS)
                    dve.sem_inc(sem("osr_ready"), 1)
            outputs(1)
            for i in range(NT):
                yv = Yn[:, i, :].rearrange("p (h k) -> p h k", h=NH)
                link(v.reduce_sum(st[:, 40 + 8 * i:48 + 8 * i], yv, AX.X))
                link(v.tensor_scalar(st[:, 40 + 8 * i:48 + 8 * i], st[:, 40 + 8 * i:48 + 8 * i], 1.0 / HD, None, ALU.mult))
                link(v.tensor_tensor(yv, yv, st[:, 40 + 8 * i:48 + 8 * i].unsqueeze(2).to_broadcast([P, NH, HD]), ALU.subtract))
                link(v.tensor_tensor(dsq[:, :], Yn[:, i, :], Yn[:, i, :], ALU.mult))
                link(v.reduce_sum(st[:, 16 + 8 * i:24 + 8 * i], dsq[:, :].rearrange("p (h k) -> p h k", h=NH), AX.X))
            rstd(16, 32, HD, GN_EPS)
            for i in range(NT):
                yv = Yn[:, i, :].rearrange("p (h k) -> p h k", h=NH)
                link(v.tensor_tensor(yv, yv, st[:, 16 + 8 * i:24 + 8 * i].unsqueeze(2).to_broadcast([P, NH, HD]), ALU.mult))
            dve.sem_inc(sem("yn_ready"), 1)
            for i in range(NT):
                tok = slice(i * P, (i + 1) * P)
                o = four(product(dve, f"ynT{i}"))
                for j in range(NP):
                    ins = v.tensor_scalar(xT[:, j, tok], o[:, j, :], pr("lnx_g", j), pr("lnx_b", j), ALU.mult, ALU.add)
                    if j < NP - 1:
                        link(ins)
                dlink(ins, f"ynT{i}")
            link(v.tensor_tensor(xT[:, 0:NP, :], xT[:, 0:NP, :], bv[:, :, :], ALU.add))
            link(v.tensor_tensor(xT[:, 0:NP, :], xT[:, 0:NP, :], gT[:, :, :], ALU.mult))
            dve.sem_inc(sem("yT_ready"), 1)
            for m in range(4):
                o = two(product(dve, f"out{m}"))
                hv = h[:, :, m * WCOL:(m + 1) * WCOL]
                dlink(v.tensor_tensor(hv, o, hv, ALU.add), f"out{m}")
            dve.sem_inc(sem("h_ready"), 1)
            scale_rows(h, 4, 3)
            take_rows("h1", xT, "norm2_g")
            for m in range(XH // 2):
                for i in range(NT):
                    o = two(product(dve, f"xs{m}{i}"))
                    col = 4 * m + 2 * i
                    link(v.reduce_max(xst[:, col:col + 2], o, AX.X))
                    link(v.tensor_scalar(xst[:, col:col + 2], xst[:, col:col + 2], -XSCALE, None, ALU.mult))
                    dve.sem_inc(sem("xmax_ready"), 1)
            for m in range(XH // 2):
                for i in range(NT):
                    taken(dve, f"xs{m}{i}")
                    col = 8 + 4 * m + 2 * i
                    link(v.reciprocal(xst[:, col:col + 2], xst[:, col:col + 2]))
                    link(v.tensor_tensor(px[m][:, i, :, :], px[m][:, i, :, :], xst[:, col:col + 2].unsqueeze(2).to_broadcast([P, 2, T]), ALU.mult))
                    dve.sem_inc(sem("xp_ready"), 1)
                for i in range(NT):
                    nm = f"xp{m}{i}"
                    o = product(dve, nm).rearrange("p (q b t) -> p b q t", q=2, b=2)
                    for kb in range(2):
                        ins = v.tensor_copy(pxT[m][:, kb, :, i * P:(i + 1) * P], o[:, kb])
                        if kb == 0:
                            link(ins)
                    dlink(ins, nm)
            for m in range(4):
                o = two(product(dve, f"wo{m}"))
                hv = h[:, :, m * WCOL:(m + 1) * WCOL]
                dlink(v.tensor_tensor(hv, o, hv, ALU.add), f"wo{m}")
            dve.sem_inc(sem("h_ready"), 1)
            scale_rows(h, 6, 4)
            take_rows("h2", x3T, "norm3_g")
            dve.wait_ge(sem("n3g_in"), 16)
            for i in range(NT):
                link(v.scalar_tensor_tensor(out=x3[:, i, :], in0=h[:, i, :], scalar=st[:, 6 + i:7 + i], in1=n3g[:, :],
                                            op0=ALU.mult, op1=ALU.mult))
            dve.sem_inc(sem("x3_ready"), 1)
            o = product(dve, "logit")
            dlink(v.tensor_copy(lg[:, :, :], o[:, 0:NT * E].rearrange("p (i e) -> p i e", i=NT)), "logit")
            for i in range(NT):
                r0 = 16 * i
                link(v.max(rt[:, r0:r0 + 8], lg[:, i, :]))
                link(v.tensor_scalar(rt[:, r0 + 12:r0 + 13], rt[:, r0:r0 + 1], -1.0, None, ALU.mult))
                dve.sem_inc(sem("top_ready"), 1)
                link(v.max_index(ix8[:, i, :], rt[:, r0:r0 + 8], lg[:, i, :]))
                link(v.tensor_copy(rt[:, 32 + 8 * i:40 + 8 * i], ix8[:, i, :]))
                link(v.tensor_scalar(mask[:, i, :], iotaE[:, :], rt[:, 32 + 8 * i:33 + 8 * i], None, ALU.is_equal))
                for k in range(1, TOPK):
                    link(v.scalar_tensor_tensor(out=mask[:, i, :], in0=iotaE[:, :], scalar=rt[:, 32 + 8 * i + k:33 + 8 * i + k],
                                                in1=mask[:, i, :], op0=ALU.is_equal, op1=ALU.add))
            dve.sem_inc(sem("mask_ready"), 1)
            for i in range(NT):
                r0 = 16 * i
                dve.wait_ge(sem("gexp_ready"), i + 1)
                link(v.reciprocal(rt[:, r0 + 14:r0 + 15], rt[:, r0 + 13:r0 + 14]))
                link(v.tensor_scalar(rt[:, r0 + 8:r0 + 12], rt[:, r0 + 8:r0 + 12], rt[:, r0 + 14:r0 + 15], None, ALU.mult))
                link(v.memset(gate[:, i, :], 0.0))
                for k in range(TOPK):
                    link(v.tensor_scalar(rt[:, 64:64 + E], iotaE[:, :], rt[:, 32 + 8 * i + k:33 + 8 * i + k], rt[:, r0 + 8 + k:r0 + 9 + k],
                                         ALU.is_equal, ALU.mult))
                    link(v.tensor_tensor(gate[:, i, :], gate[:, i, :], rt[:, 64:64 + E], ALU.add))
            dve.sem_inc(sem("gates_ready"), 1)
            o = product(dve, "pos")
            link(v.scalar_tensor_tensor(out=post[:, :, 0, :], in0=o[:, 0:NT * E].rearrange("p (i e) -> p i e", i=NT), scalar=1.0,
                                        in1=mask[:, :, :], op0=ALU.add, op1=ALU.mult))
            for k in range(PASSES, -1, -1):
                link(v.tensor_scalar(post[:, :, k, :], post[:, :, 0, :], -1.0 - BLK * k, None, ALU.add))
            link(v.reduce_max(rt[0:1, 128:129], o[0:1, 2 * E:3 * E], AX.X))
            link(v.tensor_scalar(rt[0:1, 129:130], rt[0:1, 128:129], float(BLK), 1.0, ALU.is_gt, ALU.add))
            for k in range(2, PASSES):
                link(v.tensor_scalar(rt[0:1, 130:131], rt[0:1, 128:129], float(k * BLK), None, ALU.is_gt))
                link(v.tensor_tensor(rt[0:1, 129:130], rt[0:1, 129:130], rt[0:1, 130:131], ALU.add))
            dlink(v.tensor_copy(npass[0:1, 0:1], rt[0:1, 129:130]), "pos")
            dve.sem_inc(sem("npass_ready"), 1)
            o = product(dve, "gateT")
            dlink(v.tensor_copy(gateT[0:E, :], o[0:E, 0:T]), "gateT")

            postv = [post[:, i, :, :].rearrange("p k e -> p (k e)") for i in range(NT)]

            for i in range(NT):
                v.tensor_scalar(sel[:, i, :], iota[:, 0:BLK], postv[i][:, 0:1], None, ALU.is_equal).then_inc(sem("sel_ready"), 1)
            link(v.memset(yy[:, :], 0.0))
            dve.sem_inc(sem("yy_ready"), 1)
            link(v.memset(GT[:, :], 0.0))
            dve.sem_inc(sem("GT_ready"), 1)
            dve.sem_inc(sem("lin_read"), 1)
            v.tensor_copy(onehot[0:E, :], identE[:, 0:1].to_broadcast([E, BLK])).then_inc(sem("onehot_ready"), 1)
            dve.wait_ge(sem("xeT_filled"), 1)
            v.tensor_copy(xeT[:, :], ps[:, 6, :]).then_inc(sem("xeT_ready"), 1)
            np_ = dve.value_load(npass[0:1, 0:1], min_val=1, max_val=PASSES)
            with dve.Fori(0, np_) as q_:
                with dve.Fori(0, E) as e:
                    it = dve.snap(q_ * E + e)
                    dve.wait_ge(sem("GT_ready"), it + 1)
                    for i in range(NT):
                        v.tensor_scalar(selg[:, i, :], iota[:, :], postv[i][:, bass.ds(it, 1)], gate[:, i, bass.ds(e, 1)],
                                        ALU.is_equal, ALU.mult).then_inc(sem("selg_ready"), 1)
                    dve.wait_ge(sem("xe_filled"), it + 1)
                    for i in range(NT):
                        v.tensor_scalar(sel[:, i, :], iota[:, 0:BLK], postv[i][:, bass.ds(it + 1, 1)], None, ALU.is_equal)\
                            .then_inc(sem("sel_ready"), 1)
                    dve.wait_ge(sem("hid_filled"), it + 1)
                    v.tensor_scalar(gg[:, :], ps[:, 4, :], 7.0, None, ALU.min).then_inc(sem("gate_ready"), 1)
                    v.tensor_scalar(ll[:, :], ps[:, 5, :], 7.0, -7.0, ALU.min, ALU.max).then_inc(sem("lin_read"), 1)
                    v.tensor_copy(onehot[0:E, :], identE[:, bass.ds(e + 1, 1)].to_broadcast([E, BLK])).then_inc(sem("onehot_ready"), 1)
                    dve.wait_ge(sem("lin_read"), it + 2)
                    dve.wait_ge(sem("gate_ready"), it + 1)
                    v.scalar_tensor_tensor(out=ll[:, :], in0=ll[:, :], scalar=1.0, in1=gg[:, :], op0=ALU.add, op1=ALU.mult)\
                        .then_inc(sem("swi_step"), 1)
                    dve.wait_ge(sem("swi_step"), it + 1)
                    dve.wait_ge(sem("sig_ready"), it + 1)
                    v.tensor_tensor(ac[:, :], ll[:, :], sg[:, :], ALU.mult).then_inc(sem("ac_ready"), 1)
                    dve.wait_ge(sem("xeT_filled"), it + 2)
                    v.tensor_copy(xeT[:, :], ps[:, 6, :]).then_inc(sem("xeT_ready"), 1)
                    dve.wait_ge(sem("yy_filled"), it + 1)
                    v.tensor_copy(yy[:, :], ps[:, 7, :]).then_inc(sem("yy_ready"), 1)
            dve.wait_ge(sem("sum_ready"), 1)
            for i in range(NT):
                for c in range(2):
                    hv = h[:, i, c * 512:(c + 1) * 512]
                    link(v.tensor_tensor(hv, ps[:, 2 * i + c, :], hv, ALU.add))
            dve.sem_inc(sem("h_ready"), 1)
            dve.wait_ge(sem("stat_ready"), 5)
            rstd(32, 34, D, EPS)
            dve.wait_ge(sem("fing_in"), 16)
            for i in range(NT):
                v.scalar_tensor_tensor(out=x3[:, i, :], in0=h[:, i, :], scalar=st[:, 32 + i:33 + i], in1=fing[:, :],
                                       op0=ALU.mult, op1=ALU.mult).then_inc(sem("y_ready"), 1)


_INS = ["x", "mem", "norm1_g", "w_in", "mu_shift", "w0", "w2", "a0", "a2", "g2", "k_k", "k_a", "r_k", "lnx_g", "lnx_b",
        "lam_q1", "lam_k1", "lam_q2", "lam_k2", "subln_g", "w_out", "norm2_g", "mem_norm_g", "wq_x", "wkv_x", "wo_x",
        "norm3_g", "router_w", "router_b", "moe_w1", "moe_b1", "moe_w2", "moe_b2", "final_g"]


def kernel(**inputs):
    import numpy as _np
    import concourse.bacc as _bacc
    from concourse import mybir as _mybir
    from concourse.bass_utils import run_bass_kernel_spmd as _run

    nc = _bacc.Bacc("TRN2", target_bir_lowering=False, num_devices=1)
    arrays, aps = {}, {}
    for name in _INS:
        v = _np.ascontiguousarray(inputs[name])
        arrays[f"in_{name}"] = v
        aps[name] = nc.dram_tensor(f"in_{name}", v.shape, _mybir.dt.from_np(v.dtype), kind="ExternalInput").ap()
    out = nc.dram_tensor("out_0", (1, T, D), F32, kind="ExternalOutput").ap()
    program(nc, aps, out)
    r = _run(nc, [arrays], core_ids=[0])
    return r.results[0]["out_0"]
```

```python
import itertools
from contextlib import ExitStack

import concourse.bass as bass
from concourse import mybir

F32 = mybir.dt.float32
I32 = mybir.dt.int32
U32 = mybir.dt.uint32
ALU = mybir.AluOpType
ACT = mybir.ActivationFunctionType
AX = mybir.AxisListType

P = 128
T = 256
NT = T // P
D = 1024
KC = D // P
RW = 512
NH = 8
NP = NH // 2
HD = 64
SHIFT = 3 * RW + 64 + 64 + 128
DH = 4
XH = 4
E = 32
CH = 32
NCH = T // CH
SUB = 16
F = 1024
TOPK = 4
EPS = 1e-5
GN_EPS = 64e-5
LAMBDA_INIT = 0.8 - 0.6
XSCALE = (D // XH) ** -0.5
DSCALE = 64 ** -0.5
NEG_EXP_HALF = -0.6065306597126334
SLOT = 2048
RING = 12
PRE = 3
HEAD = 5
WCOL = 256
BLK = 64
PASSES = T // BLK

ROWS = [("norm1_g", KC), ("mu_shift", SHIFT // P), ("w0", 4), ("a0", 4), ("k_k", 4), ("k_a", 4), ("r_k", 4),
        ("lnx_g", 4), ("lnx_b", 4), ("norm2_g", KC), ("mem_norm_g", KC), ("norm3_g", KC), ("subln_g", 1)]
ROW = {}
NROWS = 0
for _name, _n in ROWS:
    ROW[_name] = NROWS
    NROWS += _n

PRE_CHUNKS = {}
for _w, _m, _ns in (("in", "w_in", (2, 3, 6, 0, 1, 4, 5, 7, 8, 9, 10, 11, 12)), ("kv", "wkv_x", (0, 1, 2, 3, 4, 5)),
                    ("out", "w_out", range(4)), ("kv", "wkv_x", (6,)), ("wq", "wq_x", range(4)), ("kv", "wkv_x", (7,)),
                    ("wo", "wo_x", range(4))):
    for _n in _ns:
        PRE_CHUNKS[f"{_w}{_n}"] = (_m, _n * WCOL)
ORDER = list(PRE_CHUNKS)


def program(nc, a, out):
    with ExitStack() as ctx:
        def sb(name, shape, dt=F32):
            return ctx.enter_context(nc.sbuf_tensor(name, shape, dt))

        sems = {}

        def sem(name):
            if name not in sems:
                sems[name] = ctx.enter_context(nc.semaphore(name))
            return sems[name]

        ring = sb("ring", [P, RING, SLOT])
        NF = 25088
        arena = sb("arena", [P, NF])
        ps = ctx.enter_context(nc.psum_tensor("ps", [P, 8, 512], F32))

        def cut(at, *shape):
            n = 1
            for s in shape:
                n *= s
            assert at + n <= NF
            v = arena[:, at:at + n]
            if len(shape) == 2:
                v = v.rearrange("p (a b) -> p a b", a=shape[0])
            if len(shape) == 3:
                v = v.rearrange("p (a b c) -> p a b c", a=shape[0], b=shape[1])
            if len(shape) == 4:
                v = v.rearrange("p (a b c d) -> p a b c d", a=shape[0], b=shape[1], c=shape[2])
            return v

        def side(slot, *shape):
            v = ring[:, slot:RING, :].rearrange("p a b -> p (a b)")
            n = 1
            for s in shape:
                n *= s
            v = v[:, 0:n]
            if len(shape) == 2:
                v = v.rearrange("p (a b) -> p a b", a=shape[0])
            if len(shape) == 3:
                v = v.rearrange("p (a b c) -> p a b c", a=shape[0], b=shape[1])
            if len(shape) == 4:
                v = v.rearrange("p (a b c d) -> p a b c d", a=shape[0], b=shape[1], c=shape[2])
            return v

        H0, XT0, E0, P0, AR0, BT0, KT0, BK0, GT0, QD0 = 0, 2048, 4096, 11264, 14848, 16896, 17920, 18944, 20992, 22016
        h = cut(H0, NT, D)
        xT = cut(XT0, KC, T)
        lw, cs, aa, kk, t1, t2 = (cut(E0 + 1024 * n, NP, T) for n in range(6))
        t3 = cut(QD0 + 2048, NP, T)
        pT = cut(P0, SHIFT // P, T)
        rT, kT, vT = (pT[:, 4 * n:4 * n + 4, :] for n in range(3))
        AR = cut(AR0, NP, NT, 2, P)
        BT, KT = cut(BT0, NP, T), cut(KT0, NP, T)
        Bd, Kd = cut(BK0, NP, T), cut(BK0 + 1024, NP, T)
        xs = cut(BK0, NT, D)
        gT = cut(GT0, NP, T)
        qd, kd = cut(QD0, DH, T), cut(QD0 + 1024, DH, T)
        vd = cut(QD0 + 2048, NT, RW)
        Zr = cut(E0, NT, NH, 2 * HD)
        Vn, Bn, Kn = (cut(E0 + 2048 + 1024 * n, NT, RW) for n in range(3))
        Zf = cut(E0 + 5120, NT, NH, 2 * HD)
        LGMH = side(4, NT, NH, 4 * P)
        XTb = side(8, NT, NH, P)
        Z1 = side(9, NT, NH, P)
        Lsb = side(9, NT, NH, P)
        Z2 = cut(BK0, NT, NH, P)
        PhiPsi = side(8, NCH, NP, 2 * HD)
        kmT = side(10, KC, T)
        memT = side(3, KC, T)
        memN = side(4, NT, D)
        vm = side(11, NT, D)
        soft = [cut(XT0 + 1024, 2, 512)] * 2 + [side(11, 2, 2, 512)[:, 1]]
        St = cut(BK0, NCH, NP, HD)
        RhT = cut(BT0, NP, T)
        Y0 = cut(KT0, NT, RW)
        Yn = cut(P0 + 1024, NT, RW)
        prow = cut(GT0, P)[0:NROWS, :]
        lamv = cut(GT0 + 256, 4, HD)
        lora = cut(QD0 + 2048, RW)
        g2s = cut(QD0 + 2560, RW)
        atT = [cut(P0 + 2048 + 512 * n, 512) for n in range(2)]
        L16, X16, w16 = (cut(E0 + 5120 + 256 * n, SUB, SUB) for n in range(3))
        rk = cut(E0 + 6144, NP, T)
        krs, kra, krb = (cut(KT0 + 256 * n, T) for n in range(3))
        odn = cut(XT0, NT, RW)
        dsq = cut(P0 + 3072, 512)
        osq = side(11, P)
        squares = cut(P0, D)
        sd = cut(P0 + 3072, NP, HD)
        bv = rT
        qx = cut(E0, KC, T)
        x2T = cut(E0 + 2048, KC, T)
        oT = cut(E0 + 2048, KC, T)
        px = [cut(P0 + 1024 * n, 2, 2, T) for n in range(XH // 2)]
        pxT = [cut(AR0 + 1024 * n, NT, 2, T) for n in range(XH // 2)]
        x3T = cut(E0, KC, T)
        lg = cut(E0 + 2048, NT, E)
        rt = cut(E0 + 2112, 64)
        picks = cut(E0 + 2176, NT, TOPK, E)
        queue = cut(E0 + 2432, NT, E)
        b1a = cut(E0 + 2560, 512)
        b2a = cut(E0 + 6144, D)
        fing = cut(E0 + 3072, D)
        M0 = P0
        xe, xeT, gg, sg, ll, ac, acT, yy = (cut(M0 + 512 * n, 512) for n in range(8))
        sel = cut(M0 + 4096, NT, BLK)
        selg = cut(M0 + 4224, NT, P)
        GT = cut(M0 + 4480, T)
        onehot = cut(M0 + 4736, BLK)
        post = cut(M0 + 4800, NT, PASSES + 1, E)
        gate = cut(M0 + 5120, NT, E)
        mask = cut(M0 + 5184, NT, E)
        gateT = cut(M0 + 5248, T)
        w1_odd = [cut(XT0, SLOT), cut(E0 + 4096, SLOT), cut(E0, SLOT)]
        w2_odd = cut(BT0, KC // 2, SLOT)

        ident = sb("ident", [P, P])
        masks = sb("masks", [P, 4, P])
        onesbd = sb("onesbd", [P, P])
        keep = sb("keep", [P, T])
        iota = sb("iota", [P, P])
        iotaE = sb("iotaE", [P, E])
        tri = sb("tri", [P, P])
        ones = sb("ones", [P, P])
        hsel = sb("hsel", [P, NP, NH])
        hselT = sb("hselT", [NH, NP, P])
        identE = sb("identE", [P, E + 1])
        prm = sb("prm", [P, NROWS])
        rws = sb("rws", [P, KC, E])
        rbs = sb("rbs", [P, E])
        mu1 = sb("mu1", [P, SHIFT // P])
        w0h = sb("w0h", [P, 8])
        tail = sb("tail", [P, NP, NCH])
        dec = sb("dec", [P, NP, NCH])
        st = sb("st", [P, 64])
        lam = sb("lam", [P, 8])
        dst_ = sb("dst_", [P, 64])
        xst = sb("xst", [P, 32])
        wk = sb("wk", [P, 64])
        ix8 = sb("ix8", [P, NT, 8], U32)
        npass = sb("npass", [1, 1], I32)

        blocks = nc.dram_tensor("blocks", (2, P // SUB, NT * NH, SUB, SUB), F32, kind="Internal").ap()

        filled = [sem(f"bank{b}_filled") for b in range(8)]
        drained = [sem(f"bank{b}_drained") for b in range(8)]
        where, count = {}, [0] * 8

        def place(name, bank):
            assert name not in where
            count[bank] += 1
            where[name] = (bank, count[bank])

        def chunk(label, bank=None):
            place(label, ORDER.index(label) % 2 if bank is None else bank)

        for n in range(4):
            place(f"xT{n}", 2 + n)
        place("prm", 6)
        chunk("in2")
        chunk("in3")
        for n in range(4):
            place(f"memT{n}", 2 + n)
        chunk("in6")
        chunk("in0")
        place("ksum", 6)
        chunk("in1")
        for n in range(2):
            place(f"lw{n}", 2 + n)
            place(f"la{n}", 4 + n)
            place(f"lg{n}", 6 + n)
        chunk("in4")
        for n in range(2):
            place(f"kb{n}", 2 + n)
        for n in (5, 7, 8, 9, 10):
            chunk(f"in{n}")
        for i in range(NT):
            place(f"L{i}0", 6)
            place(f"L{i}1", 7)
        for i in range(NT):
            for q in range(4):
                place(f"nat{i}{q}", 2 + q)
        for n in range(NH):
            place(f"LGMH0{n}", 2 + n % 4)
        chunk("in11")
        chunk("in12")
        chunk("kv0")
        for n in range(NH):
            place(f"LGMH1{n}", 2 + n % 4)
        for n in range(2):
            place(f"bo{n}", 4 + n)
        for i in range(NT):
            place(f"MV{i}", 6 + i)
        UNITS = [(0, (0, 1, 2, 3)), (1, (0, 1)), (1, (2, 3))]
        for g in range(4):
            place(f"z1{g}", 2 + g)
        place("sc00", 0)
        place("sc01", 1)
        for nm in ("z2", "z3"):
            for g in range(4):
                place(f"{nm}{g}", 2 + g)
        for i in range(NT):
            place(f"Rh{i}", 6)
            place(f"yz{i}", 7)
        place("at0", 2)
        place("od0", 3)
        place("sc10", 0)
        place("sc11", 1)
        for c in range(NCH - 1):
            place(f"PP{c}", (4, 5, 6, 7)[c % 4])
        place("sc20", 0)
        place("sc21", 1)
        place("at1", 2)
        place("od1", 3)
        place("at2", 3)
        place("od2", 2)
        for i in range(NT):
            place(f"Y{i}0", 0)
            place(f"Y{i}1", 1)
            for c in range(4 * i, min(4 * i + 4, NCH - 1)):
                if c:
                    place(f"S{c}0", 6)
                    place(f"S{c}1", 7)
        chunk("kv1", 4)
        chunk("kv2", 5)
        for i in range(NT):
            place(f"odT{i}", 2 + i)
        chunk("kv3")
        chunk("kv4")
        chunk("kv5")
        for i in range(NT):
            place(f"ynT{i}", 2 + i)
        for n in range(4):
            chunk(f"out{n}")
        chunk("kv6")
        for n in range(4):
            place(f"h1T{n}", 2 + n)
        for n in range(4):
            chunk(f"wq{n}")
        for n in range(XH // 2):
            for i in range(NT):
                place(f"xs{n}{i}", 2 + 2 * n + i)
        chunk("kv7")
        for n in range(XH // 2):
            for i in range(NT):
                place(f"xp{n}{i}", (6, 4)[n] + i)
        for n in range(XH // 2):
            for m in range(2):
                place(f"xo{n}{m}", (2, 6)[n] + m)
        for n in range(4):
            chunk(f"wo{n}")
        for n in range(4):
            place(f"h2T{n}", 2 + n)
        place("logit0", 6)
        place("logit1", 7)
        place("pos", 7)
        place("gateT", 6)

        def begin(pe, name):
            b, k = where[name]
            if k > 1:
                pe.wait_ge(drained[b], k - 1)
            return ps[:, b, :]

        def done(ins, name):
            ins.then_inc(filled[where[name][0]], 1)

        def product(eng, name):
            b, k = where[name]
            eng.wait_ge(filled[b], k)
            return ps[:, b, :]

        def drain(ins, name):
            ins.then_inc(drained[where[name][0]], 1)

        def taken(eng, name):
            b, k = where[name]
            eng.wait_ge(drained[b], k)

        landed = [sem(f"slot{s}_landed") for s in range(PRE)]
        elanded = [sem(f"w1_chunk{c}_landed") for c in range(8)]
        elanded_odd = [sem(f"w1_odd_chunk{c}_landed") for c in range(HEAD, KC)]
        landed2 = [[sem(f"w2_{nm}_chunk{j}_landed") for j in range(4)] for nm in ("even", "odd")]
        eused = sem("expert_chunks_used")

        def w1_place(par, k):
            if par and k >= HEAD:
                return w1_odd[k - HEAD], elanded_odd[k - HEAD]
            return ring[:, k, :], elanded[k]

        mats = {n: a[n][0] for n in ("wkv_x", "w_in", "w_out", "wq_x", "wo_x")}

        def gbc(name, n0, n):
            r = ROW[name] + n0
            return prm[:, r:r + n].unsqueeze(2).to_broadcast([P, n, P])

        def rows_dma(eng, rows):
            for name, n in rows:
                src = a[name]
                src = src[0].rearrange("h n -> (h n)") if name == "r_k" else src[0]
                eng.dma_start(prow[ROW[name]:ROW[name] + n, :], src.rearrange("(r p) -> r p", p=P)).then_inc(sem("rows_in"), 16)

        block = ctx.enter_context(nc.Block())

        @block.sync
        def _(sp):
            for i in range(NT):
                sp.dma_start(h[:, i, :], a["x"][0, i * P:(i + 1) * P, :]).then_inc(sem(f"x{i}_in"), 16)
            rows_dma(sp, ROWS[7:])

            def w1_chunk(e, par, k, from1=False):
                dst, landed_ = w1_place(par, k)
                sp.dma_start(dst, w1v1[k, e - 1] if from1 else w1v[k, e]).then_inc(landed_, 16)

            def w2_chunk(e, par, j):
                dst = (w2_odd[:, j, :] if par else ring[:, 8 + j, :]).rearrange("p (j n) -> p j n", j=2)
                sp.dma_start(dst, w2v[j, e]).then_inc(landed2[par][j], 16)

            def w1_head(e, it, par, from1=False):
                for k in range(HEAD):
                    sp.wait_ge(eused, (it - 1) * 12 + k + 1)
                    w1_chunk(e, par, k, from1)

            def w1_tail(e, it, par):
                for k in range(HEAD, KC):
                    sp.wait_ge(eused, (it - 2) * 12 + k + 1)
                    w1_chunk(e, par, k)

            def w2(e, it, par):
                for j in range(4):
                    sp.wait_ge(eused, (it - 2) * 12 + KC + j + 1)
                    w2_chunk(e, par, j)

            w1v1 = a["moe_w1"][0][1:E].rearrange("e (c p) n -> c e p n", p=P)
            w1v = a["moe_w1"][0].rearrange("e (c p) n -> c e p n", p=P)
            w2v = a["moe_w2"][0].rearrange("e (c j p) n -> c e p j n", p=P, j=2)
            early = ([lambda k=k: w1_chunk(0, 0, k) for k in range(PRE + 1, KC)] + [lambda j=j: w2_chunk(0, 0, j) for j in range(2)]
                     + [lambda j=j: w2_chunk(1, 1, j) for j in range(4)] + [lambda k=k: w1_chunk(1, 1, k) for k in (HEAD, HEAD + 1)])
            for n, (w, c0) in enumerate(PRE_CHUNKS.values()):
                if n >= PRE:
                    product(sp, ORDER[n - PRE])
                sp.dma_start(ring[:, n % PRE, :].rearrange("p (k n) -> p k n", k=KC),
                             mats[w][:, c0:c0 + WCOL].rearrange("(k p) n -> p k n", p=P)).then_inc(landed[n % PRE], 16)
                if n == 1:
                    sp.dma_start(memN[:, :, :], a["mem"][0].rearrange("(i p) d -> p i d", p=P)).then_inc(sem("mem_in"), 16)
                if n == 2:
                    sp.dma_start(lora[0:64, :], a["w2"][0]).then_inc(sem("lora_in"), 16)
                    sp.dma_start(lora[64:128, :], a["a2"][0]).then_inc(sem("lora_in"), 16)
                    sp.dma_start(g2s[:, :], a["g2"][0]).then_inc(sem("lora_in"), 16)
                    sp.dma_start(rws[:, :, :], a["router_w"][0].rearrange("(k p) e -> p k e", p=P)).then_inc(sem("router_in"), 16)
                    sp.dma_start(rbs[:, :], a["router_b"].to_broadcast([P, E])).then_inc(sem("router_in"), 16)
                    for m, name in enumerate(("lam_q1", "lam_k1", "lam_q2", "lam_k2")):
                        sp.dma_start(lamv[:, m, :], a[name].to_broadcast([P, HD])).then_inc(sem("lam_in"), 16)
                if n >= ORDER.index("out0") + PRE and early:
                    if n == ORDER.index("out0") + PRE:
                        sp.wait_ge(sem("mixers_through"), 1)
                        sp.wait_ge(sem("yT_ready"), NT)
                    for _ in range(2):
                        if len(early) == 2:
                            product(sp, "out3")
                        early.pop(0)()
            assert not early
            sp.dma_start(b2a[0:E, :], a["moe_b2"][0]).then_inc(sem("b2_in"), 16)
            product(sp, "kv7")
            w1_chunk(0, 0, PRE)
            sp.wait_ge(sem("cross_through"), 1)
            for j in range(2, 4):
                w2_chunk(0, 0, j)
            for c in range(PRE):
                product(sp, ORDER[len(ORDER) - PRE + c])
                w1_chunk(0, 0, (len(ORDER) - PRE + c) % PRE)
            for g in range(4):
                sp.dma_start(b1a[g * E:(g + 1) * E, :], a["moe_b1"][0][:, g * 512:(g + 1) * 512]).then_inc(sem("b1_in"), 16)
            sp.dma_start(fing[:, :], a["final_g"].unsqueeze(0).to_broadcast([P, D])).then_inc(sem("fing_in"), 16)
            product(sp, "logit1")
            w1_chunk(1, 1, KC - 1)
            with sp.Fori(0, (E - 4) // 2) as r:
                for n in (1, 2):
                    w1_head(2 * r + n, 2 * r + n, n % 2, True)
                    after = sp.snap(2 * r + (n + 1))
                    w1_tail(after, after, 1 - n % 2)
                    w2(after, after, 1 - n % 2)
            w1_head(E - 3, E - 3, 1)
            w1_tail(E - 2, E - 2, 0)
            w2(E - 2, E - 2, 0)
            w1_head(E - 2, E - 2, 0)
            w1_tail(E - 1, E - 1, 1)
            w1_head(E - 1, E - 1, 1)
            w2(E - 1, E - 1, 1)
            sp.wait_ge(sem("npass_ready"), 1)
            np_ = sp.value_load(npass[0:1, 0:1], min_val=1, max_val=PASSES)
            with sp.If(np_ > 1):
                with sp.Fori(1, np_) as q:
                    with sp.Fori(0, E // 2) as r:
                        for par in range(2):
                            w1_head(2 * r + par, q * E + 2 * r + par, par)
                            w1_tail(2 * r + par, q * E + 2 * r + par, par)
                            w2(2 * r + par, q * E + 2 * r + par, par)
            for i in range(NT):
                for c in range(2):
                    sp.wait_ge(sem("y_ready"), 2 * i + c + 1)
                    sp.dma_start(out[0, i * P:(i + 1) * P, c * 512:(c + 1) * 512], h[:, i, c * 512:(c + 1) * 512])\
                      .then_inc(sem("out_written"), 16)
            sp.wait_ge(sem("out_written"), 64)

        @block.gpsimd
        def _(pool):
            g = nc.gpsimd
            n = [0]

            def link(ins):
                n[0] += 1
                ins.then_inc(sem("pool_step"), 1)
                pool.wait_ge(sem("pool_step"), n[0])

            link(g.memset(ident[:, :], 0.0))
            link(g.affine_select(out=ident[:, :], in_=ident[:, :], compare_op=ALU.not_equal, fill=1.0, base=0,
                                 pattern=[[-1, P]], channel_multiplier=1))
            pool.sem_inc(sem("ident_ready"), 1)
            g.memset(ones[:, :], 1.0).then_inc(sem("ones_ready"), 1)
            link(g.memset(onesbd[:, :], 1.0))
            link(g.affine_select(out=onesbd[:, 0:HD], in_=onesbd[:, 0:HD], compare_op=ALU.is_ge, fill=0.0, base=HD - 1,
                                 pattern=[[0, HD]], channel_multiplier=-1))
            link(g.affine_select(out=onesbd[:, HD:P], in_=onesbd[:, HD:P], compare_op=ALU.is_ge, fill=0.0, base=-HD,
                                 pattern=[[0, HD]], channel_multiplier=1))
            link(g.memset(keep[:, :], 1.0))
            link(g.memset(keep[:, 0:T:CH], 0.0))
            link(g.memset(masks[:, :, :], 1.0))
            for m in range(4):
                v = masks[:, m, :].rearrange("p (c t) -> p c t", t=CH)
                link(g.affine_select(out=v, in_=v, compare_op=ALU.is_ge, fill=0.0, base=0,
                                     pattern=[[-CH, P // CH], [0, CH]], channel_multiplier=1))
                link(g.affine_select(out=v, in_=v, compare_op=ALU.is_ge, fill=0.0, base=CH - 1 if m else SUB - 1,
                                     pattern=[[CH, P // CH], [0, CH]], channel_multiplier=-1))
                if m:
                    w = masks[:, m, :]
                    link(g.affine_select(out=w, in_=w, compare_op=ALU.is_ge, fill=0.0, base=-1 if m == 2 else 0,
                                         pattern=[[1, P]], channel_multiplier=-1))
                else:
                    link(g.affine_select(out=v, in_=v, compare_op=ALU.is_ge, fill=0.0, base=-SUB,
                                         pattern=[[0, P // CH], [1, CH]], channel_multiplier=0))
            link(g.memset(tri[:, :], 1.0))
            link(g.affine_select(out=tri[:, :], in_=tri[:, :], compare_op=ALU.is_ge, fill=0.0, base=-1,
                                 pattern=[[1, P]], channel_multiplier=-1))
            link(g.iota(iota[:, :].rearrange("p (a b) -> p a b", a=2), [[0, 2], [1, BLK]], base=0, channel_multiplier=0,
                        allow_small_or_imprecise_dtypes=True))
            link(g.iota(iotaE[:, :], [[1, E]], base=0, channel_multiplier=0, allow_small_or_imprecise_dtypes=True))
            link(g.memset(hsel[:, :, :], 0.0))
            for j in range(NP):
                link(g.memset(hsel[0:HD, j, 2 * j:2 * j + 1], 1.0))
                link(g.memset(hsel[HD:P, j, 2 * j + 1:2 * j + 2], 1.0))
            link(g.memset(hselT[:, :, :], 0.0))
            hv = hselT[:, :, :].rearrange("p j (q c) -> p j q c", q=2)
            link(g.affine_select(out=hv, in_=hv, compare_op=ALU.not_equal, fill=1.0, base=0,
                                 pattern=[[-2, NP], [-1, 2], [0, HD]], channel_multiplier=1))
            link(g.memset(identE[:, :], 0.0))
            for q in range(4):
                link(g.affine_select(out=identE[:, 0:E], in_=identE[:, 0:E], compare_op=ALU.not_equal, fill=1.0, base=-q * E,
                                     pattern=[[-1, E]], channel_multiplier=1))
                link(g.affine_select(out=identE[:, E:E + 1], in_=identE[:, E:E + 1], compare_op=ALU.not_equal, fill=1.0, base=-q * E,
                                     pattern=[[0, 1]], channel_multiplier=1))
            link(g.memset(XTb[:, :, :, :], 0.0))
            pool.sem_inc(sem("const_ready"), 1)

            product(pool, "ksum")
            link(g.memset(X16[:, :, :], 0.0))
            g.affine_select(out=X16[:, :, :], in_=X16[:, :, :], compare_op=ALU.not_equal, fill=1.0, base=0,
                            pattern=[[1, SUB], [-1, SUB]], channel_multiplier=0).then_inc(sem("X16_unit"), 1)

        @block.scalar
        def _(act):
            s = nc.scalar
            n = [0]

            def link(ins):
                n[0] += 1
                ins.then_inc(sem("act_step"), 1)
                act.wait_ge(sem("act_step"), n[0])

            rows_dma(act, ROWS[0:7])

            def sumsq(src, col):
                for i in range(NT):
                    link(s.activation(squares[:, :], src[:, i, :], ACT.Square, accum_out=st[:, col + i:col + i + 1]))
                act.sem_inc(sem("stat_ready"), 1)

            act.wait_ge(sem("ones_ready"), 1)
            link(s.activation(st[:, 63:64], ones[:, 0:1], ACT.Square))
            for i in range(NT):
                act.wait_ge(sem(f"x{i}_in"), 16)
                link(s.activation(squares[:, :], h[:, i, :], ACT.Square, accum_out=st[:, 2 + i:3 + i]))
                act.sem_inc(sem("x_stat_ready"), 1)
            act.wait_ge(sem("mem_in"), 16)
            sumsq(memN, 0)

            def copy(dst, name, view=None):
                src = product(act, name)
                drain(s.activation(dst, view(src) if view else src, ACT.Copy), name)

            two = lambda v: v.rearrange("p (a b) -> p a b", a=2)

            def unshifted(m):
                src = two(product(act, f"in{m}"))
                for q in range(2):
                    j = 2 * m + q
                    s.activation(pT[:, j, :], src[:, q, :], ACT.Identity, scale=mu1[:, j:j + 1]).then_inc(sem("unshifted_ready"), 1)

            act.wait_ge(sem("mu_ready"), 1)
            for m in (2, 3, 6):
                unshifted(m)
            act.wait_ge(sem("shifted_ready"), 3)
            s.activation(pT[0:64, 12, :], pT[0:64, 12, :], ACT.Tanh).then_inc(sem("lora_x_ready"), 1)
            s.activation(pT[:, 13, :], pT[:, 13, :], ACT.Tanh, scale=0.5).then_inc(sem("gd_tanh_ready"), 1)
            unshifted(0)
            unshifted(1)
            for m in range(2):
                for (z, dst, b0) in (("lw", lw, 0), ("la", aa, 4)):
                    src = two(product(act, f"{z}{m}"))
                    for q in range(2):
                        j = 2 * m + q
                        ins = s.activation(dst[:, j, :], src[:, q, :], ACT.Tanh, bias=w0h[:, b0 + j:b0 + j + 1], scale=0.5)
                        if q == 0:
                            link(ins)
                    drain(ins, f"{z}{m}")
                act.wait_ge(sem("lam_sum_ready"), 1)
                copy(gT[:, 2 * m:2 * m + 2, :], f"lg{m}", two)
            unshifted(4)
            act.wait_ge(sem("cs_ready"), 1)
            s.activation(t1[:, :, :], cs[:, :, :], ACT.Exp).then_inc(sem("exp_ready"), 1)
            s.activation(dec[:, :, :], tail[:, :, :], ACT.Exp).then_inc(sem("exp_ready"), 1)
            act.wait_ge(sem("ex_ready"), 1)
            s.activation(lw[:, :, :], lw[:, :, :], ACT.Exp).then_inc(sem("exp_ready"), 1)
            unshifted(5)
            act.wait_ge(sem("t1_free"), 1)
            s.activation(t1[:, :, :], cs[:, :, :], ACT.Exp, scale=-1.0).then_inc(sem("exp_ready"), 1)
            act.wait_ge(sem("rest_ready"), 1)
            s.activation(t3[:, :, :], t3[:, :, :], ACT.Exp).then_inc(sem("exp_ready"), 1)
            for m in range(2):
                copy(qd[:, 2 * m:2 * m + 2, :], f"in{7 + m}", two)
            for m in range(2):
                copy(kd[:, 2 * m:2 * m + 2, :], f"in{9 + m}", two)
            for i in range(NT):
                for q in range(2):
                    copy(Lsb[:, i, q:NH:2, :], f"L{i}{q}", lambda v: v.rearrange("p (h k) -> p h k", h=NP))
                    taken(act, f"L{i}{q}")
            for j in range(P // SUB):
                act.dma_start(blocks[0, j].rearrange("q a b -> a q b"),
                              Lsb[SUB * j:SUB * j + SUB, :, :, SUB * j:SUB * j + SUB].rearrange("a i h b -> a (i h) b"))\
                   .then_inc(sem("L_blocks_out"), 16)
            for i in range(NT):
                copy(Zr[:, i, :, 0:HD], f"nat{i}0", lambda v: v.rearrange("p (h k) -> p h k", h=NH))
                copy(Vn[:, i, :], f"nat{i}1")
            act.wait_ge(sem("L_blocks_out"), 16 * (P // SUB))
            act.dma_start(L16[:, :, :], blocks[0].rearrange("j q a b -> (j q) a b")).then_inc(sem("L16_in"), 16)
            act.wait_ge(sem("t3_free"), 1)
            for m in range(2):
                copy(vd[:, :, m * WCOL:(m + 1) * WCOL], f"in{11 + m}", two)

            act.wait_ge(sem("X16_ready"), 1)
            act.wait_ge(sem("const_ready"), 1)
            act.dma_start(blocks[1].rearrange("j q a b -> (j q) a b"), X16[:, :, :]).then_inc(sem("X_blocks_out"), 16)
            act.wait_ge(sem("X_blocks_out"), 16)
            for j in range(P // SUB):
                act.dma_start(XTb[SUB * j:SUB * j + SUB, :, :, SUB * j:SUB * j + SUB].rearrange("c i h a -> c (i h) a"),
                              blocks[1, j].rearrange("q c a -> c q a")).then_inc(sem("XT_in"), 16)
            copy(kmT[:, 0:2, :], "kv0", two)
            for i in range(NT):
                copy(Zr[:, i, :, HD:P], f"MV{i}", lambda v: v.rearrange("p (h k) -> p h k", h=NH))
            four = lambda v: v.rearrange("p (h k) -> p h k", h=4)
            for q in range(4):
                copy(Z1[:, q // 2, 4 * (q % 2):4 * (q % 2) + 4, :], f"z1{q}", four)

            def exps(u):
                i, heads = UNITS[u]
                act.wait_ge(sem("dmax_ready"), u + 1)
                w = P * (i + 1)
                if u == 1:
                    product(act, "at0")
                for c in range(2):
                    src = ps[:, where[f"sc{u}{c}"][0], :]
                    for m, hh in enumerate(heads):
                        col = 8 * u + 4 * c + m
                        ins = s.activation(soft[u][:, c, m * w:(m + 1) * w], src[:, m * w:(m + 1) * w], ACT.Exp, scale=DSCALE,
                                           bias=dst_[:, col:col + 1], accum_out=dst_[:, 32 + col:33 + col])
                        if m < len(heads) - 1:
                            link(ins)
                    drain(ins, f"sc{u}{c}")
                    taken(act, f"sc{u}{c}")
                act.sem_inc(sem("dexp_ready"), 1)

            def head_outputs(u):
                i, heads = UNITS[u]
                n0, nh = heads[0], len(heads)
                copy(odn[:, i, n0 * P:(n0 + nh) * P], f"od{u}", lambda v: v[:, 0:nh * P])
                taken(act, f"od{u}")
                for hh in heads:
                    link(s.activation(osq[:, :], odn[:, i, hh * P:(hh + 1) * P], ACT.Square,
                                      accum_out=st[:, 8 + 4 * i + hh:9 + 4 * i + hh]))

            for q in range(4):
                copy(Z2[:, q // 2, 4 * (q % 2):4 * (q % 2) + 4, :], f"z2{q}", four)
            act.wait_ge(sem("lam_sum_ready"), 1)
            s.activation(lam[:, 2:4], lam[:, 0:2], ACT.Exp).then_inc(sem("lam_exp_ready"), 1)
            exps(0)
            for i in range(NT):
                copy(Y0[:, i, :], f"yz{i}")
            taken(act, "bo1")
            copy(atT[0][:, :], "at0")
            exps(1)
            head_outputs(0)
            for c in range(4):
                copy(PhiPsi[:, c, :, :], f"PP{c}", four)
            exps(2)
            for c in range(4, NCH - 1):
                copy(PhiPsi[:, c, :, :], f"PP{c}", four)
            copy(atT[1][:, :], "at1")
            head_outputs(1)
            copy(atT[0][:, :], "at2")
            head_outputs(2)
            act.sem_inc(sem("osq_ready"), 1)
            act.wait_ge(sem("osr_ready"), 1)
            for i in range(NT):
                for hh in range(DH):
                    link(s.activation(odn[:, i, hh * P:(hh + 1) * P], odn[:, i, hh * P:(hh + 1) * P], ACT.Copy,
                                      scale=st[:, 8 + 4 * i + hh:9 + 4 * i + hh]))
            act.sem_inc(sem("odn_ready"), 1)
            copy(kmT[:, 2:4, :], "kv1", two)
            copy(kmT[:, 4:6, :], "kv2", two)
            act.wait_ge(sem("sub_gain_ready"), 1)
            for i in range(NT):
                o = product(act, f"odT{i}")
                drain(s.activation(xT[:, NP:KC, i * P:(i + 1) * P], four(o), ACT.Copy, scale=lam[:, 5:6]), f"odT{i}")
            act.wait_ge(sem("centred_ready"), 1)
            for hh in range(NH):
                link(s.activation(osq[:, 0:HD], Yn[:, 0, hh * HD:(hh + 1) * HD], ACT.Square, accum_out=st[:, 16 + hh:17 + hh]))
            act.sem_inc(sem("ysq_ready"), 1)
            copy(kmT[:, 6:8, :], "kv3", two)
            for m in range(2):
                copy(vm[:, :, m * WCOL:(m + 1) * WCOL], f"kv{4 + m}", two)
            o = four(product(act, "ynT1"))
            for j in range(NP):
                r = ROW["lnx_g"] + j
                ins = s.activation(xT[:, j, P:T], o[:, j, :], ACT.Identity, scale=prm[:, r:r + 1], bias=prm[:, r + 4:r + 5])
                if j < NP - 1:
                    link(ins)
            drain(ins, "ynT1")
            act.wait_ge(sem("h_ready"), 1)
            sumsq(h, 4)
            copy(vm[:, :, 2 * WCOL:3 * WCOL], "kv6", two)
            for m in range(4):
                copy(qx[:, 2 * m:2 * m + 2, :], f"wq{m}", two)
            for m in range(XH // 2):
                for i in range(NT):
                    act.wait_ge(sem("xmax_ready"), 2 * m + i + 1)
                    src = two(ps[:, where[f"xs{m}{i}"][0], :])
                    for q in range(2):
                        col = 4 * m + 2 * i + q
                        ins = s.activation(px[m][:, i, q, :], src[:, q, :], ACT.Exp, scale=st[:, 36 + i:37 + i], bias=xst[:, col:col + 1],
                                           accum_out=xst[:, 8 + col:9 + col])
                        if q == 0:
                            link(ins)
                    drain(ins, f"xs{m}{i}")
            copy(vm[:, :, 3 * WCOL:4 * WCOL], "kv7", two)
            for m in range(XH // 2):
                for q in range(2):
                    copy(oT[:, 4 * m + 2 * q:4 * m + 2 * q + 2, :], f"xo{m}{q}", two)
            act.wait_ge(sem("h_ready"), 2)
            sumsq(h, 6)
            act.wait_ge(sem("top_ready"), 1)
            for i in range(NT):
                s.activation(rt[:, 24 + 4 * i:28 + 4 * i], rt[:, 8 * i:8 * i + 4], ACT.Exp, bias=rt[:, 16 + i:17 + i],
                             accum_out=rt[:, 18 + i:19 + i]).then_inc(sem("gexp_ready"), 1)
            copy(gateT[0:E, :], "gateT", lambda v: v[0:E, 0:T])

            act.wait_ge(sem("npass_ready"), 1)
            act.wait_ge(sem("xe_filled"), 1)
            s.activation(xe[:, :], ps[:, 6, :], ACT.Copy).then_inc(sem("xe_ready"), 1)
            np_ = act.value_load(npass[0:1, 0:1], min_val=1, max_val=PASSES)
            with act.Fori(0, np_) as q:
                with act.Fori(0, E) as e:
                    it = act.snap(q * E + e)
                    act.wait_ge(sem("gate_ready"), it + 1)
                    s.activation(sg[:, :], gg[:, :], ACT.Sigmoid, scale=1.702).then_inc(sem("sig_ready"), 1)
                    act.wait_ge(sem("GT_filled"), it + 1)
                    s.activation(GT[:, :], ps[:, 7, 0:T], ACT.Copy).then_inc(sem("GT_ready"), 1)
                    act.wait_ge(sem("xe_filled"), it + 2)
                    s.activation(xe[:, :], ps[:, 6, :], ACT.Copy).then_inc(sem("xe_ready"), 1)
                    act.wait_ge(sem("acT_filled"), it + 1)
                    s.activation(acT[:, :], ps[:, 7, :], ACT.Copy).then_inc(sem("acT_ready"), 1)
            for i in range(NT):
                act.wait_ge(sem("h_ready"), 3 + i)
                s.activation(cut(P0 + i * D, D), h[:, i, :], ACT.Square, accum_out=st[:, 32 + i:33 + i]).then_inc(sem("out_stat_ready"), 1)

        @block.tensor
        def _(pe):
            t = nc.tensor

            def weights(label):
                n = ORDER.index(label)
                pe.wait_ge(landed[n % PRE], 16 * (n // PRE + 1))
                return ring[:, n % PRE, :].rearrange("p (k n) -> p k n", k=KC)

            def turned_parts(label, src):
                w = weights(label)
                o = begin(pe, label)
                for q in range(2):
                    for k in range(KC):
                        ins = t.matmul(o[:, q * T:(q + 1) * T], w[:, k, q * P:(q + 1) * P], src[:, k, :],
                                       start=(k == 0), stop=(k == KC - 1))
                        if k == KC // 2 - 1:
                            yield
                    if q == 0:
                        yield
                done(ins, label)
                yield

            def turned(label, src):
                for _ in turned_parts(label, src):
                    pass

            def natural(label, src, before=lambda i: None):
                w = weights(label)
                o = begin(pe, label)
                for i in range(NT):
                    before(i)
                    for k in range(KC):
                        ins = t.matmul(o[:, i * WCOL:(i + 1) * WCOL], src[:, k, i * P:(i + 1) * P], w[:, k, :],
                                       start=(k == 0), stop=(k == KC - 1))
                done(ins, label)

            def turn4(name, srcs):
                o = begin(pe, name)
                for q, v in enumerate(srcs):
                    ins = t.transpose(o[:, q * P:(q + 1) * P], v, ident[:, :])
                done(ins, name)

            def turn_half(s, q, src):
                for i in range(NT):
                    turn4(f"{s}T{2 * i + q}", [src[:, i, (4 * q + m) * P:(4 * q + m + 1) * P] for m in range(4)])

            def turn_rows(s, src):
                for i in range(NT):
                    pe.wait_ge(sem(f"{s}_scaled"), i + 1)
                    for q in range(2):
                        turn4(f"{s}T{2 * i + q}", [src[:, i, (4 * q + m) * P:(4 * q + m + 1) * P] for m in range(4)])

            pe.wait_ge(sem("ident_ready"), 1)
            turn_rows("x", xs)
            pe.wait_ge(sem("rows_in"), 16 * len(ROWS))
            o = begin(pe, "prm")
            done(t.transpose(o[:, 0:NROWS], prow[:, :], ident[0:NROWS, 0:NROWS]), "prm")
            for q in range(4):
                taken(pe, f"xT{q}")
            turned("in2", xT)
            turned("in3", xT)
            turn_rows("mem", memN)
            turned("in6", xT)
            turned("in0", xT)
            pe.wait_ge(sem("kksq_ready"), 1)
            pe.wait_ge(sem("const_ready"), 1)
            o = begin(pe, "ksum")
            for j in range(NP):
                ins = t.matmul(o[0:NH, 0:T], hsel[:, j, :], t2[:, j, :], start=(j == 0), stop=(j == NP - 1))
            done(ins, "ksum")
            turned("in1", xT)
            pe.wait_ge(sem("lora_in"), 48)
            pe.wait_ge(sem("lora_x_ready"), 1)
            pe.wait_ge(sem("gd_ready"), 1)
            for m in range(2):
                for nm, lo, hi, lw_, rhs in (("lw", 0, 64, lora, 12), ("la", 64, 128, lora, 12), ("lg", 0, 128, g2s, 13)):
                    o = begin(pe, f"{nm}{m}")
                    for q in range(2):
                        j = 2 * m + q
                        ins = t.matmul(o[:, q * T:(q + 1) * T], lw_[lo:hi, j * P:(j + 1) * P], pT[lo:hi, rhs, :], start=True, stop=True)
                    done(ins, f"{nm}{m}")
            turned("in4", xT)
            pe.wait_ge(sem("knorm_ready"), 1)
            for m in range(2):
                o = begin(pe, f"kb{m}")
                for q in range(2):
                    ins = t.matmul(o[:, q * T:(q + 1) * T], hselT[:, 2 * m + q, :], krs[0:NH, :], start=True, stop=True)
                done(ins, f"kb{m}")
            for m in (5, 7, 8, 9, 10):
                turned(f"in{m}", xT)

            pe.wait_ge(sem("ab_ready"), 1)
            for i in range(NT):
                tok = slice(i * P, (i + 1) * P)
                oL = [begin(pe, f"L{i}{q}") for q in range(2)]
                for hh in range(NH):
                    j, q = hh // 2, hh % 2
                    rows = slice(q * HD, (q + 1) * HD)
                    ins = t.matmul(oL[q][:, j * P:(j + 1) * P], AR[rows, j, i, 0, :], BT[rows, j, tok], start=True, stop=True)
                    if j == NP - 1:
                        done(ins, f"L{i}{q}")
            pe.wait_ge(sem("ops_ready"), 1)
            for i in range(NT):
                tok = slice(i * P, (i + 1) * P)
                turn4(f"nat{i}0", [AR[:, j, i, 0, :] for j in range(NP)])
                turn4(f"nat{i}1", [vT[:, j, tok] for j in range(NP)])
                turn4(f"nat{i}2", [Bd[:, j, tok] for j in range(NP)])
                turn4(f"nat{i}3", [Kd[:, j, tok] for j in range(NP)])
                if i == 0:
                    natural("in11", xT)

            def chunk_products(i):
                tok = slice(i * P, (i + 1) * P)
                for hh in range(NH):
                    j, q = hh // 2, hh % 2
                    rows = slice(q * HD, (q + 1) * HD)
                    ar = AR[rows, j, i, :, :].rearrange("p a b -> p (a b)")
                    o = begin(pe, f"LGMH{i}{hh}")
                    t.matmul(o[:, 0:T], BT[rows, j, tok], ar, start=True, stop=True)
                    done(t.matmul(o[:, T:2 * T], KT[rows, j, tok], ar, start=True, stop=True), f"LGMH{i}{hh}")

            chunk_products(0)
            natural("in12", xT)
            for q in range(4):
                taken(pe, f"memT{q}")
            turned("kv0", memT)
            chunk_products(1)
            pe.wait_ge(sem("rk_ready"), 1)
            for m in range(2):
                o = begin(pe, f"bo{m}")
                done(t.matmul(o[:, :], onesbd[:, :], rk[:, 2 * m:2 * m + 2, :].rearrange("p a b -> p (a b)"), start=True, stop=True), f"bo{m}")

            def scores(u):
                i, heads = UNITS[u]
                w = P * (i + 1)
                o = [begin(pe, f"sc{u}{c}") for c in range(2)]
                for m, hh in enumerate(heads):
                    for c in range(2):
                        rows = slice(c * HD, (c + 1) * HD)
                        ins = t.matmul(o[c][:, m * w:(m + 1) * w], qd[rows, hh, i * P:(i + 1) * P], kd[rows, hh, 0:w], start=True, stop=True)
                        if m == len(heads) - 1:
                            done(ins, f"sc{u}{c}")

            def turn_weights(u):
                pe.wait_ge(sem("attn_ready"), u + 1)
                turn4(f"at{u}", [soft[u][:, 0, m * P:(m + 1) * P] for m in range(4)])

            def values(u):
                i, heads = UNITS[u]
                oo = begin(pe, f"od{u}")
                taken(pe, f"at{u}")
                for m, hh in enumerate(heads):
                    for kb in range(i + 1):
                        ins = t.matmul(oo[:, m * P:(m + 1) * P], atT[u % 2][:, (m * (i + 1) + kb) * P:(m * (i + 1) + kb + 1) * P],
                                       vd[:, kb, hh * P:(hh + 1) * P], start=(kb == 0), stop=(kb == i))
                done(ins, f"od{u}")

            for i in range(NT):
                o = begin(pe, f"MV{i}")
                for hh in range(NH):
                    if hh == 0:
                        taken(pe, f"LGMH{i}7")
                        taken(pe, f"LGMH{i}6")
                        taken(pe, f"LGMH{i}5")
                        taken(pe, f"LGMH{i}4")
                        taken(pe, f"nat{i}1")
                    ins = t.matmul(o[:, hh * HD:(hh + 1) * HD], LGMH[:, i, hh, 2 * P:3 * P], Vn[:, i, hh * HD:(hh + 1) * HD],
                                   start=True, stop=True)
                done(ins, f"MV{i}")
            pe.wait_ge(sem("XT_in"), 16 * (P // SUB))

            def pairs(nm, left, right, before):
                for g in range(4):
                    before(g)
                    o = begin(pe, f"{nm}{g}")
                    for m in range(4):
                        i, hh = g // 2, 4 * (g % 2) + m
                        ins = t.matmul(o[:, m * P:(m + 1) * P], left(i, hh), right(i, hh), start=True, stop=True)
                    done(ins, f"{nm}{g}")

            pairs("z1", lambda i, hh: XTb[:, i, hh, :], lambda i, hh: Zr[:, i, hh, :], lambda g: taken(pe, f"MV{g // 2}"))
            for m in range(7, 13):
                taken(pe, f"in{m}")
            scores(0)
            pairs("z2", lambda i, hh: LGMH[:, i, hh, 0:P], lambda i, hh: Z1[:, i, hh, :], lambda g: taken(pe, f"z1{g}"))
            pairs("z3", lambda i, hh: XTb[:, i, hh, :], lambda i, hh: Z2[:, i, hh, :], lambda g: taken(pe, f"z2{g}"))
            for q in range(4):
                taken(pe, f"z3{q}")
            for i in range(NT):
                tok = slice(i * P, (i + 1) * P)
                o = begin(pe, f"Rh{i}")
                for hh in range(NH):
                    j, q = hh // 2, hh % 2
                    ins = t.matmul(o[q * HD:(q + 1) * HD, j * P:(j + 1) * P], Zf[:, i, hh, 0:HD], LGMH[:, i, hh, P:2 * P],
                                   start=True, stop=True)
                done(ins, f"Rh{i}")
                o = begin(pe, f"yz{i}")
                for hh in range(NH):
                    t.matmul(o[:, hh * HD:(hh + 1) * HD], LGMH[:, i, hh, P:2 * P], Zf[:, i, hh, HD:P], start=True, stop=False)
                    ins = t.matmul(o[:, hh * HD:(hh + 1) * HD], LGMH[:, i, hh, 3 * P:4 * P], Vn[:, i, hh * HD:(hh + 1) * HD],
                                   start=False, stop=True)
                done(ins, f"yz{i}")
            turn_weights(0)
            values(0)
            scores(1)
            for i in range(NT):
                chunks = [c for c in range(4 * i, 4 * i + 4) if c < NCH - 1]
                os_ = {c: begin(pe, f"PP{c}") for c in chunks}
                for j in range(NP):
                    for step, c, q in itertools.product(range(3), chunks, range(2)):
                        hh = 2 * j + q
                        col = slice(hh * HD, (hh + 1) * HD)
                        r = slice(CH * (c % 4), CH * (c % 4) + CH)
                        at = os_[c][q * HD:(q + 1) * HD, j * P + (HD if step else 0):j * P + (2 * HD if step else HD)]
                        left, right = ((Zf[r, i, hh, 0:HD], Bn[r, i, col]), (Bn[r, i, col], Zf[r, i, hh, HD:P]),
                                       (Kn[r, i, col], Vn[r, i, col]))[step]
                        ins = t.matmul(at, left, right, start=(step < 2), stop=(step != 1),
                                       tile_position=(CH * (c % 4), q * HD))
                        if step == 2 and hh == NH - 1:
                            done(ins, f"PP{c}")
                if i == 0:
                    scores(2)
            turn_weights(1)
            values(1)
            turn_weights(2)
            values(2)
            filler = itertools.chain(turned_parts("kv1", memT), turned_parts("kv2", memT))
            for i in range(NT):
                oy = [begin(pe, f"Y{i}{q}") for q in range(2)]
                for c in range(4 * i, 4 * i + 4):
                    pe.wait_ge(sem("S_ready"), c + 1)
                    if c == 0:
                        taken(pe, "Rh0")
                        taken(pe, "Rh1")
                    if 0 < c < NCH - 1:
                        taken(pe, f"PP{c}")
                        o = [begin(pe, f"S{c}{q}") for q in range(2)]
                        for j in range(NP):
                            for q in range(2):
                                rows = slice(q * HD, (q + 1) * HD)
                                ins = t.matmul(o[q][rows, j * HD:(j + 1) * HD], PhiPsi[rows, c, j, 0:HD], St[rows, c, j, :],
                                               start=True, stop=True)
                                if j == NP - 1:
                                    done(ins, f"S{c}{q}")
                        next(filler)
                    r = slice(CH * (c % 4), CH * (c % 4) + CH)
                    for j in range(NP):
                        for q in range(2):
                            rows = slice(q * HD, (q + 1) * HD)
                            ins = t.matmul(oy[q][r, j * HD:(j + 1) * HD], RhT[rows, j, c * CH:(c + 1) * CH], St[rows, c, j, :],
                                           start=True, stop=True, tile_position=(q * HD, CH * (c % 4)))
                            if j == NP - 1 and c % 4 == 3:
                                done(ins, f"Y{i}{q}")
            for _ in filler:
                pass
            pe.wait_ge(sem("odn_ready"), 1)
            for i in range(NT):
                turn4(f"odT{i}", [odn[:, i, m * P:(m + 1) * P] for m in range(4)])
            turned("kv3", memT)
            natural("kv4", memT)
            natural("kv5", memT)
            for i in range(NT):
                pe.wait_ge(sem("yn_ready"), i + 1)
                turn4(f"ynT{i}", [Yn[:, i, m * P:(m + 1) * P] for m in range(4)])
            t.sem_inc(sem("mixers_through"), 1)
            for i in range(NT):
                taken(pe, f"odT{i}")
            for m in range(4):
                natural(f"out{m}", xT, lambda i: pe.wait_ge(sem("yT_ready"), i + 1))
                if m == 2:
                    pe.wait_ge(sem("h_cols_ready"), 2)
                    turn_half("h1", 0, h)
            natural("kv6", memT)
            pe.wait_ge(sem("h_cols_ready"), 4)
            turn_half("h1", 1, h)
            for q in range(4):
                taken(pe, f"h1T{q}")
            for m in range(4):
                turned(f"wq{m}", x2T)
            for m in range(4):
                taken(pe, f"wq{m}")
                taken(pe, f"kv{m}")
            for m in range(XH // 2):
                for i in range(NT):
                    o = begin(pe, f"xs{m}{i}")
                    for q in range(2):
                        for k in range(2):
                            c = 2 * (2 * m + q) + k
                            ins = t.matmul(o[:, q * T:(q + 1) * T], qx[:, c, i * P:(i + 1) * P], kmT[:, c, :], start=(k == 0), stop=(k == 1))
                    done(ins, f"xs{m}{i}")
            natural("kv7", memT)
            for m in range(4, 8):
                taken(pe, f"kv{m}")
            for m in range(XH // 2):
                for i in range(NT):
                    pe.wait_ge(sem("xp_ready"), 2 * m + i + 1)
                    turn4(f"xp{m}{i}", [px[m][:, i, q, kb * P:(kb + 1) * P] for q in range(2) for kb in range(2)])
            for m in range(XH // 2):
                for i in range(NT):
                    taken(pe, f"xp{m}{i}")
                for q in range(2):
                    o = begin(pe, f"xo{m}{q}")
                    for c in range(2):
                        for kb in range(2):
                            col = (2 * m + q) * T + c * P
                            ins = t.matmul(o[:, c * T:(c + 1) * T], vm[:, kb, col:col + P], pxT[m][:, kb, q, :], start=(kb == 0), stop=(kb == 1))
                    done(ins, f"xo{m}{q}")
            for m in range(XH // 2):
                for q in range(2):
                    taken(pe, f"xo{m}{q}")
            t.sem_inc(sem("cross_through"), 1)
            for m in range(4):
                natural(f"wo{m}", oT)
                if m == 2:
                    pe.wait_ge(sem("h_cols_ready"), 6)
                    turn_half("h2", 0, h)
            pe.wait_ge(sem("router_in"), 32)
            logits = [begin(pe, f"logit{i}") for i in range(NT)]

            def router(q):
                for i in range(NT):
                    taken(pe, f"h2T{2 * i + q}")
                for i in range(NT):
                    for k in range(4 * q, 4 * q + 4):
                        ins = t.matmul(logits[i][:, 0:E], x3T[:, k, i * P:(i + 1) * P], rws[:, k, :], start=(k == 0),
                                       stop=(k == KC - 1))
                    if q:
                        done(ins, f"logit{i}")

            router(0)
            pe.wait_ge(sem("h_cols_ready"), 8)
            turn_half("h2", 1, h)
            router(1)
            pe.wait_ge(sem("mask_ready"), 1)
            o = begin(pe, "pos")
            t.matmul(o[:, 0:E], tri[:, :], mask[:, 0, :], start=True, stop=True)
            t.matmul(o[:, E:2 * E], tri[:, :], mask[:, 1, :], start=True, stop=False)
            t.matmul(o[:, E:2 * E], ones[:, :], mask[:, 0, :], start=False, stop=True)
            t.matmul(o[0:1, 2 * E:3 * E], ones[:, 0:1], mask[:, 0, :], start=True, stop=False)
            done(t.matmul(o[0:1, 2 * E:3 * E], ones[:, 0:1], mask[:, 1, :], start=False, stop=True), "pos")
            pe.wait_ge(sem("gates_ready"), 1)
            o = begin(pe, "gateT")
            for i in range(NT):
                ins = t.transpose(o[0:E, i * P:(i + 1) * P], gate[:, i, :], ident[:, :])
            done(ins, "gateT")
            def gather():
                for i in range(NT):
                    for c in range(2):
                        ins = t.matmul(ps[c * BLK:(c + 1) * BLK, 6, :], sel[:, i, :], h[:, i, c * 512:(c + 1) * 512],
                                       start=(i == 0), stop=(i == NT - 1), skip_group_check=True)
                ins.then_inc(sem("xe_filled"), 1)

            def gather_turn():
                for m in range(4):
                    ins = t.transpose(ps[:, 6, m * P:(m + 1) * P], xe[:, m * P:(m + 1) * P], ident[:, :])
                ins.then_inc(sem("xeT_filled"), 1)

            def gate_turn():
                for i in range(NT):
                    ins = t.transpose(ps[:, 7, i * P:(i + 1) * P], selg[:, i, :], ident[:, :])
                ins.then_inc(sem("GT_filled"), 1)

            def scatter():
                for i in range(NT):
                    for c in range(2):
                        rows = slice(c * BLK, (c + 1) * BLK)
                        ins = t.matmul(ps[:, 2 * i + c, :], GT[rows, i * P:(i + 1) * P], yy[rows, :], start=False, stop=False,
                                       skip_group_check=True)
                ins.then_inc(sem("scattered"), 1)

            pe.wait_ge(sem("b2_in"), 16)
            for nm in ("wo2", "wo3", "h2T0", "h2T1", "gateT"):
                taken(pe, nm)
            for i in range(NT):
                for c in range(2):
                    t.matmul(ps[:, 2 * i + c, :], gateT[0:E, i * P:(i + 1) * P], b2a[0:E, c * 512:(c + 1) * 512],
                             start=True, stop=False, skip_group_check=True)
            for nm in ("xp10", "xp11", "h2T2", "h2T3", "gateT", "pos"):
                taken(pe, nm)
            pe.wait_ge(sem("sel_ready"), 2)
            gather()
            pe.wait_ge(sem("xe_ready"), 1)
            gather_turn()
            pe.wait_ge(sem("npass_ready"), 1)
            np_ = pe.value_load(npass[0:1, 0:1], min_val=1, max_val=PASSES)
            second = (ring[:, 8:12, :], w2_odd)
            pe.wait_ge(sem("b1_in"), 64)

            def expert(it, pair, par):
                pe.wait_ge(sem("onehot_ready"), it + 1)
                pe.wait_ge(sem("lin_read"), it + 1)
                for b in range(2):
                    for c in range(2):
                        g = slice((2 * b + c) * E, (2 * b + c + 1) * E)
                        t.matmul(ps[c * BLK:(c + 1) * BLK, 4 + b, :], onehot[g, :], b1a[g, :], start=True, stop=False,
                                 tile_position=((2 * b + c) * E, c * BLK), skip_group_check=True)
                pe.wait_ge(sem("xeT_ready"), it + 1)
                for k in range(KC):
                    w, landed_ = w1_place(par, k)
                    pe.wait_ge(landed_, (it if k < HEAD else pair) * 16 + 16)
                    for b in range(2):
                        for c in range(2):
                            f0 = b * F + c * 512
                            col = (k % 4) * P + (k // 4) * BLK
                            ins = t.matmul(ps[c * BLK:(c + 1) * BLK, 4 + b, :], xeT[:, col:col + BLK], w[:, f0:f0 + 512],
                                           start=False, stop=(k == KC - 1), skip_group_check=True)
                    if k < KC - 1:
                        ins.then_inc(eused, 1)
                    else:
                        ins.then_inc(sem("hid_filled"), 1)
                pe.wait_ge(sem("GT_ready"), it + 1)
                pe.wait_ge(sem("yy_ready"), it + 1)
                scatter()
                pe.wait_ge(sem("selg_ready"), it * 2 + 2)
                gate_turn()
                pe.wait_ge(sem("hid_filled"), it + 1)
                t.sem_inc(eused, 1)
                pe.wait_ge(sem("sel_ready"), it * 2 + 4)
                gather()
                pe.wait_ge(sem("GT_ready"), it + 2)
                pe.wait_ge(sem("ac_ready"), it + 1)
                for m in range(4):
                    ins = t.transpose(ps[:, 7, m * P:(m + 1) * P], ac[:, m * P:(m + 1) * P], ident[:, :])
                ins.then_inc(sem("acT_filled"), 1)
                pe.wait_ge(sem("xe_ready"), it + 2)
                gather_turn()
                pe.wait_ge(sem("acT_ready"), it + 1)
                for k in range(KC):
                    if k % 2 == 0:
                        pe.wait_ge(landed2[par][k // 2], pair * 16 + 16)
                    w = second[par][:, k // 2, (k % 2) * D:(k % 2 + 1) * D]
                    col = (k % 4) * P + (k // 4) * BLK
                    for c in range(2):
                        ins = t.matmul(ps[c * BLK:(c + 1) * BLK, 7, :], acT[:, col:col + BLK], w[:, c * 512:(c + 1) * 512],
                                       start=(k == 0), stop=(k == KC - 1), skip_group_check=True)
                    if k % 2 and k < KC - 1:
                        ins.then_inc(eused, 1)
                ins.then_inc(sem("yy_filled"), 1)
                pe.wait_ge(sem("yy_filled"), it + 1)
                t.sem_inc(eused, 1)

            with pe.Fori(0, np_) as q_:
                with pe.Fori(0, E // 2) as r:
                    pair = pe.snap(q_ * (E // 2) + r)
                    for par in range(2):
                        expert(pe.snap(pair * 2 + par), pair, par)
            n_it = pe.snap(np_ * E)
            pe.wait_ge(sem("GT_ready"), n_it + 1)
            pe.wait_ge(sem("yy_ready"), n_it + 1)
            for i in range(NT):
                for c in range(2):
                    rows = slice(c * BLK, (c + 1) * BLK)
                    ins = t.matmul(ps[:, 2 * i + c, :], GT[rows, i * P:(i + 1) * P], yy[rows, :], start=False, stop=True,
                                   skip_group_check=True)
                ins.then_inc(sem("sum_ready"), 1)

        @block.vector
        def _(dve):
            v = nc.vector
            n = [0]

            def link(ins):
                n[0] += 1
                ins.then_inc(sem("dve_step"), 1)
                dve.wait_ge(sem("dve_step"), n[0])

            def dlink(ins, name):
                drain(ins, name)
                taken(dve, name)

            four = lambda x: x.rearrange("p (h k) -> p h k", h=4)
            two = lambda x: x.rearrange("p (a b) -> p a b", a=2)

            def rsqrt(y, x, s1, s2):
                link(v.tensor_scalar(s1, x, -0.5, None, ALU.mult))
                link(v.tensor_scalar(y.bitcast(I32), x.bitcast(I32), -0.5, 1597463007.0, ALU.mult, ALU.add))
                for _ in range(3):
                    link(v.tensor_tensor(s2, y, y, ALU.mult))
                    link(v.tensor_tensor(s2, s2, s1, ALU.mult))
                    link(v.scalar_tensor_tensor(out=y, in0=s2, scalar=1.5, in1=y, op0=ALU.add, op1=ALU.mult))

            def rstd(c0, c1, width, eps):
                x = st[:, c0:c1]
                link(v.tensor_scalar(x, x, 1.0 / width, eps, ALU.mult, ALU.add))
                rsqrt(x, x, wk[:, 0:c1 - c0], wk[:, 32:32 + c1 - c0])

            def take_rows(s, dst, g):
                for i in range(NT):
                    for q in range(2):
                        nm = f"{s}T{2 * i + q}"
                        o = four(product(dve, nm))
                        drain(v.tensor_tensor(dst[:, 4 * q:4 * q + 4, i * P:(i + 1) * P], o, gbc(g, 4 * q, 4), ALU.mult), nm)

            for i in range(NT):
                dve.wait_ge(sem("x_stat_ready"), i + 1)
                rstd(2 + i, 3 + i, D, EPS)
                v.tensor_scalar(xs[:, i, :], h[:, i, :], st[:, 2 + i:3 + i], None, ALU.mult).then_inc(sem("x_scaled"), 1)
            o = product(dve, "prm")
            for q in range(4):
                product(dve, f"xT{q}")
            dlink(v.tensor_copy(prm[:, :], o[:, 0:NROWS]), "prm")
            take_rows("x", xT, "norm1_g")
            link(v.tensor_scalar(mu1[:, :], prm[:, ROW["mu_shift"]:ROW["mu_shift"] + 14], -1.0, 1.0, ALU.mult, ALU.add))
            dve.sem_inc(sem("mu_ready"), 1)
            link(v.tensor_scalar(w0h[:, :], prm[:, ROW["w0"]:ROW["w0"] + 8], 0.5, None, ALU.mult))
            dve.wait_ge(sem("stat_ready"), 1)
            rstd(0, 2, D, EPS)
            for i in range(NT):
                v.tensor_scalar(memN[:, i, :], memN[:, i, :], st[:, i:i + 1], None, ALU.mult).then_inc(sem("mem_scaled"), 1)
            dve.wait_ge(sem("const_ready"), 1)

            shifts = [0]

            def shift(m):
                src = two(product(dve, f"in{m}"))
                shifts[0] += 1
                dve.wait_ge(sem("unshifted_ready"), 2 * shifts[0])
                for q in range(2):
                    j = 2 * m + q
                    mu = prm[:, ROW["mu_shift"] + j:ROW["mu_shift"] + j + 1]
                    ins = v.scalar_tensor_tensor(out=pT[:, j, 1:T], in0=src[:, q, 0:T - 1], scalar=mu, in1=pT[:, j, 1:T],
                                                 op0=ALU.mult, op1=ALU.add)
                    if q == 0:
                        link(ins)
                dlink(ins, f"in{m}")
                dve.sem_inc(sem("shifted_ready"), 1)

            pr = lambda nm, j: prm[:, ROW[nm] + j:ROW[nm] + j + 1]
            shift(2)
            shift(3)
            for j in range(NP):
                ins = v.tensor_scalar(kk[:, j, :], kT[:, j, :], pr("k_k", j), None, ALU.mult)
            link(ins)
            link(v.tensor_tensor(t2[:, :, :], kk[:, :, :], kk[:, :, :], ALU.mult))
            dve.sem_inc(sem("kksq_ready"), 1)
            take_rows("mem", memT, "mem_norm_g")
            shift(6)
            dve.wait_ge(sem("gd_tanh_ready"), 1)
            link(v.tensor_scalar(pT[:, 13, :], pT[:, 13, :], 0.5, 0.5, ALU.mult, ALU.add))
            dve.sem_inc(sem("gd_ready"), 1)
            dve.wait_ge(sem("lam_in"), 64)
            for m in range(2):
                link(v.tensor_tensor(lamv[:, 2 * m, :], lamv[:, 2 * m, :], lamv[:, 2 * m + 1, :], ALU.mult))
                link(v.reduce_sum(lam[:, m:m + 1], lamv[:, 2 * m, :], AX.X))
            dve.sem_inc(sem("lam_sum_ready"), 1)
            shift(0)
            o = product(dve, "ksum")
            dlink(v.tensor_scalar(krs[0:NH, :], o[0:NH, 0:T], 1e-24, None, ALU.max), "ksum")
            rsqrt(krs[0:NH, :], krs[0:NH, :], kra[0:NH, :], krb[0:NH, :])
            dve.sem_inc(sem("knorm_ready"), 1)
            shift(1)
            for m in range(2):
                taken(dve, f"lw{m}")
            link(v.tensor_scalar(lw[:, :, :], lw[:, :, :], 1.0, 0.5 * NEG_EXP_HALF, ALU.add, ALU.mult))
            for j in range(NP):
                ins = v.tensor_tensor_scan(cs[:, j, :], keep[:, :], lw[:, j, :], 0.0, ALU.mult, ALU.add)
            link(ins)
            link(v.tensor_copy(tail[:, :, :], cs[:, :, CH - 1:T:CH]))
            dve.sem_inc(sem("cs_ready"), 1)
            link(v.tensor_tensor(lw[:, :, :], cs[:, :, :], lw[:, :, :], ALU.subtract))
            dve.sem_inc(sem("ex_ready"), 1)
            cs4 = cs[:, :, :].rearrange("p j (c t) -> p j c t", t=CH)
            t34 = t3[:, :, :].rearrange("p j (c t) -> p j c t", t=CH)
            for m in range(2):
                taken(dve, f"la{m}")
            link(v.tensor_scalar(aa[:, :, :], aa[:, :, :], 0.5, 0.5, ALU.mult, ALU.add))
            for m in range(2):
                o = two(product(dve, f"kb{m}"))
                kv = kk[:, 2 * m:2 * m + 2, :]
                dlink(v.tensor_tensor(kv, o, kv, ALU.mult), f"kb{m}")
            dve.wait_ge(sem("exp_ready"), 1)
            for j in range(NP):
                ins = v.tensor_tensor(AR[:, j, :, 1, :], two(rT[:, j, :]), two(t1[:, j, :]), ALU.mult)
            link(ins)
            dve.sem_inc(sem("t1_free"), 1)
            shift(4)
            product(dve, "lg1")
            for j in range(NP):
                ins = v.tensor_tensor(t34[:, j], tail[:, j, :].unsqueeze(2).to_broadcast([P, NCH, CH]), cs4[:, j], ALU.subtract)
            link(ins)
            dve.sem_inc(sem("rest_ready"), 1)
            for j in range(NP):
                link(v.tensor_scalar(KT[:, j, :], aa[:, j, :], 1.0, pr("k_a", j), ALU.subtract, ALU.mult))
                link(v.scalar_tensor_tensor(out=kT[:, j, :], in0=KT[:, j, :], scalar=1.0, in1=kT[:, j, :], op0=ALU.add, op1=ALU.mult))
            link(v.tensor_tensor(aa[:, :, :], kk[:, :, :], aa[:, :, :], ALU.mult))
            dve.wait_ge(sem("exp_ready"), 3)
            for j in range(NP):
                link(v.scalar_tensor_tensor(out=AR[:, j, :, 0, :], in0=two(kk[:, j, :]), scalar=-1.0, in1=two(lw[:, j, :]),
                                            op0=ALU.mult, op1=ALU.mult))
            dve.wait_ge(sem("exp_ready"), 4)
            link(v.tensor_tensor(BT[:, :, :], aa[:, :, :], t1[:, :, :], ALU.mult))
            dve.sem_inc(sem("ab_ready"), 1)
            shift(5)
            link(v.tensor_tensor(KT[:, :, :], kT[:, :, :], t1[:, :, :], ALU.mult))
            dve.wait_ge(sem("exp_ready"), 5)
            link(v.tensor_tensor(Bd[:, :, :], aa[:, :, :], t3[:, :, :], ALU.mult))
            link(v.tensor_tensor(Kd[:, :, :], kT[:, :, :], t3[:, :, :], ALU.mult))
            dve.sem_inc(sem("t3_free"), 1)
            dve.sem_inc(sem("ops_ready"), 1)
            for i in range(NT):
                o = product(dve, f"nat{i}2")
                drain(v.tensor_copy(Bn[:, i, :], o), f"nat{i}2")
                o = product(dve, f"nat{i}3")
                drain(v.tensor_copy(Kn[:, i, :], o), f"nat{i}3")

            def masked(i):
                for hh in range(NH):
                    o = product(dve, f"LGMH{i}{hh}")
                    drain(v.tensor_tensor(LGMH[:, i, hh, :], o, masks[:, :, :].rearrange("p a b -> p (a b)"), ALU.mult), f"LGMH{i}{hh}")

            masked(0)
            dve.wait_ge(sem("L16_in"), 16)
            dve.wait_ge(sem("X16_unit"), 1)
            for r in range(1, SUB):
                link(v.tensor_tensor(w16[:, 0:r, 0:r], X16[:, 0:r, 0:r], L16[:, r:r + 1, 0:r].to_broadcast([P, r, r]), ALU.mult))
                link(v.reduce_sum(X16[:, 0:r, r:r + 1], w16[:, 0:r, 0:r], AX.X))
            dve.sem_inc(sem("X16_ready"), 1)

            for j in range(NP):
                ins = v.scalar_tensor_tensor(out=rk[:, j, :], in0=rT[:, j, :], scalar=pr("r_k", j), in1=kT[:, j, :],
                                             op0=ALU.mult, op1=ALU.mult)
            link(ins)
            dve.sem_inc(sem("rk_ready"), 1)
            masked(1)
            for m in range(2):
                o = two(product(dve, f"bo{m}"))
                dlink(v.tensor_tensor(bv[:, 2 * m:2 * m + 2, :], o, vT[:, 2 * m:2 * m + 2, :], ALU.mult), f"bo{m}")

            link(v.tensor_scalar(lam[:, 5:6], prm[:, ROW["subln_g"]:ROW["subln_g"] + 1], 1.0 - LAMBDA_INIT, None, ALU.mult))
            dve.sem_inc(sem("sub_gain_ready"), 1)

            def score_max(u):
                i, heads = UNITS[u]
                w = P * (i + 1)
                nh = len(heads)
                for c in range(2):
                    o = product(dve, f"sc{u}{c}").rearrange("p (h k) -> p h k", h=nh)
                    link(v.memset(o[0:64, :, w - 64:w], -1e30))
                    col = 8 * u + 4 * c
                    link(v.reduce_max(dst_[:, col:col + nh], o, AX.X))
                    link(v.tensor_scalar(dst_[:, col:col + nh], dst_[:, col:col + nh], -DSCALE, None, ALU.mult))
                dve.sem_inc(sem("dmax_ready"), 1)

            def combine(u):
                i, heads = UNITS[u]
                w = P * (i + 1)
                nh = len(heads)
                dve.wait_ge(sem("dexp_ready"), u + 1)
                for c in range(2):
                    col = 32 + 8 * u + 4 * c
                    link(v.reciprocal(dst_[:, col:col + nh], dst_[:, col:col + nh]))
                col = 32 + 8 * u + 4
                link(v.tensor_scalar(dst_[:, col:col + nh], dst_[:, col:col + nh], lam[:, 4:5], None, ALU.mult))
                for m in range(nh):
                    a0 = soft[u][:, 0, m * w:(m + 1) * w]
                    a1 = soft[u][:, 1, m * w:(m + 1) * w]
                    link(v.tensor_scalar(a0, a0, dst_[:, 32 + 8 * u + m:33 + 8 * u + m], None, ALU.mult))
                    link(v.scalar_tensor_tensor(out=a0, in0=a1, scalar=dst_[:, 36 + 8 * u + m:37 + 8 * u + m], in1=a0,
                                                op0=ALU.mult, op1=ALU.add))
                dve.sem_inc(sem("attn_ready"), 1)

            score_max(0)
            for q in range(4):
                i, h0 = q // 2, 4 * (q % 2)
                o = four(product(dve, f"z3{q}"))
                drain(v.tensor_tensor(Zf[:, i, h0:h0 + 4, :], o, Z1[:, i, h0:h0 + 4, :], ALU.add), f"z3{q}")
            for i in range(NT):
                o = four(product(dve, f"Rh{i}"))
                drain(v.tensor_tensor(RhT[:, :, i * P:(i + 1) * P], o, AR[:, :, i, 1, :], ALU.add), f"Rh{i}")
            dve.wait_ge(sem("lam_exp_ready"), 1)
            link(v.tensor_tensor(lam[:, 4:5], lam[:, 3:4], lam[:, 2:3], ALU.subtract))
            link(v.tensor_scalar(lam[:, 4:5], lam[:, 4:5], -LAMBDA_INIT, None, ALU.add))
            combine(0)
            score_max(1)
            combine(1)
            score_max(2)
            combine(2)

            def outputs(i):
                for q in range(2):
                    o = product(dve, f"Y{i}{q}")[:, 0:NP * HD].rearrange("p (j k) -> p j k", j=NP)
                    y0 = Y0[:, i, :].rearrange("p (j q k) -> p j q k", j=NP, q=2)[:, :, q, :]
                    yn = Yn[:, i, :].rearrange("p (j q k) -> p j q k", j=NP, q=2)[:, :, q, :]
                    dlink(v.tensor_tensor(yn, o, y0, ALU.add), f"Y{i}{q}")

            def centre(i):
                yv = Yn[:, i, :].rearrange("p (h k) -> p h k", h=NH)
                link(v.reduce_sum(st[:, 40 + 8 * i:48 + 8 * i], yv, AX.X))
                link(v.tensor_scalar(st[:, 40 + 8 * i:48 + 8 * i], st[:, 40 + 8 * i:48 + 8 * i], 1.0 / HD, None, ALU.mult))
                link(v.tensor_tensor(yv, yv, st[:, 40 + 8 * i:48 + 8 * i].unsqueeze(2).to_broadcast([P, NH, HD]), ALU.subtract))
                dve.sem_inc(sem("centred_ready"), 1)

            link(v.memset(St[:, 0, :, :], 0.0))
            dve.sem_inc(sem("S_ready"), 1)
            taken(dve, "PP0")
            link(v.tensor_copy(St[:, 1, :, :], PhiPsi[:, 0, :, HD:P]))
            dve.sem_inc(sem("S_ready"), 1)
            for c in range(1, NCH - 1):
                taken(dve, f"PP{c}")
                link(v.tensor_tensor(sd[:, :, :], St[:, c, :, :], dec[:, :, c:c + 1].to_broadcast([P, NP, HD]), ALU.mult))
                link(v.tensor_tensor(sd[:, :, :], sd[:, :, :], PhiPsi[:, c, :, HD:P], ALU.add))
                for q in range(2):
                    rows = slice(q * HD, (q + 1) * HD)
                    o = product(dve, f"S{c}{q}")[rows, 0:NP * HD].rearrange("p (j k) -> p j k", j=NP)
                    dlink(v.tensor_tensor(St[rows, c + 1, :, :], o, sd[rows, :, :], ALU.add), f"S{c}{q}")
                dve.sem_inc(sem("S_ready"), 1)
                if c == 3:
                    outputs(0)
                if c == 5:
                    centre(0)
                if c == 4:
                    dve.wait_ge(sem("osq_ready"), 1)
                    rstd(8, 16, P, EPS)
                    dve.sem_inc(sem("osr_ready"), 1)
            outputs(1)
            centre(1)
            link(v.tensor_tensor(dsq[:, :], Yn[:, 1, :], Yn[:, 1, :], ALU.mult))
            link(v.reduce_sum(st[:, 24:32], dsq[:, :].rearrange("p (h k) -> p h k", h=NH), AX.X))
            dve.wait_ge(sem("ysq_ready"), 1)
            rstd(16, 32, HD, GN_EPS)
            for i in range(NT):
                yv = Yn[:, i, :].rearrange("p (h k) -> p h k", h=NH)
                link(v.tensor_tensor(yv, yv, st[:, 16 + 8 * i:24 + 8 * i].unsqueeze(2).to_broadcast([P, NH, HD]), ALU.mult))
                dve.sem_inc(sem("yn_ready"), 1)
            o = four(product(dve, "ynT0"))
            for j in range(NP):
                ins = v.tensor_scalar(xT[:, j, 0:P], o[:, j, :], pr("lnx_g", j), pr("lnx_b", j), ALU.mult, ALU.add)
                if j < NP - 1:
                    link(ins)
            dlink(ins, "ynT0")
            for i in range(NT):
                tok = slice(i * P, (i + 1) * P)
                taken(dve, f"ynT{i}")
                link(v.tensor_tensor(xT[:, 0:NP, tok], xT[:, 0:NP, tok], bv[:, :, tok], ALU.add))
                link(v.tensor_tensor(xT[:, 0:NP, tok], xT[:, 0:NP, tok], gT[:, :, tok], ALU.mult))
                dve.sem_inc(sem("yT_ready"), 1)

            def take_half(s, q, dst, g):
                for i in range(NT):
                    nm = f"{s}T{2 * i + q}"
                    o = four(product(dve, nm))
                    drain(v.tensor_tensor(dst[:, 4 * q:4 * q + 4, i * P:(i + 1) * P], o, gbc(g, 4 * q, 4), ALU.mult), nm)

            def residual(w, s, dst, g):
                for m in range(4):
                    o = two(product(dve, f"{w}{m}"))
                    hv = h[:, :, m * WCOL:(m + 1) * WCOL]
                    dlink(v.tensor_tensor(hv, o, hv, ALU.add), f"{w}{m}")
                    dve.sem_inc(sem("h_cols_ready"), 1)
                    if m == 2:
                        take_half(s, 0, dst, g)
                dve.sem_inc(sem("h_ready"), 1)
                take_half(s, 1, dst, g)

            residual("out", "h1", x2T, "norm2_g")
            dve.wait_ge(sem("stat_ready"), 2)
            rstd(4, 6, D, EPS)
            link(v.tensor_scalar(st[:, 36:38], st[:, 4:6], XSCALE, None, ALU.mult))
            link(v.tensor_scalar(st[:, 38:40], st[:, 4:6], -XSCALE, None, ALU.mult))
            for m in range(XH // 2):
                for i in range(NT):
                    o = two(product(dve, f"xs{m}{i}"))
                    col = 4 * m + 2 * i
                    link(v.reduce_max(xst[:, col:col + 2], o, AX.X))
                    link(v.tensor_scalar(xst[:, col:col + 2], xst[:, col:col + 2], st[:, 38 + i:39 + i], None, ALU.mult))
                    dve.sem_inc(sem("xmax_ready"), 1)
            for m in range(XH // 2):
                for i in range(NT):
                    taken(dve, f"xs{m}{i}")
                    col = 8 + 4 * m + 2 * i
                    link(v.reciprocal(xst[:, col:col + 2], xst[:, col:col + 2]))
                    link(v.tensor_tensor(px[m][:, i, :, :], px[m][:, i, :, :], xst[:, col:col + 2].unsqueeze(2).to_broadcast([P, 2, T]), ALU.mult))
                    dve.sem_inc(sem("xp_ready"), 1)
            for m in range(XH // 2):
                for i in range(NT):
                    nm = f"xp{m}{i}"
                    o = product(dve, nm).rearrange("p (q b t) -> p b q t", q=2, b=2)
                    for kb in range(2):
                        ins = v.tensor_copy(pxT[m][:, kb, :, i * P:(i + 1) * P], o[:, kb])
                        if kb == 0:
                            link(ins)
                    dlink(ins, nm)
            residual("wo", "h2", x3T, "norm3_g")
            dve.wait_ge(sem("stat_ready"), 3)
            rstd(6, 8, D, EPS)
            link(v.memset(yy[:, :], 0.0))
            dve.sem_inc(sem("yy_ready"), 1)
            link(v.memset(GT[:, :], 0.0))
            dve.sem_inc(sem("GT_ready"), 1)
            dve.sem_inc(sem("lin_read"), 1)
            v.tensor_copy(onehot[:, :], identE[:, 0:1].to_broadcast([P, BLK])).then_inc(sem("onehot_ready"), 1)
            dve.wait_ge(sem("router_in"), 32)
            for i in range(NT):
                drain(v.scalar_tensor_tensor(out=lg[:, i, :], in0=product(dve, f"logit{i}")[:, 0:E], scalar=st[:, 6 + i:7 + i],
                                             in1=rbs[:, :], op0=ALU.mult, op1=ALU.add), f"logit{i}")
            for i in range(NT):
                taken(dve, f"logit{i}")
            for i in range(NT):
                ins = v.max(rt[:, 8 * i:8 * i + 8], lg[:, i, :])
            link(ins)
            link(v.tensor_scalar(rt[:, 16:18], rt[:, 0:16:8], -1.0, None, ALU.mult))
            dve.sem_inc(sem("top_ready"), 1)
            for i in range(NT):
                ins = v.max_index(ix8[:, i, :], rt[:, 8 * i:8 * i + 8], lg[:, i, :])
            link(ins)
            link(v.tensor_copy(rt[:, 32:48].rearrange("p (i k) -> p i k", i=NT), ix8[:, :, :]))
            for i in range(NT):
                ins = v.tensor_tensor(picks[:, i, :, :], iotaE[:, :].unsqueeze(1).to_broadcast([P, TOPK, E]),
                                      rt[:, 32 + 8 * i:36 + 8 * i].unsqueeze(2).to_broadcast([P, TOPK, E]), ALU.is_equal)
            link(ins)
            link(v.reduce_sum(mask[:, :, :], picks[:, :, :, :].rearrange("p i k e -> p i e k"), AX.X))
            dve.sem_inc(sem("mask_ready"), 1)
            dve.wait_ge(sem("gexp_ready"), NT)
            link(v.reciprocal(rt[:, 20:22], rt[:, 18:20]))
            ex = rt[:, 24:32].rearrange("p (i k) -> p i k", i=NT)
            link(v.tensor_tensor(ex, ex, rt[:, 20:22].unsqueeze(2).to_broadcast([P, NT, TOPK]), ALU.mult))
            for i in range(NT):
                ins = v.tensor_tensor(picks[:, i, :, :], picks[:, i, :, :],
                                      rt[:, 24 + 4 * i:28 + 4 * i].unsqueeze(2).to_broadcast([P, TOPK, E]), ALU.mult)
            link(ins)
            link(v.reduce_sum(gate[:, :, :], picks[:, :, :, :].rearrange("p i k e -> p i e k"), AX.X))
            dve.sem_inc(sem("gates_ready"), 1)
            o = product(dve, "pos")
            link(v.scalar_tensor_tensor(out=queue[:, :, :], in0=o[:, 0:NT * E].rearrange("p (i e) -> p i e", i=NT), scalar=1.0,
                                        in1=mask[:, :, :], op0=ALU.add, op1=ALU.mult))
            link(v.tensor_scalar(post[:, :, 0, :], queue[:, :, :], -1.0, None, ALU.add))
            postv = [post[:, i, :, :].rearrange("p k e -> p (k e)") for i in range(NT)]

            for i in range(NT):
                v.tensor_scalar(sel[:, i, :], iota[:, 0:BLK], postv[i][:, 0:1], st[:, 6 + i:7 + i], ALU.is_equal, ALU.mult).then_inc(sem("sel_ready"), 1)
            link(v.reduce_max(rt[0:1, 48:49], o[0:1, 2 * E:3 * E], AX.X))
            link(v.tensor_scalar(rt[0:1, 49:50], rt[0:1, 48:49], float(BLK), 1.0, ALU.is_gt, ALU.add))
            for k in range(2, PASSES):
                link(v.tensor_scalar(rt[0:1, 50:51], rt[0:1, 48:49], float(k * BLK), None, ALU.is_gt))
                link(v.tensor_tensor(rt[0:1, 49:50], rt[0:1, 49:50], rt[0:1, 50:51], ALU.add))
            dlink(v.tensor_copy(npass[0:1, 0:1], rt[0:1, 49:50]), "pos")
            dve.sem_inc(sem("npass_ready"), 1)
            for k in range(1, PASSES + 1):
                ins = v.tensor_scalar(post[:, :, k, :], queue[:, :, :], -1.0 - BLK * k, None, ALU.add)
            link(ins)
            r = ROW["norm3_g"]
            gains = prm[:, r:r + KC].rearrange("p (c m) -> p m c", c=2).unsqueeze(3).to_broadcast([P, 4, 2, BLK])

            def take_block():
                v.tensor_tensor(xeT[:, :].rearrange("p (m c t) -> p m c t", m=4, c=2),
                                ps[:, 6, :].rearrange("p (m c t) -> p m c t", m=4, c=2), gains, ALU.mult).then_inc(sem("xeT_ready"), 1)

            dve.wait_ge(sem("xeT_filled"), 1)
            take_block()
            np_ = dve.value_load(npass[0:1, 0:1], min_val=1, max_val=PASSES)
            with dve.Fori(0, np_) as q_:
                with dve.Fori(0, E) as e:
                    it = dve.snap(q_ * E + e)
                    dve.wait_ge(sem("GT_ready"), it + 1)
                    for i in range(NT):
                        v.tensor_scalar(selg[:, i, :], iota[:, :], postv[i][:, bass.ds(it, 1)], gate[:, i, bass.ds(e, 1)],
                                        ALU.is_equal, ALU.mult).then_inc(sem("selg_ready"), 1)
                    dve.wait_ge(sem("xe_filled"), it + 1)
                    for i in range(NT):
                        v.tensor_scalar(sel[:, i, :], iota[:, 0:BLK], postv[i][:, bass.ds(it + 1, 1)], st[:, 6 + i:7 + i], ALU.is_equal, ALU.mult)\
                            .then_inc(sem("sel_ready"), 1)
                    dve.wait_ge(sem("hid_filled"), it + 1)
                    v.tensor_scalar(gg[:, :], ps[:, 4, :], 7.0, None, ALU.min).then_inc(sem("gate_ready"), 1)
                    v.tensor_scalar(ll[:, :], ps[:, 5, :], 7.0, -7.0, ALU.min, ALU.max).then_inc(sem("lin_read"), 1)
                    v.tensor_copy(onehot[:, :], identE[:, bass.ds(e + 1, 1)].to_broadcast([P, BLK])).then_inc(sem("onehot_ready"), 1)
                    dve.wait_ge(sem("lin_read"), it + 2)
                    dve.wait_ge(sem("gate_ready"), it + 1)
                    v.scalar_tensor_tensor(out=ll[:, :], in0=ll[:, :], scalar=1.0, in1=gg[:, :], op0=ALU.add, op1=ALU.mult)\
                        .then_inc(sem("swi_step"), 1)
                    dve.wait_ge(sem("swi_step"), it + 1)
                    dve.wait_ge(sem("sig_ready"), it + 1)
                    v.tensor_tensor(ac[:, :], ll[:, :], sg[:, :], ALU.mult).then_inc(sem("ac_ready"), 1)
                    dve.wait_ge(sem("xeT_filled"), it + 2)
                    take_block()
                    dve.wait_ge(sem("yy_filled"), it + 1)
                    v.tensor_copy(yy[:, :], ps[:, 7, :]).then_inc(sem("yy_ready"), 1)
            for i in range(NT):
                dve.wait_ge(sem("sum_ready"), i + 1)
                for c in range(2):
                    hv = h[:, i, c * 512:(c + 1) * 512]
                    link(v.tensor_tensor(hv, ps[:, 2 * i + c, :], hv, ALU.add))
                dve.sem_inc(sem("h_ready"), 1)
            dve.wait_ge(sem("out_stat_ready"), NT)
            rstd(32, 34, D, EPS)
            dve.wait_ge(sem("fing_in"), 16)
            for i in range(NT):
                for c in range(2):
                    cols = slice(c * 512, (c + 1) * 512)
                    v.scalar_tensor_tensor(out=h[:, i, cols], in0=h[:, i, cols], scalar=st[:, 32 + i:33 + i], in1=fing[:, cols],
                                           op0=ALU.mult, op1=ALU.mult).then_inc(sem("y_ready"), 1)


_INS = ["x", "mem", "norm1_g", "w_in", "mu_shift", "w0", "w2", "a0", "a2", "g2", "k_k", "k_a", "r_k", "lnx_g", "lnx_b",
        "lam_q1", "lam_k1", "lam_q2", "lam_k2", "subln_g", "w_out", "norm2_g", "mem_norm_g", "wq_x", "wkv_x", "wo_x",
        "norm3_g", "router_w", "router_b", "moe_w1", "moe_b1", "moe_w2", "moe_b2", "final_g"]


def kernel(**inputs):
    import numpy as _np
    import concourse.bacc as _bacc
    from concourse import mybir as _mybir
    from concourse.bass_utils import run_bass_kernel_spmd as _run

    nc = _bacc.Bacc("TRN2", target_bir_lowering=False, num_devices=1)
    arrays, aps = {}, {}
    for name in _INS:
        v = _np.ascontiguousarray(inputs[name])
        arrays[f"in_{name}"] = v
        aps[name] = nc.dram_tensor(f"in_{name}", v.shape, _mybir.dt.from_np(v.dtype), kind="ExternalInput").ap()
    out = nc.dram_tensor("out_0", (1, T, D), F32, kind="ExternalOutput").ap()
    program(nc, aps, out)
    r = _run(nc, [arrays], core_ids=[0])
    return r.results[0]["out_0"]
```
